# Optimizing a Trainium2 kernel written in Bass

```python
import math
import jax
import jax.numpy as jnp
from jax import lax
import numpy as np

D_MODEL = 1024
BATCH = 1
SEQ = 1024
DEPTH = 1
DEC_BATCH = 1
DEC_SEQ = 512
PAST_LEN = 128

RMS_EPS = 1e-6
DN_HEADS = 4
DN_HEAD_DIM = 128
DN_WIDTH = DN_HEADS * DN_HEAD_DIM
DN_CONV = 5
DN_CHUNK = 64
RW_HEADS = 8
RW_HEAD_DIM = 64
RW_WIDTH = RW_HEADS * RW_HEAD_DIM
RW_DECAY_LORA = 64
RW_ICLR_LORA = 64
RW_GATE_LORA = 128
RW_GN_EPS = 64e-5
DN_COLS = 4 * DN_WIDTH + 4 * DN_HEADS
RW_COLS = 3 * RW_WIDTH + 2 * RW_DECAY_LORA + RW_ICLR_LORA + RW_GATE_LORA
GATE_COLS = 2 * D_MODEL
IN_COLS = DN_COLS + RW_COLS + GATE_COLS
MOE_GROUPS = 4
MOE_PER_GROUP = 8
N_EXPERTS = MOE_GROUPS * MOE_PER_GROUP
TOP_K = 2
EXPERT_FF = 512
MOE_BLOCK = 128

kernel_name = 'hybrid_deltanet_rwkv7_hmoe_encoder'

def rms_norm(x, gain, eps=RMS_EPS):
    xf = x.astype(jnp.float32)
    y = xf * lax.rsqrt(jnp.mean(xf * xf, axis=-1, keepdims=True) + eps)
    return (y * gain.astype(jnp.float32)).astype(x.dtype)

def l2_normalize(t, eps):
    return t * lax.rsqrt(jnp.sum(t * t, axis=-1, keepdims=True) + eps)

def flip_time(t):
    return t[:, ::-1]

def stack_directions(fwd, bwd):
    return jnp.concatenate([fwd, flip_time(bwd)], axis=0)

def merge_directions(o, batch):
    return o[:batch] + flip_time(o[batch:])

def centred_depthwise_conv(x, w):
    k, ch = w.shape
    return lax.conv_general_dilated(
        x, w.astype(x.dtype).reshape(k, 1, ch), window_strides=(1,),
        padding=[(k // 2, k // 2)], dimension_numbers=('NWC', 'WIO', 'NWC'),
        feature_group_count=ch)

def gated_delta_rule_chunked(q, k, v, log_alpha, beta):
    b, t, h, dk = q.shape
    dv = v.shape[-1]
    nc = t // DN_CHUNK

    def chunks(a):
        return a.reshape(b, nc, DN_CHUNK, h, -1).transpose(0, 3, 1, 2, 4)

    q, k, v = chunks(q), chunks(k), chunks(v)
    la = chunks(log_alpha[..., None])[..., 0]
    bt = chunks(beta[..., None])[..., 0]
    g = jnp.cumsum(la, axis=-1)
    idx = jnp.arange(DN_CHUNK)
    incl = idx[:, None] >= idx[None, :]
    strict = idx[:, None] > idx[None, :]
    decay = jnp.exp(jnp.where(incl, g[..., :, None] - g[..., None, :], -jnp.inf))
    kk = jnp.einsum('bhnid,bhnjd->bhnij', k, k)
    lower = jnp.where(strict, bt[..., :, None] * kk * decay, 0.0)
    eye = jnp.eye(DN_CHUNK, dtype=q.dtype)
    rhs = jnp.concatenate([v * bt[..., None], k * (bt * jnp.exp(g))[..., None]], axis=-1)
    wy = lax.linalg.triangular_solve(lower + eye, rhs, left_side=True, lower=True, unit_diagonal=True)
    w_v, w_k = wy[..., :dv], wy[..., dv:]
    a_qk = jnp.einsum('bhnid,bhnjd->bhnij', q, k) * decay
    q_g = q * jnp.exp(g)[..., None]
    k_tail = k * jnp.exp(g[..., -1:] - g)[..., None]
    g_tot = jnp.exp(g[..., -1])

    def step(s, xs):
        w_v_c, w_k_c, q_g_c, a_qk_c, k_tail_c, g_tot_c = xs
        u = w_v_c - jnp.einsum('bhck,bhkv->bhcv', w_k_c, s)
        o = jnp.einsum('bhck,bhkv->bhcv', q_g_c, s) + jnp.einsum('bhij,bhjv->bhiv', a_qk_c, u)
        s = s * g_tot_c[..., None, None] + jnp.einsum('bhck,bhcv->bhkv', k_tail_c, u)
        return s, o

    xs = tuple(jnp.moveaxis(a, 2, 0) for a in (w_v, w_k, q_g, a_qk, k_tail, g_tot))
    s0 = jnp.zeros((b, h, dk, dv), q.dtype)
    _, o = lax.scan(step, s0, xs)
    return o.transpose(1, 0, 3, 2, 4).reshape(b, t, h, dv)

def rwkv7_scan(r, w, k, v, kk, a):
    b, t, h, n = r.shape

    def step(s, xs):
        r_t, w_t, k_t, v_t, kk_t, a_t = xs
        s_kk = jnp.einsum('bhvk,bhk->bhv', s, kk_t)
        s = (s * w_t[:, :, None, :] - s_kk[..., None] * (kk_t * a_t)[:, :, None, :]
             + v_t[..., None] * k_t[:, :, None, :])
        return s, jnp.einsum('bhvk,bhk->bhv', s, r_t)

    xs = tuple(jnp.moveaxis(z, 1, 0) for z in (r, w, k, v, kk, a))
    _, o = lax.scan(step, jnp.zeros((b, h, n, n), r.dtype), xs)
    return jnp.moveaxis(o, 0, 1)

def deltanet_branch(cols, conv_w, a_log, dt_bias, norm_w):
    b, t, _ = cols.shape
    w3 = 3 * DN_WIDTH
    qkv = jax.nn.silu(centred_depthwise_conv(cols[..., :w3], conv_w))

    def heads(z):
        return z.reshape(b, t, DN_HEADS, DN_HEAD_DIM)

    q = l2_normalize(heads(qkv[..., :DN_WIDTH]), 1e-6) * DN_HEAD_DIM ** -0.5
    k = l2_normalize(heads(qkv[..., DN_WIDTH:2 * DN_WIDTH]), 1e-6)
    v = heads(qkv[..., 2 * DN_WIDTH:])
    z = heads(cols[..., w3:4 * DN_WIDTH])
    ab = cols[..., 4 * DN_WIDTH:].reshape(b, t, 2, 2, DN_HEADS)
    log_alpha = -jnp.exp(a_log) * jax.nn.softplus(ab[:, :, 0] + dt_bias)
    beta = jax.nn.sigmoid(ab[:, :, 1])
    o = gated_delta_rule_chunked(
        stack_directions(q, q), stack_directions(k, k), stack_directions(v, v),
        stack_directions(log_alpha[:, :, 0], log_alpha[:, :, 1]),
        stack_directions(beta[:, :, 0], beta[:, :, 1]))
    o = merge_directions(o, b)
    o = rms_norm(o, norm_w) * jax.nn.silu(z)
    return o.reshape(b, t, DN_WIDTH)

def rwkv7_branch(cols, mu, w0, w2, a0, a2, g2, k_k, k_a, r_k, ln_w, ln_b):
    b, t, _ = cols.shape
    padded = jnp.pad(cols, ((0, 0), (1, 1), (0, 0)))
    cols = cols + (0.5 * (padded[:, :-2] + padded[:, 2:]) - cols) * mu
    wd_ = RW_WIDTH
    r, k, v = cols[..., :wd_], cols[..., wd_:2 * wd_], cols[..., 2 * wd_:3 * wd_]
    o0 = 3 * wd_
    o1 = o0 + 2 * RW_DECAY_LORA
    w_down = cols[..., o0:o1].reshape(b, t, 2, RW_DECAY_LORA)
    a_down = cols[..., o1:o1 + RW_ICLR_LORA]
    g_down = cols[..., o1 + RW_ICLR_LORA:]
    w_log = -jax.nn.softplus(-(w0 + jnp.einsum('btdr,drc->btdc', jnp.tanh(w_down), w2))) - 0.5
    decay = jnp.exp(-jnp.exp(w_log)).reshape(b, t, 2, RW_HEADS, RW_HEAD_DIM)
    a = jax.nn.sigmoid(a0 + a_down @ a2)
    g = jax.nn.sigmoid(g_down) @ g2

    def heads(z):
        return z.reshape(b, t, RW_HEADS, RW_HEAD_DIM)

    kk = l2_normalize(heads(k * k_k), 1e-12)
    k = k * (1.0 + (a - 1.0) * k_a)
    r, k, v, a = heads(r), heads(k), heads(v), heads(a)
    o = rwkv7_scan(stack_directions(r, r), stack_directions(decay[:, :, 0], decay[:, :, 1]),
                   stack_directions(k, k), stack_directions(v, v),
                   stack_directions(kk, kk), stack_directions(a, a))
    o = merge_directions(o, b)
    mean = jnp.mean(o, axis=-1, keepdims=True)
    var = jnp.mean(jnp.square(o - mean), axis=-1, keepdims=True)
    o = ((o - mean) * lax.rsqrt(var + RW_GN_EPS) * ln_w.reshape(RW_HEADS, RW_HEAD_DIM)
         + ln_b.reshape(RW_HEADS, RW_HEAD_DIM))
    o = o + jnp.sum(r * k * r_k, axis=-1, keepdims=True) * v
    return o.reshape(b, t, RW_WIDTH) * g

def token_mixer(h, p):
    proj = (h @ p['w_in']).astype(jnp.float32)
    y_dn = deltanet_branch(proj[..., :DN_COLS], p['dn_conv_w'], p['dn_a_log'], p['dn_dt_bias'], p['dn_norm_w'])
    y_rw = rwkv7_branch(proj[..., DN_COLS:DN_COLS + RW_COLS], p['rw_mu'], p['rw_w0'], p['rw_w2'],
                        p['rw_a0'], p['rw_a2'], p['rw_g2'], p['rw_k_k'], p['rw_k_a'], p['rw_r_k'],
                        p['rw_ln_w'], p['rw_ln_b'])
    gates = jax.nn.sigmoid(proj[..., DN_COLS + RW_COLS:])
    merged = (gates[..., :D_MODEL] * (y_dn.astype(h.dtype) @ p['w_br_dn'])
              + gates[..., D_MODEL:] * (y_rw.astype(h.dtype) @ p['w_br_rw']))
    return merged.astype(h.dtype) @ p['w_out']

def routed_experts(xt, expert_id, weight, w_gate, w_up, w_down):
    n, d = xt.shape
    n_assign = expert_id.shape[0]
    token = jnp.arange(n_assign, dtype=jnp.int32) // TOP_K
    order = jnp.argsort(expert_id)
    e_sorted = expert_id[order]
    counts = jnp.zeros((N_EXPERTS,), jnp.int32).at[expert_id].add(1)
    padded = (counts + MOE_BLOCK - 1) // MOE_BLOCK * MOE_BLOCK
    start = jnp.cumsum(counts) - counts
    pstart = jnp.cumsum(padded) - padded
    dest = pstart[e_sorted] + jnp.arange(n_assign, dtype=jnp.int32) - start[e_sorted]
    n_blocks = (n_assign + N_EXPERTS * (MOE_BLOCK - 1)) // MOE_BLOCK + 1
    n_slots = n_blocks * MOE_BLOCK
    slot_tok = jnp.full((n_slots,), n, jnp.int32).at[dest].set(token[order])
    slot_w = jnp.zeros((n_slots,), weight.dtype).at[dest].set(weight[order])
    block_exp = jnp.minimum(
        jnp.searchsorted(jnp.cumsum(padded), jnp.arange(n_blocks, dtype=jnp.int32) * MOE_BLOCK, side='right'),
        N_EXPERTS - 1)
    x_pad = jnp.concatenate([xt, jnp.zeros((1, d), xt.dtype)], axis=0)
    xb = x_pad[slot_tok].reshape(n_blocks, MOE_BLOCK, d)

    def expert_block(args):
        xblk, e = args
        hid = jax.nn.silu(xblk @ w_gate[e]) * (xblk @ w_up[e])
        return hid @ w_down[e]

    yb = lax.map(expert_block, (xb, block_exp)).reshape(n_slots, d)
    contrib = (yb * slot_w[:, None]).astype(xt.dtype)
    y = jnp.zeros((n + 1, d), xt.dtype).at[slot_tok].add(contrib)
    return y[:n]

def hierarchical_moe(h, p):
    b, t, d = h.shape
    n = b * t
    xt = h.reshape(n, d)
    g_logits = (xt @ p['moe_w_group']).astype(jnp.float32) + p['moe_b_group']
    _, g_idx = lax.top_k(g_logits, 1)
    g_prob = jnp.take_along_axis(jax.nn.softmax(g_logits, axis=-1), g_idx, axis=-1)[:, 0]
    e_logits = ((xt @ p['moe_w_expert']).astype(jnp.float32) + p['moe_b_expert']).reshape(n, MOE_GROUPS, MOE_PER_GROUP)
    e_in_group = e_logits[jnp.arange(n), g_idx[:, 0]]
    e_top, e_idx = lax.top_k(e_in_group, TOP_K)
    weights = jax.nn.softmax(e_top, axis=-1) * g_prob[:, None]
    expert_id = g_idx * MOE_PER_GROUP + e_idx
    y = routed_experts(xt, expert_id.reshape(-1), weights.reshape(-1),
                       p['moe_w_gate'], p['moe_w_up'], p['moe_w_down'])
    return y.reshape(b, t, d)

def encoder_layer(x, c, p):
    ada = jax.nn.silu(c) @ p['w_ada'] + p['b_ada']
    shift1, scale1, gate1, shift2, scale2, gate2 = jnp.split(ada[:, None, :], 6, axis=-1)
    h = rms_norm(x, p['norm1']) * (1 + scale1) + shift1
    x = x + gate1 * token_mixer(h, p)
    h = rms_norm(x, p['norm2']) * (1 + scale2) + shift2
    x = x + gate2 * hierarchical_moe(h, p)
    return x

def encoder(x, c, layers, final_norm):
    for layer in range(DEPTH):
        x = encoder_layer(x, c, {name: arr[layer] for name, arr in layers.items()})
    return rms_norm(x, final_norm)

def setup_inputs(seed: int = 0) -> dict:
    key = jax.random.key(seed)
    ks = iter(jax.random.split(key, 48))
    L, D = DEPTH, D_MODEL

    def nrm(shape, scale):
        return scale * jax.random.normal(next(ks), shape, jnp.float32)

    dt = jnp.exp(jax.random.uniform(next(ks), (L, 2, DN_HEADS), minval=math.log(1e-3), maxval=math.log(1e-1)))
    inputs = {
        'x_prompt': nrm((BATCH, SEQ, D), 1.0),
        'x_sample': nrm((DEC_BATCH, DEC_SEQ, D), 1.0),
        'c_prompt': nrm((BATCH, D), 1.0),
        'c_sample': nrm((DEC_BATCH, D), 1.0),
        'w_ada': nrm((L, D, 6 * D), D ** -0.5),
        'b_ada': nrm((L, 6 * D), 0.02),
        'norm1': 1.0 + nrm((L, D), 0.02),
        'norm2': 1.0 + nrm((L, D), 0.02),
        'w_in': nrm((L, D, IN_COLS), D ** -0.5),
        'dn_conv_w': nrm((L, DN_CONV, 3 * DN_WIDTH), DN_CONV ** -0.5),
        'dn_a_log': jnp.log(jax.random.uniform(next(ks), (L, 2, DN_HEADS), minval=1.0, maxval=16.0)),
        'dn_dt_bias': dt + jnp.log(-jnp.expm1(-dt)),
        'dn_norm_w': 1.0 + nrm((L, DN_HEAD_DIM), 0.02),
        'rw_mu': jax.random.uniform(next(ks), (L, RW_COLS), jnp.float32),
        'rw_w0': jax.random.uniform(next(ks), (L, 2, RW_WIDTH), minval=-5.0, maxval=-0.5),
        'rw_w2': nrm((L, 2, RW_DECAY_LORA, RW_WIDTH), 0.5 * RW_DECAY_LORA ** -0.5),
        'rw_a0': nrm((L, RW_WIDTH), 0.1),
        'rw_a2': nrm((L, RW_ICLR_LORA, RW_WIDTH), RW_ICLR_LORA ** -0.5),
        'rw_g2': nrm((L, RW_GATE_LORA, RW_WIDTH), RW_GATE_LORA ** -0.5),
        'rw_k_k': 0.85 + nrm((L, RW_WIDTH), 0.05),
        'rw_k_a': 1.0 + nrm((L, RW_WIDTH), 0.05),
        'rw_r_k': nrm((L, RW_HEADS, RW_HEAD_DIM), 0.1),
        'rw_ln_w': 1.0 + nrm((L, RW_WIDTH), 0.02),
        'rw_ln_b': nrm((L, RW_WIDTH), 0.02),
        'w_br_dn': nrm((L, DN_WIDTH, D), DN_WIDTH ** -0.5),
        'w_br_rw': nrm((L, RW_WIDTH, D), RW_WIDTH ** -0.5),
        'w_out': nrm((L, D, D), D ** -0.5),
        'moe_w_group': nrm((L, D, MOE_GROUPS), D ** -0.5),
        'moe_b_group': nrm((L, MOE_GROUPS), 0.01),
        'moe_w_expert': nrm((L, D, N_EXPERTS), D ** -0.5),
        'moe_b_expert': nrm((L, N_EXPERTS), 0.01),
        'moe_w_gate': nrm((L, N_EXPERTS, D, EXPERT_FF), D ** -0.5),
        'moe_w_up': nrm((L, N_EXPERTS, D, EXPERT_FF), D ** -0.5),
        'moe_w_down': nrm((L, N_EXPERTS, EXPERT_FF, D), EXPERT_FF ** -0.5),
        'final_norm': 1.0 + nrm((D,), 0.02),
    }
    return inputs

def reference(x_prompt, x_sample, c_prompt, c_sample, w_ada, b_ada, norm1, norm2, w_in,
              dn_conv_w, dn_a_log, dn_dt_bias, dn_norm_w, rw_mu, rw_w0, rw_w2, rw_a0, rw_a2, rw_g2,
              rw_k_k, rw_k_a, rw_r_k, rw_ln_w, rw_ln_b, w_br_dn, w_br_rw, w_out,
              moe_w_group, moe_b_group, moe_w_expert, moe_b_expert, moe_w_gate, moe_w_up, moe_w_down,
              final_norm):
    layers = {
        'w_ada': w_ada, 'b_ada': b_ada, 'norm1': norm1, 'norm2': norm2, 'w_in': w_in,
        'dn_conv_w': dn_conv_w, 'dn_a_log': dn_a_log, 'dn_dt_bias': dn_dt_bias, 'dn_norm_w': dn_norm_w,
        'rw_mu': rw_mu, 'rw_w0': rw_w0, 'rw_w2': rw_w2, 'rw_a0': rw_a0, 'rw_a2': rw_a2, 'rw_g2': rw_g2,
        'rw_k_k': rw_k_k, 'rw_k_a': rw_k_a, 'rw_r_k': rw_r_k, 'rw_ln_w': rw_ln_w, 'rw_ln_b': rw_ln_b,
        'w_br_dn': w_br_dn, 'w_br_rw': w_br_rw, 'w_out': w_out,
        'moe_w_group': moe_w_group, 'moe_b_group': moe_b_group, 'moe_w_expert': moe_w_expert,
        'moe_b_expert': moe_b_expert, 'moe_w_gate': moe_w_gate, 'moe_w_up': moe_w_up, 'moe_w_down': moe_w_down,
    }
    y_prompt = encoder(x_prompt, c_prompt, layers, final_norm)
    y_sample = encoder(x_sample, c_sample, layers, final_norm)
    return (y_prompt, y_sample)


_drawn_inputs = setup_inputs


def setup_inputs(seed=0):
    import zlib

    import numpy as np

    out = dict(_drawn_inputs(seed))
    spreads = {}
    factors = {'norm1': 2.73,
     'dn_norm_w': 11.927,
     'rw_ln_w': 31.398,
     'rw_ln_b': 38.266,
     'moe_b_group': 64.0,
     'moe_b_expert': 31.033,
     'final_norm': 8.132,
     'norm2': 6.194,
     'rw_a0': 3.734,
     'rw_k_k': 3.303}
    for name, (base, spread) in spreads.items():
        noise = np.random.default_rng([zlib.crc32(name.encode()), seed]).standard_normal(out[name].shape)
        drawn = base * np.exp(spread * noise) if base else spread * noise
        out[name] = jnp.asarray(drawn.astype(out[name].dtype))
    for name, factor in factors.items():
        out[name] = (out[name] * factor).astype(out[name].dtype)
    return out
```

```python
import math
from contextlib import ExitStack

import concourse.bass as bass
from concourse import mybir

ALU = mybir.AluOpType
ACT = mybir.ActivationFunctionType
F32 = mybir.dt.float32
I32 = mybir.dt.int32
U32 = mybir.dt.uint32
AX = mybir.AxisListType.X
ds = bass.ds

P = 128
D = 1024
KD = D // P
SEQ = (1024, 512)
TOK = sum(SEQ)
NT = TOK // P
SEQS = ((0, SEQ[0] // P), (SEQ[0] // P, SEQ[1] // P))
BLK = 512
NB = TOK // BLK
DNH, DNW = 4, 512
RWH, RWW = 8, 512
DN_CONV = 5
QKV_T = 3 * DNW // P
Z0 = 3 * DNW
AB0 = 4 * DNW
RW0 = AB0 + 4 * DNH
RW_COLS = 3 * RWW + 128 + 64 + 128
RW_T = RW_COLS // P
G0 = RW0 + RW_COLS
IN_COLS = G0 + 2 * D
LEVELS = 7
NG, NPG, NE = 4, 8, 32
FF = 512
NBLOCKS = 2 * TOK // P + NE
SLOTS = NBLOCKS * P
HALF_DECAY = -math.exp(-0.5)


class Event:

    def __init__(self, sem, per=1, base=0, unit=1):
        self.sem, self.per, self.base, self.unit = sem, per, base, unit
        self.counted = 0

    def done(self, turn=0, k=None):
        k = self.per if k is None else k
        return turn * (self.per * self.unit) + (self.base + k) * self.unit

    def next(self):
        self.counted += 1
        return self.counted


class Env:

    def __init__(self, nc, ctx, io):
        self.nc, self.ctx, self.io = nc, ctx, io
        self.sems = []

    def sem(self, name):
        self.sems.append(self.nc.alloc_semaphore(name))
        return self.sems[-1]

    def recycle(self):
        self.nc.all_engine_barrier()
        self.nc.clear_and_free_semaphores(self.sems)
        self.nc.all_engine_barrier()
        self.sems = []

    def event(self, name, per=1, base=0, dma=False):
        return Event(self.sem(name), per, base, 16 if dma else 1)

    def keep(self, name, shape, dt=F32):
        return self.ctx.enter_context(self.nc.sbuf_tensor(name, shape, dt))


def tools(nc, ctx):
    def sb(name, shape, dt=F32):
        return ctx.enter_context(nc.sbuf_tensor(name, shape, dt))

    def pb(name, shape, dt=F32):
        return ctx.enter_context(nc.psum_tensor(name, shape, dt))

    return sb, pb


def settle_pool(pool, env):
    return pool.tensor_tensor(env.settled[:, 0:1], env.ones[:, 0:1], env.ones[:, 0:1], ALU.mult)


def spread(ap, n, axis=2):
    shape = list(ap.shape)
    shape.insert(axis, n)
    return ap.unsqueeze(axis).to_broadcast(shape)


V_CONV, V_MU, V_W0, V_A0, V_KK, V_KA, V_RK = 0, 60, 75, 83, 87, 91, 95
V_ROWS = 99


def constants(env):
    nc, io = env.nc, env.io
    env.ident = env.keep("ident", [P, P])
    env.ones = env.keep("ones", [P, P])
    env.settled = env.keep("settled", [P, 2])
    env.headones = env.keep("headones", [P, P])
    env.upper_incl = env.keep("upper_incl", [P, P])
    env.upper = env.keep("upper", [P, P])
    env.lower_incl = env.keep("lower_incl", [P, P])
    env.lower = env.keep("lower", [P, P])
    env.lower_level = env.keep("lower_level", [P, LEVELS, P])
    env.upper_level = env.keep("upper_level", [P, LEVELS, P])
    env.vec = env.keep("vec", [P, V_ROWS + 1])
    env.conv_w = env.keep("conv_w", [P, QKV_T * DN_CONV])
    env.mu_keep = env.keep("mu_keep", [P, RW_T + 1])
    env.mu_half = env.keep("mu_half", [P, RW_T + 1])
    env.ka_rest = env.keep("ka_rest", [P, 4])
    made = env.event("constants_made")
    rows_in = env.event("vec_rows_loaded", per=8, dma=True)
    turned = env.event("vec_turned")
    copied = env.event("vec_copied")
    rows_clear = env.event("vec_rows_clear")

    with ExitStack() as ctx:
        sb, pb = tools(nc, ctx)
        rows = sb("vec_rows", [P, P])
        turned_ps = pb("vec_ps", [P, P])
        block = ctx.enter_context(nc.Block())

        @block.gpsimd
        def _(pool):
            def keep_where(out, base, per_row, pattern):
                pool.affine_select(out=out, in_=out, compare_op=ALU.is_ge, fill=0.0, base=base,
                                        pattern=pattern, channel_multiplier=per_row).then_inc(made.sem, made.unit)
                pool.wait_ge(made.sem, made.next())

            pool.memset(env.ones[:], 1.0).then_inc(made.sem, made.unit)
            pool.wait_ge(made.sem, made.next())
            pool.memset(env.ident[:], 0.0).then_inc(made.sem, made.unit)
            pool.wait_ge(made.sem, made.next())
            pool.affine_select(out=env.ident[:], in_=env.ident[:], compare_op=ALU.not_equal, fill=1.0,
                                    base=0, pattern=[[-1, P]], channel_multiplier=1).then_inc(made.sem, made.unit)
            pool.wait_ge(made.sem, made.next())
            for m, base, per_row in ((env.upper_incl, 0, -1), (env.upper, -1, -1),
                                     (env.lower_incl, 0, 1), (env.lower, -1, 1)):
                pool.memset(m[:], 1.0).then_inc(made.sem, made.unit)
                pool.wait_ge(made.sem, made.next())
                keep_where(m[:], base, per_row, [[-per_row, P]])
            pool.memset(env.headones[:], 1.0).then_inc(made.sem, made.unit)
            pool.wait_ge(made.sem, made.next())
            by_head = env.headones[:].rearrange("p (b c) -> p b c", c=64)
            keep_where(by_head, 0, 1, [[-64, 2], [0, 64]])
            keep_where(by_head, 63, -1, [[64, 2], [0, 64]])
            for m, row_half, col_zero in ((env.lower_level, 1, 1), (env.upper_level, 0, 0)):
                pool.memset(m[:], 1.0).then_inc(made.sem, made.unit)
                pool.wait_ge(made.sem, made.next())
                for l in range(LEVELS):
                    s = 1 << l
                    v = m[:, l, :].rearrange("p (b h c) -> p b h c", h=2, c=s)
                    pool.memset(v[:, :, col_zero, :], 0.0).then_inc(made.sem, made.unit)
                    pool.wait_ge(made.sem, made.next())
                    v = m[:, l, :].rearrange("p (b c) -> p b c", c=2 * s)
                    keep_where(v, -s * row_half, 1, [[-2 * s, P // (2 * s)], [0, 2 * s]])
                    keep_where(v, s * (row_half + 1) - 1, -1, [[2 * s, P // (2 * s)], [0, 2 * s]])

        @block.sync
        def _(sp):
            sp.wait_ge(rows_clear.sem, rows_clear.done())
            conv = io["dn_conv_w"].rearrange("o k (t p) -> (o k t) p", p=P)
            sp.dma_start(rows[V_CONV:V_CONV + 60, :], conv).then_inc(rows_in.sem, rows_in.unit)
            mu = io["rw_mu"]
            sp.dma_start(rows[V_MU:V_MU + RW_T, :],
                                    mu[:, 0:RW_T * P].rearrange("o (t p) -> (o t) p", p=P)).then_inc(rows_in.sem, rows_in.unit)
            sp.dma_start(rows[V_MU + RW_T:V_MU + RW_T + 1, 0:RW_COLS - RW_T * P], mu[:, RW_T * P:RW_COLS]).then_inc(rows_in.sem, rows_in.unit)
            sp.dma_start(rows[V_W0:V_W0 + 8, :], io["rw_w0"].rearrange("o d (t p) -> (o d t) p", p=P)).then_inc(rows_in.sem, rows_in.unit)
            for at, name in ((V_A0, "rw_a0"), (V_KK, "rw_k_k"), (V_KA, "rw_k_a")):
                sp.dma_start(rows[at:at + 4, :], io[name].rearrange("o (t p) -> (o t) p", p=P)).then_inc(rows_in.sem, rows_in.unit)
            sp.dma_start(rows[V_RK:V_RK + 4, :],
                                    io["rw_r_k"].rearrange("o (t h) c -> (o t) (h c)", h=2)).then_inc(rows_in.sem, rows_in.unit)

        @block.tensor
        def _(pe):
            pe.wait_ge(made.sem, made.done(0, 3))
            pe.wait_ge(rows_in.sem, rows_in.done())
            pe.transpose(turned_ps[:, 0:V_ROWS + 1], rows[0:V_ROWS + 1, :], env.ident[0:V_ROWS + 1, 0:V_ROWS + 1]).then_inc(turned.sem, turned.unit)

        @block.vector
        def _(dve):
            dve.memset(rows[:], 0.0).then_inc(rows_clear.sem, rows_clear.unit)
            dve.wait_ge(turned.sem, turned.done())
            v = env.vec
            dve.tensor_copy(v[:], turned_ps[:, 0:V_ROWS + 1]).then_inc(copied.sem, copied.unit)
            dve.wait_ge(copied.sem, copied.done())
            dve.tensor_copy(env.conv_w[:].rearrange("p (t k) -> p t k", k=DN_CONV),
                            v[:, V_CONV:V_CONV + 60].rearrange("p (k t) -> p t k", t=QKV_T))
            mu = v[:, V_MU:V_MU + RW_T + 1]
            dve.tensor_scalar(env.mu_keep[:], mu, -1.0, 1.0, ALU.mult, ALU.add)
            dve.tensor_scalar(env.mu_half[:], mu, 0.5, None, ALU.mult)
            dve.tensor_scalar(env.ka_rest[:], v[:, V_KA:V_KA + 4], -1.0, 1.0, ALU.mult, ALU.add)


def ada(env):
    nc, io = env.nc, env.io
    NC = 6 * D // BLK
    c_in = env.event("ada_c_loaded", per=3, dma=True)
    c_ready = env.event("ada_c_ready")
    w_in = [env.event(f"ada_w_loaded{s}", dma=True) for s in range(2)]
    summed = env.event("ada_summed", per=2)
    added = env.event("ada_added", per=2)
    stored = env.event("ada_stored", dma=True)
    with ExitStack() as ctx:
        sb, pb = tools(nc, ctx)
        c_raw = sb("ada_c_raw", [P, 2, KD])
        c_act = sb("ada_c", [P, 2, KD])
        bias = sb("ada_bias", [2, 6 * D])
        w = sb("ada_w", [P, 2, KD, BLK])
        out = sb("ada_out", [2, 6 * D])
        ps = [pb(f"ada_ps{s}", [2, BLK]) for s in range(2)]
        w_view = io["w_ada"].rearrange("o (p k) n -> (o p) k n", k=KD)
        block = ctx.enter_context(nc.Block())

        @block.sync
        def _(sp):
            sp.dma_start(c_raw[:, 0, :], io["c_prompt"].rearrange("o (p k) -> (o p) k", k=KD)).then_inc(c_in.sem, c_in.unit)
            sp.dma_start(c_raw[:, 1, :], io["c_sample"].rearrange("o (p k) -> (o p) k", k=KD)).then_inc(c_in.sem, c_in.unit)
            sp.dma_start(bias[:], io["b_ada"].to_broadcast([2, 6 * D])).then_inc(c_in.sem, c_in.unit)
            for s in range(2):
                sp.dma_start(w[:, s], w_view[:, :, s * BLK:(s + 1) * BLK]).then_inc(w_in[s].sem, w_in[s].unit)
            with sp.Fori(1, NC // 2) as i:
                for s in range(2):
                    sp.wait_ge(summed.sem, summed.done(i - 1, s + 1))
                    sp.dma_start(w[:, s], w_view[:, :, ds((i * 2 + s) * BLK, BLK)]).then_inc(w_in[s].sem, w_in[s].unit)
            sp.wait_ge(added.sem, added.done(NC // 2 - 1))
            sp.dma_start(io["ada_rows"], out[:]).then_inc(stored.sem, stored.unit)
            sp.wait_ge(stored.sem, stored.done())

        @block.scalar
        def _(act):
            act.wait_ge(c_in.sem, c_in.done())
            act.activation(c_act[:], c_raw[:], ACT.Silu).then_inc(c_ready.sem, c_ready.unit)

        @block.tensor
        def _(pe):
            pe.wait_ge(c_ready.sem, c_ready.done())
            with pe.Fori(0, NC // 2) as i:
                for s in range(2):
                    pe.wait_ge(w_in[s].sem, w_in[s].done(i))
                    pe.wait_ge(added.sem, added.done(i, s)) if s else None
                    for k in range(KD):
                        mm = pe.matmul(ps[s][:], c_act[:, :, k], w[:, s, k, :], start=(k == 0), stop=(k == KD - 1))
                    mm.then_inc(summed.sem, summed.unit)
                pe.wait_ge(added.sem, added.done(i))

        @block.vector
        def _(dve):
            with dve.Fori(0, NC // 2) as i:
                for s in range(2):
                    dve.wait_ge(summed.sem, summed.done(i, s + 1))
                    cols = ds((i * 2 + s) * BLK, BLK)
                    dve.tensor_tensor(out[:, cols], ps[s][:], bias[:, cols], ALU.add).then_inc(added.sem, added.unit)


def norm_in(env, ctx):
    nc, io = env.nc, env.io
    env.hT = ctx.enter_context(nc.sbuf_tensor("hT", [P, KD, TOK], F32))
    cols_in = env.event("n1_cols_loaded", per=5, dma=True)
    gain_ready = env.event("n1_gain_ready")
    x_in = env.event("n1_x_loaded", dma=True)
    squared = env.event("n1_squared")
    meaned = env.event("n1_meaned")
    rooted = env.event("n1_rooted")
    inverted = env.event("n1_inverted")
    scaled = env.event("n1_scaled")
    turned = env.event("n1_turned")
    multiplied = env.event("n1_multiplied")
    shifted = env.event("n1_shifted")
    with ExitStack() as inner:
        sb, pb = tools(nc, inner)
        norm1 = sb("n1_norm", [P, KD])
        shift = sb("n1_shift", [P, 2, KD])
        scale = sb("n1_scale", [P, 2, KD])
        gain = sb("n1_gain", [P, 2, KD])
        x = sb("n1_x", [P, D])
        sq = sb("n1_sq", [P, D])
        ss = sb("n1_ss", [P, 1])
        mean = sb("n1_mean", [P, 1])
        root = sb("n1_root", [P, 1])
        rstd = sb("n1_rstd", [P, 1])
        xn = sb("n1_xn", [P, D])
        xT = pb("n1_xT", [P, KD, P])
        part = io["ada_rows"].rearrange("g (s p k) -> s g p k", s=6, k=KD)
        block = inner.enter_context(nc.Block())

        @block.sync
        def _(sp):
            sp.dma_start(norm1[:], io["norm1"].rearrange("o (p k) -> (o p) k", k=KD)).then_inc(cols_in.sem, cols_in.unit)
            for g in range(2):
                sp.dma_start(shift[:, g, :], part[0, g]).then_inc(cols_in.sem, cols_in.unit)
                sp.dma_start(scale[:, g, :], part[1, g]).then_inc(cols_in.sem, cols_in.unit)
            sp.dma_start(x[:], io["x_prompt"][0, 0:P, :]).then_inc(x_in.sem, x_in.unit)
            for g, (t0, n) in enumerate(SEQS):
                src = io["x_prompt"][0] if g == 0 else io["x_sample"][0]
                first = 1 if g == 0 else 0
                with sp.Fori(first, n) as t:
                    sp.wait_ge(scaled.sem, scaled.done(t + t0 - 1))
                    sp.dma_start(x[:], src[ds(t * P, P), :]).then_inc(x_in.sem, x_in.unit)

        @block.scalar
        def _(act):
            with act.Fori(0, NT) as t:
                act.wait_ge(x_in.sem, x_in.done(t))
                act.activation(sq[:], x[:], ACT.Square, accum_out=ss[:]).then_inc(squared.sem, squared.unit)
                act.wait_ge(meaned.sem, meaned.done(t))
                act.activation(root[:], mean[:], ACT.Sqrt).then_inc(rooted.sem, rooted.unit)

        @block.tensor
        def _(pe):
            with pe.Fori(0, NT) as t:
                pe.wait_ge(scaled.sem, scaled.done(t))
                for k in range(KD):
                    mm = pe.transpose(xT[:, k, :], xn[:].rearrange("t (p k) -> t k p", k=KD)[:, k, :], env.ident[:])
                mm.then_inc(turned.sem, turned.unit)
                pe.wait_ge(multiplied.sem, multiplied.done(t))

        @block.vector
        def _(dve):
            dve.wait_ge(cols_in.sem, cols_in.done())
            dve.tensor_scalar(scale[:], scale[:], 1.0, None, ALU.add).then_inc(gain_ready.sem, gain_ready.unit)
            dve.wait_ge(gain_ready.sem, gain_ready.done(0, 1))
            dve.tensor_tensor(gain[:], scale[:], norm1[:].unsqueeze(1).to_broadcast([P, 2, KD]), ALU.mult).then_inc(gain_ready.sem, gain_ready.unit)
            dve.wait_ge(gain_ready.sem, gain_ready.done(0, 2))
            for g, (t0, n) in enumerate(SEQS):
                with dve.Fori(t0, t0 + n) as t:
                    dve.wait_ge(squared.sem, squared.done(t))
                    dve.tensor_scalar(mean[:], ss[:], 1.0 / D, 1e-6, ALU.mult, ALU.add).then_inc(meaned.sem, meaned.unit)
                    dve.wait_ge(rooted.sem, rooted.done(t))
                    dve.reciprocal(rstd[:], root[:]).then_inc(inverted.sem, inverted.unit)
                    dve.wait_ge(inverted.sem, inverted.done(t))
                    dve.tensor_scalar(xn[:], x[:], rstd[:, 0:1], None, ALU.mult).then_inc(scaled.sem, scaled.unit)
                    dve.wait_ge(turned.sem, turned.done(t))
                    h = env.hT[:, :, ds(t * P, P)]
                    dve.tensor_tensor(h, xT[:], spread(gain[:, g, :], P), ALU.mult).then_inc(multiplied.sem, multiplied.unit)
                    dve.wait_ge(multiplied.sem, multiplied.done(t))
                    dve.tensor_tensor(h, h, spread(shift[:, g, :], P), ALU.add).then_inc(shifted.sem, shifted.unit)


def project(env):
    nc, io = env.nc, env.io
    kinds = (("conv", 0, QKV_T, P), ("silu", Z0, DNW // P, P), ("shift", RW0, RW_T, P),
             ("sigmoid", G0, 2 * D // P, P), ("shift", RW0 + RW_T * P, 1, RW_COLS - RW_T * P),
             ("copy", AB0, 1, 4 * DNH))
    w_in = [env.event(f"pj_w_loaded{s}", dma=True) for s in range(2)]
    summed = env.event("pj_summed")
    drained = env.event("pj_drained", per=2)
    padded = env.event("pj_padded")
    tapped = env.event("pj_tapped", per=5)
    shaped = env.event("pj_shaped", per=3)
    ready = env.event("pj_ready")
    stored = [env.event(f"pj_stored{s}", per=2, dma=True) for s in range(2)]
    GAP = 4
    S0 = 2 + SEQ[0] + GAP
    WIDE = S0 + SEQ[1] + 2
    OUTW = WIDE - GAP
    OUT1 = S0 - 2
    w_view = io["w_in"].rearrange("o (p k) n -> (o p) k n", k=KD)

    with ExitStack() as ctx:
        sb, pb = tools(nc, ctx)
        w = [sb(f"pj_w{s}", [P, KD, P]) for s in range(2)]
        raw = [sb(f"pj_raw{s}", [P, WIDE]) for s in range(2)]
        mid = sb("pj_mid", [P, OUTW])
        out = [sb(f"pj_out{s}", [P, OUTW]) for s in range(2)]
        ps = [pb(f"pj_ps{s}", [P, NB, BLK]) for s in range(2)]
        block = ctx.enter_context(nc.Block())

        runs, n = [], 0
        for kind, c0, tiles, width in kinds:
            runs.append((kind, c0, tiles, width, n))
            n += tiles
        total = n

        @block.sync
        def _(sp):
            for kind, c0, tiles, width, n0 in runs:
                if tiles == 1:
                    s = n0 % 2
                    sp.wait_ge(summed.sem, summed.done(n0 - 2))
                    sp.dma_start(w[s][:, :, 0:width], w_view[:, :, c0:c0 + width]).then_inc(w_in[s].sem, w_in[s].unit)
                    continue
                if n0 == 0:
                    for s in range(2):
                        sp.dma_start(w[s][:], w_view[:, :, c0 + s * P:c0 + (s + 1) * P]).then_inc(w_in[s].sem, w_in[s].unit)
                with sp.Fori(1 if n0 == 0 else 0, tiles // 2) as i:
                    for s in range(2):
                        sp.wait_ge(summed.sem, summed.done(n0 - 2 + i * 2 + s))
                        sp.dma_start(w[s][:], w_view[:, :, ds(c0 + (i * 2 + s) * P, P)]).then_inc(w_in[s].sem, w_in[s].unit)

        @block.tensor
        def _(pe):
            for kind, c0, tiles, width, n0 in runs:
                def tile(s, i, n, wait_drained=True):
                    pe.wait_ge(w_in[s].sem, w_in[s].done(i))
                    if wait_drained:
                        pe.wait_ge(drained.sem, drained.done(n - 2))
                    for b in range(NB):
                        for k in range(KD):
                            mm = pe.matmul(ps[s][0:width, b, :], w[s][:, k, 0:width], env.hT[:, k, b * BLK:(b + 1) * BLK],
                                           start=(k == 0), stop=(k == KD - 1))
                    mm.then_inc(summed.sem, summed.unit)
                if tiles == 1:
                    tile(n0 % 2, n0 // 2, n0)
                    continue
                if n0 == 0:
                    tile(0, 0, 0, False)
                    tile(1, 0, 1, False)
                with pe.Fori(1 if n0 == 0 else 0, tiles // 2) as i:
                    for s in range(2):
                        tile(s, n0 // 2 + i, n0 + i * 2 + s)

        def columns(t):
            return (t[:, 0:SEQ[0]], t[:, OUT1:OUT1 + SEQ[1]])

        @block.scalar
        def _(act):
            act.wait_ge(padded.sem, padded.done(0, 2))
            shaped_base = 0
            for kind, c0, tiles, width, n0 in runs:
                def tile(s, i, n, c, m, first=False):
                    act.wait_ge(summed.sem, summed.done(n))
                    rows = slice(0, width)
                    flat = ps[s][rows].rearrange("p b t -> p (b t)")
                    if not first:
                        act.wait_ge(stored[s].sem, stored[s].done(i - 1))
                    if kind in ("conv", "shift"):
                        targets = (raw[s][rows, 2:2 + SEQ[0]], raw[s][rows, S0:S0 + SEQ[1]])
                        func = ACT.Identity
                    else:
                        targets = columns(out[s][rows])
                        func = {"silu": ACT.Silu, "sigmoid": ACT.Sigmoid, "copy": ACT.Identity}[kind]
                    for dst, src in zip(targets, (flat[:, 0:SEQ[0]], flat[:, SEQ[0]:TOK])):
                        act.activation(dst, src, func).then_inc(drained.sem, drained.unit)
                    if kind == "conv":
                        act.wait_ge(tapped.sem, tapped.done(n))
                        act.activation(out[s][:], mid[:], ACT.Silu).then_inc(ready.sem, ready.unit)
                        act.wait_ge(ready.sem, ready.done(n))
                    elif kind == "shift":
                        act.wait_ge(shaped.sem, shaped.done(m))
                    else:
                        act.wait_ge(drained.sem, drained.done(n))
                    dst = io["ch"][ds(c0 + c * P, width), :]
                    for (a, b), src in zip(((0, SEQ[0]), (SEQ[0], TOK)), columns(out[s][0:width])):
                        act.dma_start(dst[:, a:b], src).then_inc(stored[s].sem, stored[s].unit)
                if tiles == 1:
                    tile(n0 % 2, n0 // 2, n0, 0, shaped_base)
                else:
                    if n0 == 0:
                        tile(0, 0, 0, 0, 0, True)
                        tile(1, 0, 1, 1, 1, True)
                    with act.Fori(1 if n0 == 0 else 0, tiles // 2) as i:
                        for s in range(2):
                            tile(s, n0 // 2 + i, n0 + i * 2 + s, i * 2 + s, shaped_base + i * 2 + s)
                if kind == "shift":
                    shaped_base += tiles
            for s in range(2):
                act.wait_ge(stored[s].sem, stored[s].done((total - 1 - s) // 2))

        @block.vector
        def _(dve):
            for s in range(2):
                dve.memset(raw[s][:], 0.0).then_inc(padded.sem, padded.unit)
            shaped_base = 0
            for kind, c0, tiles, width, n0 in runs:
                if kind not in ("conv", "shift"):
                    continue
                rows = slice(0, width)

                def conv(s, n, c):
                    dve.wait_ge(drained.sem, drained.done(n))
                    taps = env.conv_w
                    dve.tensor_scalar(mid[:], raw[s][:, 0:OUTW], taps[:, ds(c * DN_CONV, 1)], None, ALU.mult).then_inc(tapped.sem, tapped.unit)
                    for k in range(1, DN_CONV):
                        dve.wait_ge(tapped.sem, tapped.done(n, k))
                        dve.scalar_tensor_tensor(mid[:], raw[s][:, k:k + OUTW], taps[:, ds(c * DN_CONV + k, 1)],
                                                           mid[:], ALU.mult, ALU.add).then_inc(tapped.sem, tapped.unit)

                def shift(s, n, m, c):
                    dve.wait_ge(drained.sem, drained.done(n))
                    x = raw[s][rows]
                    dve.tensor_tensor(mid[rows], x[:, 1:1 + OUTW], x[:, 3:3 + OUTW], ALU.add).then_inc(shaped.sem, shaped.unit)
                    dve.tensor_scalar(out[s][rows], x[:, 2:2 + OUTW], env.mu_keep[rows, ds(c, 1)], None, ALU.mult).then_inc(shaped.sem, shaped.unit)
                    dve.wait_ge(shaped.sem, shaped.done(m, 2))
                    dve.scalar_tensor_tensor(out[s][rows], mid[rows], env.mu_half[rows, ds(c, 1)], out[s][rows],
                                                       ALU.mult, ALU.add).then_inc(shaped.sem, shaped.unit)

                if kind == "conv":
                    conv(0, 0, 0)
                    dve.wait_ge(ready.sem, ready.done(0))
                    conv(1, 1, 1)
                    with dve.Fori(1, tiles // 2) as i:
                        for s in range(2):
                            dve.wait_ge(ready.sem, ready.done(i * 2 + s - 1))
                            conv(s, i * 2 + s, i * 2 + s)
                    dve.wait_ge(ready.sem, ready.done(tiles - 1))
                elif tiles == 1:
                    shift(n0 % 2, n0, shaped_base, RW_T)
                    shaped_base += 1
                else:
                    with dve.Fori(0, tiles // 2) as i:
                        for s in range(2):
                            shift(s, n0 + i * 2 + s, shaped_base + i * 2 + s, i * 2 + s)
                            dve.wait_ge(shaped.sem, shaped.done(shaped_base + i * 2 + s))
                    shaped_base += tiles


HALF = DNH * P


class Solver:

    def __init__(self, env, name, sb, sum_p, sum_x):
        self.a = sb(f"{name}_a", [P, 4, P])
        self.at = sb(f"{name}_at", [P, 4, P])
        self.x = sb(f"{name}_x", [P, 2, 4, P])
        self.p = sb(f"{name}_p", [P, 4, P])
        self.sum_p, self.sum_x = sum_p, sum_x
        self.x_ready = env.event(f"{name}_x_ready", per=3 + LEVELS - 1)
        self.p_summed = env.event(f"{name}_p_summed", per=LEVELS - 1)
        self.p_masked = env.event(f"{name}_p_masked", per=LEVELS - 1)
        self.x_summed = env.event(f"{name}_x_summed", per=LEVELS - 1)

    @property
    def xt(self):
        return self.x[:, 1]

    def start(self, dve, turn, ident, mask, mask_t):
        dve.tensor_tensor(self.x[:, 0], self.a[:], mask[:, 0:1, :].to_broadcast([P, 4, P]), ALU.mult).then_inc(self.x_ready.sem, self.x_ready.unit)
        dve.tensor_tensor(self.x[:, 1], self.at[:], mask_t[:, 0:1, :].to_broadcast([P, 4, P]), ALU.mult).then_inc(self.x_ready.sem, self.x_ready.unit)
        dve.wait_ge(self.x_ready.sem, self.x_ready.done(turn, 2))
        flat = self.x[:].rearrange("p x c n -> p (x c) n")
        dve.tensor_tensor(flat, flat, ident[:].unsqueeze(1).to_broadcast([P, 8, P]), ALU.add).then_inc(self.x_ready.sem, self.x_ready.unit)

    def multiply_p(self, pe, turn, level):
        pe.wait_ge(self.x_ready.sem, self.x_ready.done(turn, 2 + level))
        for c in range(4):
            mm = pe.matmul(self.sum_p[:, c, :], self.at[:, c, :], self.x[:, 0, c, :], start=True, stop=True)
        mm.then_inc(self.p_summed.sem, self.p_summed.unit)

    def mask_p(self, dve, turn, level, mask):
        dve.wait_ge(self.p_summed.sem, self.p_summed.done(turn, level))
        dve.tensor_tensor(self.p[:], self.sum_p, mask[:, level:level + 1, :].to_broadcast([P, 4, P]), ALU.mult).then_inc(self.p_masked.sem, self.p_masked.unit)

    def multiply_x(self, pe, turn, level):
        pe.wait_ge(self.p_masked.sem, self.p_masked.done(turn, level))
        for c in range(4):
            if level < LEVELS - 1:
                pe.matmul(self.sum_x[:, 0, c, :], self.x[:, 1, c, :], self.p[:, c, :], start=True, stop=True)
            mm = pe.matmul(self.sum_x[:, 1, c, :], self.p[:, c, :], self.x[:, 1, c, :], start=True, stop=True)
        mm.then_inc(self.x_summed.sem, self.x_summed.unit)

    def add_x(self, dve, turn, level):
        dve.wait_ge(self.x_summed.sem, self.x_summed.done(turn, level))
        which = slice(0, 2) if level < LEVELS - 1 else slice(1, 2)
        v = self.x[:, which].rearrange("p x c n -> p (x c) n")
        dve.tensor_tensor(v, v, self.sum_x[:, which].rearrange("p x c n -> p (x c) n"), ALU.add).then_inc(self.x_ready.sem, self.x_ready.unit)

    def solved(self, eng, turn):
        eng.wait_ge(self.x_ready.sem, self.x_ready.done(turn))


def solve_products(pe, solvers, turn):
    for level in range(1, LEVELS):
        for s in solvers:
            s.multiply_p(pe, turn, level)
        for s in solvers:
            s.multiply_x(pe, turn, level)


def solve_sums(dve, solvers, turn, masks):
    for level in range(1, LEVELS):
        for s, m in zip(solvers, masks):
            s.mask_p(dve, turn, level, m)
        for s in solvers:
            s.add_x(dve, turn, level)


def delta(env):
    nc, io = env.nc, env.io
    E = env.event
    qkv_in = E("dn_qkv_loaded", per=2, dma=True)
    rows_in = E("dn_rows_loaded", per=2, dma=True)
    neg_a_ready = E("dn_neg_a_ready")
    taken = E("dn_taken")
    read_out = E("dn_read_out", per=3)
    norm_steps = E("dn_norm_steps", per=4)
    rooted = E("dn_rooted")
    k_ready = E("dn_k_ready", per=2)
    gate_steps = E("dn_gate_steps", per=5)
    gate_act = E("dn_gate_act", per=3)
    summed_g = E("dn_g_summed")
    g_copied = E("dn_g_copied", per=3)
    decay_steps = E("dn_decay_steps", per=3)
    decayed = E("dn_decayed", per=2)
    small_exp = E("dn_small_exp", per=3)
    turned_kq = E("dn_kq_turned")
    kq_copied = E("dn_kq_copied", per=2)
    crossed = E("dn_crossed")
    masked = E("dn_masked", per=5)
    scaled = E("dn_scaled", per=11)
    a_ready = E("dn_a_ready", per=4)
    at_turned = E("dn_at_turned")
    at_copied = E("dn_at_copied", per=2)
    w_summed = E("dn_w_summed", per=2)
    w_copied = E("dn_w_copied", per=2)
    out_summed = E("dn_out_summed", per=3)
    o_kept = E("dn_o_kept")
    out_ready = E("dn_out_ready", per=5)
    rec_stored = E("dn_rec_stored", per=2, dma=True)

    with ExitStack() as ctx:
        sb, pb = tools(nc, ctx)
        bank = pb("dn_banks", [P, 8, 4, P])
        qkvT = sb("dn_qkvT", [P, QKV_T, P])
        abT = sb("dn_abT", [4 * DNH, P])
        dt_bias = sb("dn_dt_bias", [P, 8])
        neg_a = sb("dn_neg_a", [P, 8])
        sq = sb("dn_sq", [P, 8, P])
        ss = sb("dn_ss", [P, 8])
        root = sb("dn_root", [P, 8])
        rnorm = sb("dn_rnorm", [P, 8])
        v = sb("dn_v", [P, DNH, P])
        qk = sb("dn_qk", [P, 2, DNH, P])
        qkT = sb("dn_qkT", [P, 2, DNH, P])
        ab = sb("dn_ab", [P, 16])
        soft = sb("dn_soft", [P, 4, 8])
        la = sb("dn_la", [P, 8])
        beta = sb("dn_beta", [P, 8])
        g = sb("dn_g", [P, 16])
        tail = sb("dn_tail", [P, 8])
        eg = sb("dn_eg", [P, 8])
        etail = sb("dn_etail", [P, 8])
        etot = sb("dn_etot", [P, 8])
        neg_beta = sb("dn_neg_beta", [P, 8])
        neg_beg = sb("dn_neg_beg", [P, 8])
        diff = sb("dn_diff", [P, 8, P])
        dpos = sb("dn_dpos", [P, 8, P])
        decay = sb("dn_decay", [P, 8, P])
        decayT = sb("dn_decayT", [P, 8, P])
        qkm = sb("dn_qkm", [P, 8, P])
        rhs = sb("dn_rhs", [P, 8, 2, P])
        qe = sb("dn_qe", [P, 8, P])
        kt = sb("dn_kt", [P, 8, P])
        diag = sb("dn_diag", [P, 8, P])
        w = sb("dn_w", [P, 8, 2, P])
        rec = sb("dn_rec", [P, 2, 3, DNH, P])
        sf = Solver(env, "dn_sf", sb, bank[:, 6], bank[:, 0:2])
        sr = Solver(env, "dn_sr", sb, bank[:, 7], bank[:, 2:4])
        block = ctx.enter_context(nc.Block())
        lead = (env.upper_incl, env.lower_incl)

        def dirs(m):
            return m[:].rearrange("p (d h) n -> p d h n", d=2)

        def per_head(v8):
            return spread(v8, P)

        @block.sync
        def _(sp):
            sp.dma_start(dt_bias[:], io["dn_dt_bias"].rearrange("o d h -> o (d h)").to_broadcast([P, 8])).then_inc(rows_in.sem, rows_in.unit)
            sp.dma_start(neg_a[:], io["dn_a_log"].rearrange("o d h -> o (d h)").to_broadcast([P, 8])).then_inc(rows_in.sem, rows_in.unit)

            def load(t):
                cols = ds(t * P, P)
                sp.dma_start(qkvT[:], io["ch"][0:3 * DNW, cols].rearrange("(c p) t -> p c t", p=P)).then_inc(qkv_in.sem, qkv_in.unit)
                sp.dma_start(abT[:], io["ch"][AB0:RW0, cols]).then_inc(qkv_in.sem, qkv_in.unit)

            load(0)

            def store(t):
                sp.wait_ge(out_ready.sem, out_ready.done(t))
                for d in range(2):
                    sp.dma_start(io["dn_rec"][ds(t * 2 + d, 1)].rearrange("a p x -> p (a x)"),
                                               rec[:, d].rearrange("p x c n -> p (x c n)")).then_inc(rec_stored.sem, rec_stored.unit)

            with sp.Fori(1, NT) as t:
                sp.wait_ge(taken.sem, taken.done(t - 1))
                load(t)
                store(t - 1)
            store(NT - 1)
            sp.wait_ge(rec_stored.sem, rec_stored.done(NT - 1))

        @block.tensor
        def _(pe):
            ident = env.ident[:]
            pe.wait_ge(neg_a_ready.sem, neg_a_ready.done())
            with pe.Fori(0, NT) as t:
                pe.wait_ge(qkv_in.sem, qkv_in.done(t))
                for c in range(QKV_T):
                    pe.transpose(bank[:, c // 4, c % 4, :], qkvT[:, c, :], ident)
                pe.transpose(bank[:, 3, 0, 0:16], abT[:], ident[0:16, 0:16]).then_inc(taken.sem, taken.unit)
                pe.wait_ge(gate_steps.sem, gate_steps.done(t))
                for d in range(2):
                    pe.matmul(bank[:, 3, 1, 4 * d:4 * d + 4], lead[d][:], la[:, 4 * d:4 * d + 4], start=True, stop=True)
                pe.matmul(bank[:, 3, 1, 8:16], env.ones[:], la[:], start=True, stop=True)
                for c in range(8):
                    mm = pe.matmul(bank[:, 4 + c // 4, c % 4, :], la[:, c:c + 1].to_broadcast([P, P]), lead[c // 4][:],
                                   start=True, stop=True)
                mm.then_inc(summed_g.sem, summed_g.unit)
                pe.wait_ge(k_ready.sem, k_ready.done(t))
                for c in range(8):
                    tr = pe.transpose(bank[:, 6 + c // 4, c % 4, :], qk[:, c // 4, c % 4, :], ident)
                tr.then_inc(turned_kq.sem, turned_kq.unit)
                pe.wait_ge(kq_copied.sem, kq_copied.done(t))
                for h in range(DNH):
                    pe.matmul(bank[:, 0, h, :], qkT[:, 1, h, :], qkT[:, 1, h, :], start=True, stop=True)
                    mm = pe.matmul(bank[:, 1, h, :], qkT[:, 1, h, :], qkT[:, 0, h, :], start=True, stop=True)
                mm.then_inc(crossed.sem, crossed.unit)
                pe.wait_ge(a_ready.sem, a_ready.done(t))
                for c in range(8):
                    s = (sf, sr)[c // 4]
                    tr = pe.transpose(bank[:, 4 + c // 4, c % 4, :], s.a[:, c % 4, :], ident)
                tr.then_inc(at_turned.sem, at_turned.unit)
                solve_products(pe, (sf, sr), t)
                pe.wait_ge(scaled.sem, scaled.done(t))
                for d, s in enumerate((sf, sr)):
                    s.solved(pe, t)
                    for h in range(DNH):
                        mm = pe.matmul(bank[:, 2 * d + h // 2, 2 * (h % 2):2 * (h % 2) + 2, :], s.xt[:, h, :],
                                       rhs[:, 4 * d + h], start=True, stop=True)
                    mm.then_inc(w_summed.sem, w_summed.unit)
                pe.wait_ge(w_copied.sem, w_copied.done(t))
                for h in range(DNH):
                    for d in range(2):
                        c = 4 * d + h
                        mm = pe.matmul(bank[:, 6, h, :], qkm[:, c, :], w[:, c, 0, :], start=(d == 0), stop=(d == 1))
                mm.then_inc(out_summed.sem, out_summed.unit)
                for c in range(8):
                    d, h = c // 4, c % 4
                    pe.matmul(bank[:, 4 + d, h, :], qe[:, c, :], ident, start=True, stop=False)
                    mm = pe.matmul(bank[:, 4 + d, h, :], w[:, c, 1, :], qkm[:, c, :], start=False, stop=True)
                mm.then_inc(out_summed.sem, out_summed.unit)
                for c in range(8):
                    d, h = c // 4, c % 4
                    pe.matmul(bank[:, d, h, :], w[:, c, 1, :], kt[:, c, :], start=True, stop=True)
                    mm = pe.matmul(bank[:, 2 + d, h, :], kt[:, c, :], w[:, c, 0, :], start=True, stop=True)
                mm.then_inc(out_summed.sem, out_summed.unit)
                pe.wait_ge(o_kept.sem, o_kept.done(t))
                pe.wait_ge(out_ready.sem, out_ready.done(t))

        @block.scalar
        def _(act):
            act.wait_ge(rows_in.sem, rows_in.done())
            act.activation(neg_a[:], neg_a[:], ACT.Exp).then_inc(neg_a_ready.sem, neg_a_ready.unit)
            with act.Fori(0, NT) as t:
                act.wait_ge(taken.sem, taken.done(t))
                act.activation(ab[:], bank[:, 3, 0, 0:16], ACT.Identity).then_inc(read_out.sem, read_out.unit)
                act.activation(v[:], bank[:, 2], ACT.Identity).then_inc(read_out.sem, read_out.unit)
                act.activation(sq[:], bank[:, 0:2].rearrange("p b c n -> p (b c) n"), ACT.Square).then_inc(read_out.sem, read_out.unit)
                act.wait_ge(gate_steps.sem, gate_steps.done(t, 2))
                act.activation(soft[:, 2, :], soft[:, 1, :], ACT.Exp, scale=-1.0).then_inc(gate_act.sem, gate_act.unit)
                act.wait_ge(gate_act.sem, gate_act.done(t, 1))
                act.activation(soft[:, 3, :], soft[:, 2, :], ACT.Ln, bias=1.0).then_inc(gate_act.sem, gate_act.unit)
                act.wait_ge(norm_steps.sem, norm_steps.done(t, 2))
                act.activation(root[:], ss[:], ACT.Sqrt).then_inc(rooted.sem, rooted.unit)
                act.activation(beta[:], ab[:, 8:16], ACT.Sigmoid).then_inc(gate_act.sem, gate_act.unit)
                act.wait_ge(turned_kq.sem, turned_kq.done(t))
                for x in range(2):
                    act.activation(qkT[:, x], bank[:, 6 + x], ACT.Identity).then_inc(kq_copied.sem, kq_copied.unit)
                act.wait_ge(decay_steps.sem, decay_steps.done(t))
                act.activation(decay[:], dpos[:], ACT.Exp, scale=-1.0).then_inc(decayed.sem, decayed.unit)
                act.activation(decayT[:], diff[:], ACT.Exp).then_inc(decayed.sem, decayed.unit)
                act.wait_ge(g_copied.sem, g_copied.done(t))
                act.activation(eg[:], g[:, 0:8], ACT.Exp).then_inc(small_exp.sem, small_exp.unit)
                act.activation(etail[:], tail[:], ACT.Exp).then_inc(small_exp.sem, small_exp.unit)
                act.activation(etot[:], g[:, 8:16], ACT.Exp).then_inc(small_exp.sem, small_exp.unit)
                act.wait_ge(at_turned.sem, at_turned.done(t))
                for d, s in enumerate((sf, sr)):
                    act.activation(s.at[:], bank[:, 4 + d], ACT.Identity).then_inc(at_copied.sem, at_copied.unit)
                for d in range(2):
                    act.wait_ge(w_summed.sem, w_summed.done(t, d + 1))
                    act.activation(w[:, 4 * d:4 * d + 4].rearrange("p c x n -> p (c x) n"),
                                               bank[:, 2 * d:2 * d + 2].rearrange("p b c n -> p (b c) n"), ACT.Identity).then_inc(w_copied.sem, w_copied.unit)
                act.wait_ge(out_summed.sem, out_summed.done(t, 2))
                act.wait_ge(rec_stored.sem, rec_stored.done(t, 0))
                act.activation(rec[:, :, 0], bank[:, 4:6], ACT.Identity).then_inc(out_ready.sem, out_ready.unit)
                act.wait_ge(out_summed.sem, out_summed.done(t, 3))
                for d in range(2):
                    act.activation(rec[:, d, 2], bank[:, 2 + d], ACT.Identity).then_inc(out_ready.sem, out_ready.unit)

        @block.vector
        def _(dve):
            dve.wait_ge(neg_a_ready.sem, neg_a_ready.done())
            with dve.Fori(0, NT) as t:
                dve.wait_ge(read_out.sem, read_out.done(t, 1))
                dve.tensor_tensor(soft[:, 0, :], ab[:, 0:8], dt_bias[:], ALU.add).then_inc(gate_steps.sem, gate_steps.unit)
                dve.wait_ge(gate_steps.sem, gate_steps.done(t, 1))
                dve.scalar_tensor_tensor(soft[:, 1, :], soft[:, 0, :], -1.0, soft[:, 0, :], ALU.mult, ALU.max).then_inc(gate_steps.sem, gate_steps.unit)
                dve.tensor_scalar(soft[:, 0, :], soft[:, 0, :], 0.0, None, ALU.max).then_inc(gate_steps.sem, gate_steps.unit)
                dve.wait_ge(gate_act.sem, gate_act.done(t, 2))
                dve.wait_ge(gate_steps.sem, gate_steps.done(t, 3))
                dve.tensor_tensor(soft[:, 1, :], soft[:, 0, :], soft[:, 3, :], ALU.add).then_inc(gate_steps.sem, gate_steps.unit)
                dve.wait_ge(gate_steps.sem, gate_steps.done(t, 4))
                dve.scalar_tensor_tensor(la[:], soft[:, 1, :], -1.0, neg_a[:], ALU.mult, ALU.mult).then_inc(gate_steps.sem, gate_steps.unit)
                dve.wait_ge(read_out.sem, read_out.done(t, 3))
                dve.tensor_reduce(ss[:], sq[:], AX, ALU.add).then_inc(norm_steps.sem, norm_steps.unit)
                dve.wait_ge(norm_steps.sem, norm_steps.done(t, 1))
                dve.tensor_scalar(ss[:], ss[:], 1e-6, None, ALU.add).then_inc(norm_steps.sem, norm_steps.unit)
                dve.wait_ge(rooted.sem, rooted.done(t))
                dve.reciprocal(rnorm[:], root[:]).then_inc(norm_steps.sem, norm_steps.unit)
                dve.wait_ge(norm_steps.sem, norm_steps.done(t, 3))
                dve.tensor_scalar(rnorm[:, 0:4], rnorm[:, 0:4], float(P) ** -0.5, None, ALU.mult).then_inc(norm_steps.sem, norm_steps.unit)
                dve.wait_ge(norm_steps.sem, norm_steps.done(t, 4))
                for x in range(2):
                    dve.tensor_tensor(qk[:, x], bank[:, x], per_head(rnorm[:, 4 * x:4 * x + 4]), ALU.mult).then_inc(k_ready.sem, k_ready.unit)
                dve.wait_ge(summed_g.sem, summed_g.done(t))
                dve.tensor_copy(g[:], bank[:, 3, 1, 0:16]).then_inc(g_copied.sem, g_copied.unit)
                dve.wait_ge(g_copied.sem, g_copied.done(t, 1))
                dve.tensor_tensor(diff[:], bank[:, 4:6].rearrange("p b c n -> p (b c) n"), per_head(g[:, 0:8]), ALU.subtract).then_inc(decay_steps.sem, decay_steps.unit)
                dve.wait_ge(decay_steps.sem, decay_steps.done(t, 1))
                dve.tensor_scalar(dpos[:], diff[:], 0.0, None, ALU.max).then_inc(decay_steps.sem, decay_steps.unit)
                dve.tensor_scalar(diff[:], diff[:], 0.0, None, ALU.min).then_inc(decay_steps.sem, decay_steps.unit)
                dve.tensor_tensor(tail[:], g[:, 8:16], g[:, 0:8], ALU.subtract).then_inc(g_copied.sem, g_copied.unit)
                dve.wait_ge(gate_act.sem, gate_act.done(t))
                dve.tensor_scalar(neg_beta[:], beta[:], -1.0, None, ALU.mult).then_inc(g_copied.sem, g_copied.unit)
                dve.wait_ge(g_copied.sem, g_copied.done(t))
                dve.wait_ge(crossed.sem, crossed.done(t))
                dve.wait_ge(masked.sem, masked.done(t))
                for d, s in enumerate((sf, sr)):
                    dve.tensor_tensor(s.a[:], bank[:, 0], decay[:, 4 * d:4 * d + 4], ALU.mult).then_inc(a_ready.sem, a_ready.unit)
                    dve.tensor_tensor(qkm[:, 4 * d:4 * d + 4], bank[:, 1], decayT[:, 4 * d:4 * d + 4], ALU.mult).then_inc(a_ready.sem, a_ready.unit)
                dve.wait_ge(at_copied.sem, at_copied.done(t))
                dve.wait_ge(a_ready.sem, a_ready.done(t))
                sf.start(dve, t, env.ident, env.lower_level, env.upper_level)
                sr.start(dve, t, env.ident, env.upper_level, env.lower_level)
                solve_sums(dve, (sf, sr), t, (env.lower_level, env.upper_level))
                dve.wait_ge(out_summed.sem, out_summed.done(t, 1))
                dve.tensor_copy(env.dn_o[:, ds(t, 1), :].rearrange("p a (c n) -> p (a c) n", n=P), bank[:, 6]).then_inc(o_kept.sem, o_kept.unit)
                dve.wait_ge(out_summed.sem, out_summed.done(t, 3))
                dve.wait_ge(rec_stored.sem, rec_stored.done(t, 0))
                dve.wait_ge(scaled.sem, scaled.done(t))
                for d in range(2):
                    dve.tensor_tensor(rec[:, d, 1], bank[:, d], diag[:, 4 * d:4 * d + 4], ALU.add).then_inc(out_ready.sem, out_ready.unit)

        @block.gpsimd
        def _(pool):
            with pool.Fori(0, NT) as t:
                pool.wait_ge(g_copied.sem, g_copied.done(t))
                pool.wait_ge(decayed.sem, decayed.done(t))
                pool.tensor_tensor(dirs(decayT)[:, 0], dirs(decayT)[:, 0], env.upper_incl[:].unsqueeze(1).to_broadcast([P, 4, P]), ALU.mult).then_inc(masked.sem, masked.unit)
                pool.tensor_tensor(dirs(decayT)[:, 1], dirs(decayT)[:, 1], env.lower_incl[:].unsqueeze(1).to_broadcast([P, 4, P]), ALU.mult).then_inc(masked.sem, masked.unit)
                pool.tensor_tensor(decay[:], decay[:], per_head(neg_beta[:]), ALU.mult).then_inc(masked.sem, masked.unit)
                pool.wait_ge(masked.sem, masked.done(t, 3))
                pool.tensor_tensor(dirs(decay)[:, 0], dirs(decay)[:, 0], env.lower[:].unsqueeze(1).to_broadcast([P, 4, P]), ALU.mult).then_inc(masked.sem, masked.unit)
                pool.tensor_tensor(dirs(decay)[:, 1], dirs(decay)[:, 1], env.upper[:].unsqueeze(1).to_broadcast([P, 4, P]), ALU.mult).then_inc(masked.sem, masked.unit)
                pool.wait_ge(small_exp.sem, small_exp.done(t))
                pool.tensor_tensor(neg_beg[:], neg_beta[:], eg[:], ALU.mult).then_inc(scaled.sem, scaled.unit)
                pool.wait_ge(scaled.sem, scaled.done(t, 1))
                for d in range(2):
                    cs = slice(4 * d, 4 * d + 4)
                    for out, in_, factor in ((rhs[:, cs, 0], v[:], beta), (rhs[:, cs, 1], qk[:, 1], neg_beg),
                                             (qe[:, cs], qk[:, 0], eg), (kt[:, cs], qk[:, 1], etail),
                                             (diag[:, cs], env.ident[:].unsqueeze(1).to_broadcast([P, 4, P]), etot)):
                        pool.tensor_tensor(out, in_, per_head(factor[:, cs]), ALU.mult).then_inc(scaled.sem, scaled.unit)


RCH = RWW // P


def rwkv(env):
    nc, io = env.nc, env.io
    E = env.event
    weights_in = E("rw_weights_loaded", per=3, dma=True)
    consts_ready = E("rw_consts_ready", per=5)
    masks_ready = E("rw_masks_ready", per=2)
    cols_in = E("rw_cols_loaded", per=4, dma=True)
    low_ready = E("rw_low_ready", per=2)
    low_summed = E("rw_low_summed", per=2)
    biased = E("rw_biased", per=2)
    sigmoided = E("rw_sigmoided", per=2)
    scan_steps = E("rw_scan_steps", per=3)
    decayed = E("rw_decayed", per=2)
    kk_steps = E("rw_kk_steps", per=3)
    kk_summed = E("rw_kk_summed")
    kk_norm = E("rw_kk_norm", per=3)
    mid_kept = E("rw_mid_kept")
    rooted = E("rw_rooted")
    kp_steps = E("rw_kp_steps", per=3)
    bonus_steps = E("rw_bonus_steps", per=2)
    bonus_summed = E("rw_bonus_summed")
    bonus_ready = E("rw_bonus_ready", per=2)
    v_turned = E("rw_v_turned")
    v_ready = E("rw_v_ready", per=2)
    side_stored = E("rw_side_stored", dma=True)
    prod_pool = E("rw_prod_pool", per=4)
    prod_dve = E("rw_prod_dve", per=4)
    tok_turned = E("rw_tok_turned", per=2)
    tok_copied = E("rw_tok_copied", per=6)
    crossed = E("rw_crossed", per=16)
    cross_kept = E("rw_cross_kept", per=16)
    a_kept = E("rw_a_kept", per=4)
    m2v_summed = E("rw_m2v_summed", per=2)
    m2v_copied = E("rw_m2v_copied", per=2)
    w_summed = E("rw_w_summed", per=2)
    w_copied = E("rw_w_copied", per=2)
    out_summed = E("rw_out_summed", per=4)
    o_kept = E("rw_o_kept", per=2)
    out_dve = E("rw_out_dve", per=4)
    out_act = E("rw_out_act", per=2)
    scal_ready = E("rw_scal_ready", per=4)
    rec_stored = E("rw_rec_stored", per=2, dma=True)

    with ExitStack() as ctx:
        sb, pb = tools(nc, ctx)
        bank = pb("rw_banks", [P, 8, 4, P])
        w2 = sb("rw_w2s", [P, RWW])
        a2 = sb("rw_a2s", [64, RWW])
        g2 = sb("rw_g2s", [P, RWW])
        head_ident = sb("rw_head_ident", [P, 64])
        seg = sb("rw_seg", [P, 8, P + 1])
        lw = sb("rw_lw", [P, 8, P + 1])
        cross_mask = sb("rw_cross_mask", [P, 2, 4, P])
        rkvT = sb("rw_rkvT", [P, 3 * RCH, P])
        wdT = sb("rw_wdT", [P, P])
        adT = sb("rw_adT", [64, P])
        gdT = sb("rw_gdT", [P, P])
        pre = sb("rw_pre", [P, 12, P])
        cum = sb("rw_cum", [P, 8, P + 1])
        ep = sb("rw_ep", [P, 8, P + 1])
        en = sb("rw_en", [P, 8, P + 1])
        kk = sb("rw_kk", [P, RCH, P])
        sq = sb("rw_sq", [P, RCH, P])
        inv = sb("rw_inv", [P, RCH, P])
        kp = sb("rw_kp", [P, RCH, P])
        nb = sb("rw_nb", [P, RCH, P])
        bon = sb("rw_bon", [P, RCH, P])
        bonus = sb("rw_bonus", [P, 8])
        mid = sb("rw_mid", [P, 8])
        v = sb("rw_v", [P, RWH, 64])
        side = sb("rw_side", [P, 2, RWW])
        kr = sb("rw_kr", [P, 2, RCH, 2, P])
        bt = sb("rw_bt", [P, 2, RCH, P])
        kt = sb("rw_kt", [P, 2, RCH, P])
        tok_b = sb("rw_tok_b", [P, RWH, 64])
        tok_k = sb("rw_tok_k", [P, RWH, 64])
        rhs = sb("rw_rhs", [P, RWH, 2, 64])
        w = sb("rw_w", [P, RWH, 2, 64])
        cross = sb("rw_cross", [P, RWH, 4, P])
        rec = sb("rw_rec", [P, 2, 1032])
        solvers = (Solver(env, "rw_s0", sb, bank[:, 6], bank[:, 0:2]),
                   Solver(env, "rw_s1", sb, bank[:, 7], bank[:, 2:4]))
        for n, s in enumerate(solvers):
            s.at = cross[:, n:RWH:2, 0, :]
        block = ctx.enter_context(nc.Block())
        r, k = rkvT[:, 0:RCH], rkvT[:, RCH:2 * RCH]
        levels = (env.lower_level, env.upper_level)

        def per_channel(at, n=RCH):
            return spread(env.vec[:, at:at + n], P)

        @block.sync
        def _(sp):
            sp.dma_start(w2[:], io["rw_w2"].rearrange("o d r c -> (o d r) c")).then_inc(weights_in.sem, weights_in.unit)
            sp.dma_start(a2[:], io["rw_a2"][0]).then_inc(weights_in.sem, weights_in.unit)
            sp.dma_start(g2[:], io["rw_g2"][0]).then_inc(weights_in.sem, weights_in.unit)

            def load(t):
                cols = ds(t * P, P)
                low = RW0 + 3 * RWW
                sp.dma_start(rkvT[:], io["ch"][RW0:low, cols].rearrange("(c p) t -> p c t", p=P)).then_inc(cols_in.sem, cols_in.unit)
                sp.dma_start(wdT[:], io["ch"][low:low + 128, cols]).then_inc(cols_in.sem, cols_in.unit)
                sp.dma_start(adT[:], io["ch"][low + 128:low + 192, cols]).then_inc(cols_in.sem, cols_in.unit)
                sp.dma_start(gdT[:], io["ch"][low + 192:G0, cols]).then_inc(cols_in.sem, cols_in.unit)

            def store(t):
                sp.wait_ge(bonus_ready.sem, bonus_ready.done(t))
                sp.wait_ge(v_ready.sem, v_ready.done(t))
                sp.dma_start(io["rw_side"][ds(t, 1)].rearrange("a p x -> p (a x)"), side[:].rearrange("p x n -> p (x n)")).then_inc(side_stored.sem, side_stored.unit)
                sp.wait_ge(out_dve.sem, out_dve.done(t))
                sp.wait_ge(out_act.sem, out_act.done(t))
                sp.wait_ge(scal_ready.sem, scal_ready.done(t))
                for d in range(2):
                    sp.dma_start(io["rw_rec"][ds(t * 2 + d, 1)].rearrange("a p x -> p (a x)"), rec[:, d]).then_inc(rec_stored.sem, rec_stored.unit)

            load(0)
            with sp.Fori(1, NT) as t:
                sp.wait_ge(low_summed.sem, low_summed.done(t - 1))
                sp.wait_ge(v_turned.sem, v_turned.done(t - 1))
                sp.wait_ge(prod_pool.sem, prod_pool.done(t - 1))
                sp.wait_ge(prod_dve.sem, prod_dve.done(t - 1))
                sp.wait_ge(bonus_steps.sem, bonus_steps.done(t - 1))
                load(t)
                store(t - 1)
            store(NT - 1)
            sp.wait_ge(rec_stored.sem, rec_stored.done(NT - 1))
            sp.wait_ge(side_stored.sem, side_stored.done(NT - 1))

        @block.tensor
        def _(pe):
            pe.wait_ge(weights_in.sem, weights_in.done())
            with pe.Fori(0, NT) as t:
                pe.wait_ge(cols_in.sem, cols_in.done(t))
                pe.wait_ge(low_ready.sem, low_ready.done(t))
                for d in range(2):
                    rows = slice(64 * d, 64 * d + 64)
                    for c in range(RCH):
                        pe.matmul(bank[:, d, c, :], w2[rows, c * P:(c + 1) * P], wdT[rows, :], start=True, stop=True)
                for c in range(RCH):
                    mm = pe.matmul(bank[:, 2, c, :], a2[:, c * P:(c + 1) * P], adT[:], start=True, stop=True)
                mm.then_inc(low_summed.sem, low_summed.unit)
                pe.matmul(bank[:, 3].rearrange("p c n -> p (c n)"), gdT[:], g2[:], start=True, stop=True).then_inc(low_summed.sem, low_summed.unit)
                for c in range(RCH):
                    tr = pe.transpose(bank[:, 5, c, :], rkvT[:, 2 * RCH + c, :], env.ident[:])
                tr.then_inc(v_turned.sem, v_turned.unit)
                pe.wait_ge(kk_steps.sem, kk_steps.done(t, 2))
                pe.matmul(bank[:, 4].rearrange("p c n -> p (c n)"), env.headones[:], sq[:].rearrange("p c n -> p (c n)"),
                                       start=True, stop=True).then_inc(kk_summed.sem, kk_summed.unit)
                pe.wait_ge(bonus_steps.sem, bonus_steps.done(t))
                for c in range(RCH):
                    mm = pe.matmul(bank[:, 7, 0, 2 * c:2 * c + 2], bon[:, c, :], env.headones[:, 0:P:64], start=True, stop=True)
                mm.then_inc(bonus_summed.sem, bonus_summed.unit)
                pe.wait_ge(prod_pool.sem, prod_pool.done(t))
                pe.wait_ge(prod_dve.sem, prod_dve.done(t))
                pe.wait_ge(bonus_ready.sem, bonus_ready.done(t, 1))
                pe.wait_ge(v_ready.sem, v_ready.done(t))
                pe.wait_ge(kk_norm.sem, kk_norm.done(t))
                for d in range(2):
                    for c in range(RCH):
                        pe.transpose(bank[:, 4, c, :], kr[:, d, c, 0, :], env.ident[:])
                        pe.transpose(bank[:, 5, c, :], bt[:, d, c, :], env.ident[:])
                        tr = pe.transpose(bank[:, 6, c, :], kt[:, d, c, :], env.ident[:])
                    tr.then_inc(tok_turned.sem, tok_turned.unit)
                    for h in range(RWH):
                        rows, c = slice(64 * (h % 2), 64 * (h % 2) + 64), h // 2
                        both = kr[rows, d, c].rearrange("p x n -> p (x n)")
                        if h >= 4:
                            pe.wait_ge(cross_kept.sem, cross_kept.done(t, 8 * d + h - 3))
                        if h == 1:
                            pe.wait_ge(tok_copied.sem, tok_copied.done(t, 3 * d + 1))
                        pe.matmul(bank[:, h % 4, 0:2, :], bt[rows, d, c, :], both, start=True, stop=True)
                        pe.matmul(bank[:, h % 4, 2:4, :], kt[rows, d, c, :], both, start=True, stop=True)
                        mm = pe.matmul(bank[:, (7, 4)[h % 2], c, :], kr[rows, d, c, 0, :], bt[rows, d, c, :],
                                       start=True, stop=True)
                        mm.then_inc(crossed.sem, crossed.unit)
                    pe.wait_ge(tok_copied.sem, tok_copied.done(t, 3 * d + 3))
                    pe.wait_ge(a_kept.sem, a_kept.done(t, 2 * d + 2))
                    solve_products(pe, solvers, t * 2 + d)
                    for h in range(RWH):
                        mm = pe.matmul(bank[:, 4].rearrange("p c (x n) -> p (c x) n", n=64)[:, h, :], cross[:, h, 2, :], v[:, h, :],
                                       start=True, stop=True)
                    mm.then_inc(m2v_summed.sem, m2v_summed.unit)
                    for s in solvers:
                        s.solved(pe, t * 2 + d)
                    pe.wait_ge(m2v_copied.sem, m2v_copied.done(t, d + 1))
                    for h in range(RWH):
                        mm = pe.matmul(bank[:, h // 4, h % 4, :], solvers[h % 2].xt[:, h // 2, :], rhs[:, h].rearrange("p x n -> p (x n)"),
                                       start=True, stop=True)
                    mm.then_inc(w_summed.sem, w_summed.unit)
                    pe.wait_ge(w_copied.sem, w_copied.done(t, d + 1))
                    for h in range(RWH):
                        o = bank[:, 5].rearrange("p c (x n) -> p (c x) n", n=64)[:, h, :]
                        pe.matmul(o, cross[:, h, 3, :], v[:, h, :], start=True, stop=False)
                        mm = pe.matmul(o, cross[:, h, 1, :], w[:, h, 1, :], start=False, stop=True)
                    mm.then_inc(out_summed.sem, out_summed.unit)
                    for h in range(RWH):
                        rows, c = slice(64 * (h % 2), 64 * (h % 2) + 64), h // 2
                        pe.matmul(bank[rows, 2, c, :], w[:, h, 0, :], cross[:, h, 1, :], start=True, stop=True)
                        small = bank[rows, 3].rearrange("p (x c2) (y n) -> p x (c2 y) n", x=2, n=64)
                        pe.matmul(small[:, 0, c, :], w[:, h, 0, :], tok_b[:, h, :], start=True, stop=True)
                        pe.matmul(small[:, 1, c, :], tok_k[:, h, :], v[:, h, :], start=True, stop=False)
                        mm = pe.matmul(small[:, 1, c, :], tok_b[:, h, :], w[:, h, 1, :], start=False, stop=True)
                    mm.then_inc(out_summed.sem, out_summed.unit)
                    pe.wait_ge(o_kept.sem, o_kept.done(t, d + 1))
                    pe.wait_ge(out_dve.sem, out_dve.done(t, 2 * d + 2))
                    pe.wait_ge(out_act.sem, out_act.done(t, d + 1))

        @block.scalar
        def _(act):
            with act.Fori(0, NT) as t:
                act.wait_ge(cols_in.sem, cols_in.done(t))
                act.activation(wdT[:], wdT[:], ACT.Tanh).then_inc(low_ready.sem, low_ready.unit)
                act.activation(gdT[:], gdT[:], ACT.Sigmoid).then_inc(low_ready.sem, low_ready.unit)
                for x in range(2):
                    cs = (slice(0, 8), slice(8, 12))[x]
                    act.wait_ge(biased.sem, biased.done(t, x + 1))
                    act.activation(pre[:, cs], pre[:, cs], ACT.Sigmoid).then_inc(sigmoided.sem, sigmoided.unit)
                act.wait_ge(v_turned.sem, v_turned.done(t))
                act.wait_ge(side_stored.sem, side_stored.done(t, 0))
                act.activation(v[:].rearrange("p (c x) n -> p c (x n)", x=2), bank[:, 5], ACT.Identity).then_inc(v_ready.sem, v_ready.unit)
                act.activation(side[:, 1], bank[:, 3].rearrange("p c n -> p (c n)"), ACT.Identity).then_inc(v_ready.sem, v_ready.unit)
                act.wait_ge(kk_norm.sem, kk_norm.done(t, 1))
                act.activation(inv[:], sq[:], ACT.Sqrt).then_inc(rooted.sem, rooted.unit)
                act.wait_ge(scan_steps.sem, scan_steps.done(t))
                act.activation(ep[:], cum[:], ACT.Exp).then_inc(decayed.sem, decayed.unit)
                act.activation(en[:], cum[:], ACT.Exp, scale=-1.0).then_inc(decayed.sem, decayed.unit)
                for d in range(2):
                    act.wait_ge(tok_turned.sem, tok_turned.done(t, d + 1))
                    dst = rhs[:, :, 0, :].rearrange("p (c x) n -> p c x n", x=2)
                    act.activation(dst, bank[:, 4].rearrange("p c (x n) -> p c x n", x=2), ACT.Identity).then_inc(tok_copied.sem, tok_copied.unit)
                    act.activation(tok_b[:].rearrange("p (c x) n -> p c (x n)", x=2), bank[:, 5], ACT.Identity).then_inc(tok_copied.sem, tok_copied.unit)
                    act.activation(tok_k[:].rearrange("p (c x) n -> p c (x n)", x=2), bank[:, 6], ACT.Identity).then_inc(tok_copied.sem, tok_copied.unit)
                    act.wait_ge(m2v_summed.sem, m2v_summed.done(t, d + 1))
                    act.activation(rhs[:, :, 1, :], bank[:, 4].rearrange("p c (x n) -> p (c x) n", x=2), ACT.Identity).then_inc(m2v_copied.sem, m2v_copied.unit)
                    act.wait_ge(w_summed.sem, w_summed.done(t, d + 1))
                    act.activation(w[:].rearrange("p h x n -> p (h x n)"), bank[:, 0:2].rearrange("p b c n -> p (b c n)"),
                                               ACT.Identity).then_inc(w_copied.sem, w_copied.unit)
                    act.wait_ge(out_summed.sem, out_summed.done(t, 2 * d + 2))
                    if d == 0:
                        act.wait_ge(rec_stored.sem, rec_stored.done(t, 0))
                    act.activation(rec[:, d, 768:1024], bank[:, 3, 2:4].rearrange("p c n -> p (c n)"), ACT.Identity).then_inc(out_act.sem, out_act.unit)
                for d, (before, at0, behind, at1) in enumerate(((en, 0, ep, P), (ep, P, en, 0))):
                    act.activation(rec[:, d, 1024:1028], before[:, 4 * d:4 * d + 4, at0], ACT.Identity).then_inc(scal_ready.sem, scal_ready.unit)
                    act.activation(rec[:, d, 1028:1032], behind[:, 4 * d:4 * d + 4, at1], ACT.Identity).then_inc(scal_ready.sem, scal_ready.unit)

        @block.vector
        def _(dve):
            dve.wait_ge(masks_ready.sem, masks_ready.done())
            dve.tensor_tensor(head_ident[:], env.ident[:, 0:64], env.ident[:, 64:128], ALU.add).then_inc(consts_ready.sem, consts_ready.unit)
            for d, (strict, incl) in enumerate(((env.upper, env.upper_incl), (env.lower, env.lower_incl))):
                for x, m in enumerate((strict, incl)):
                    dve.tensor_copy(cross_mask[:, d, x:4:2, :], m[:].unsqueeze(1).to_broadcast([P, 2, P])).then_inc(consts_ready.sem, consts_ready.unit)
            dve.wait_ge(consts_ready.sem, consts_ready.done())
            with dve.Fori(0, NT) as t:
                dve.wait_ge(cols_in.sem, cols_in.done(t))
                dve.tensor_tensor(kk[:], k, per_channel(V_KK), ALU.mult).then_inc(kk_steps.sem, kk_steps.unit)
                dve.wait_ge(kk_steps.sem, kk_steps.done(t, 1))
                dve.tensor_tensor(sq[:], kk[:], kk[:], ALU.mult).then_inc(kk_steps.sem, kk_steps.unit)
                dve.wait_ge(low_summed.sem, low_summed.done(t, 1))
                dve.tensor_tensor(pre[:, 0:8], bank[:, 0:2].rearrange("p b c n -> p (b c) n"), per_channel(V_W0, 8), ALU.add).then_inc(biased.sem, biased.unit)
                dve.tensor_tensor(pre[:, 8:12], bank[:, 2], per_channel(V_A0), ALU.add).then_inc(biased.sem, biased.unit)
                dve.wait_ge(kk_summed.sem, kk_summed.done(t))
                dve.tensor_scalar(sq[:], bank[:, 4], 1e-12, None, ALU.add).then_inc(kk_norm.sem, kk_norm.unit)
                dve.wait_ge(sigmoided.sem, sigmoided.done(t, 1))
                dve.tensor_scalar(lw[:, :, 1:P + 1], pre[:, 0:8], HALF_DECAY, None, ALU.mult).then_inc(scan_steps.sem, scan_steps.unit)
                dve.wait_ge(scan_steps.sem, scan_steps.done(t, 1))
                dve.tensor_tensor_scan(cum[:].rearrange("p c n -> p (c n)"), seg[:].rearrange("p c n -> p (c n)"),
                                                     lw[:].rearrange("p c n -> p (c n)"), 0.0, ALU.mult, ALU.add).then_inc(scan_steps.sem, scan_steps.unit)
                dve.wait_ge(scan_steps.sem, scan_steps.done(t, 2))
                dve.tensor_copy(mid[:], cum[:, :, 64]).then_inc(mid_kept.sem, mid_kept.unit)
                dve.wait_ge(mid_kept.sem, mid_kept.done(t))
                dve.tensor_tensor(cum[:], cum[:], spread(mid[:], P + 1), ALU.subtract).then_inc(scan_steps.sem, scan_steps.unit)
                dve.wait_ge(rooted.sem, rooted.done(t))
                dve.reciprocal(inv[:], inv[:]).then_inc(kk_norm.sem, kk_norm.unit)
                dve.wait_ge(kk_norm.sem, kk_norm.done(t, 2))
                dve.tensor_tensor(kk[:], kk[:], inv[:], ALU.mult).then_inc(kk_norm.sem, kk_norm.unit)
                dve.wait_ge(kk_norm.sem, kk_norm.done(t, 3))
                dve.wait_ge(sigmoided.sem, sigmoided.done(t, 2))
                dve.scalar_tensor_tensor(nb[:], kk[:], -1.0, pre[:, 8:12], ALU.mult, ALU.mult).then_inc(kk_steps.sem, kk_steps.unit)
                dve.wait_ge(kk_steps.sem, kk_steps.done(t, 3))
                dve.wait_ge(decayed.sem, decayed.done(t))
                dve.tensor_tensor(kr[:, 0, :, 0, :], kk[:], ep[:, 0:4, 0:P], ALU.mult).then_inc(prod_dve.sem, prod_dve.unit)
                dve.tensor_tensor(kr[:, 1, :, 0, :], kk[:], en[:, 4:8, 1:P + 1], ALU.mult).then_inc(prod_dve.sem, prod_dve.unit)
                dve.tensor_tensor(bt[:, 0], nb[:], en[:, 0:4, 1:P + 1], ALU.mult).then_inc(prod_dve.sem, prod_dve.unit)
                dve.tensor_tensor(bt[:, 1], nb[:], ep[:, 4:8, 0:P], ALU.mult).then_inc(prod_dve.sem, prod_dve.unit)
                dve.wait_ge(bonus_summed.sem, bonus_summed.done(t))
                dve.tensor_copy(bonus[:], bank[:, 7, 0, 0:8]).then_inc(bonus_ready.sem, bonus_ready.unit)
                dve.wait_ge(bonus_ready.sem, bonus_ready.done(t, 1))
                dve.wait_ge(v_ready.sem, v_ready.done(t))
                dve.wait_ge(side_stored.sem, side_stored.done(t, 0))
                dve.tensor_tensor(side[:, 0].rearrange("p (h n) -> p h n", n=64), v[:], spread(bonus[:], 64), ALU.mult).then_inc(bonus_ready.sem, bonus_ready.unit)
                for d in range(2):
                    strict_a = (env.lower, env.upper)[d]
                    for h in range(RWH):
                        dve.wait_ge(crossed.sem, crossed.done(t, 8 * d + h + 1))
                        dve.tensor_tensor(cross[:, h], bank[:, h % 4], cross_mask[:, d], ALU.mult).then_inc(cross_kept.sem, cross_kept.unit)
                    for n in range(2):
                        dve.tensor_tensor(solvers[n].a[:], bank[:, (7, 4)[n]], strict_a[:].unsqueeze(1).to_broadcast([P, 4, P]),
                                                    ALU.mult).then_inc(a_kept.sem, a_kept.unit)
                    dve.wait_ge(cross_kept.sem, cross_kept.done(t, 8 * d + 8))
                    dve.wait_ge(a_kept.sem, a_kept.done(t, 2 * d + 2))
                    for s in solvers:
                        s.start(dve, t * 2 + d, env.ident, levels[d], levels[1 - d])
                    solve_sums(dve, solvers, t * 2 + d, (levels[d], levels[d]))
                    dve.wait_ge(out_summed.sem, out_summed.done(t, 2 * d + 1))
                    kept = env.rw_o[:, ds(t, 1), :].rearrange("p a n -> p (a n)")
                    o0 = bank[:, 5].rearrange("p c n -> p (c n)")
                    if d == 0:
                        dve.tensor_copy(kept, o0).then_inc(o_kept.sem, o_kept.unit)
                    else:
                        dve.wait_ge(o_kept.sem, o_kept.done(t, 1))
                        dve.tensor_tensor(kept, kept, o0, ALU.add).then_inc(o_kept.sem, o_kept.unit)
                    dve.wait_ge(out_summed.sem, out_summed.done(t, 2 * d + 2))
                    if d == 0:
                        dve.wait_ge(rec_stored.sem, rec_stored.done(t, 0))
                    dve.tensor_tensor(rec[:, d, 0:512].rearrange("p (c n) -> p c n", n=P), bank[:, 2], kr[:, d, :, 1, :], ALU.add).then_inc(out_dve.sem, out_dve.unit)
                    dve.wait_ge(out_act.sem, out_act.done(t, d + 1))
                    dve.tensor_tensor(rec[:, d, 512:768].rearrange("p (c n) -> p c n", n=64),
                                                 bank[:, 3, 0:2].rearrange("p c (x n) -> p (c x) n", n=64),
                                                 head_ident[:].unsqueeze(1).to_broadcast([P, RCH, 64]), ALU.add).then_inc(out_dve.sem, out_dve.unit)

        @block.gpsimd
        def _(pool):
            pool.memset(seg[:], 1.0).then_inc(masks_ready.sem, masks_ready.unit)
            pool.wait_ge(masks_ready.sem, masks_ready.done(0, 1))
            pool.memset(seg[:, :, 0:1], 0.0)
            pool.memset(lw[:], 0.0).then_inc(masks_ready.sem, masks_ready.unit)
            with pool.Fori(0, NT) as t:
                pool.wait_ge(cols_in.sem, cols_in.done(t))
                pool.wait_ge(sigmoided.sem, sigmoided.done(t, 2))
                pool.tensor_tensor(kp[:], pre[:, 8:12], per_channel(V_KA), ALU.mult).then_inc(kp_steps.sem, kp_steps.unit)
                pool.wait_ge(kp_steps.sem, kp_steps.done(t, 1))
                pool.tensor_tensor(kp[:], kp[:], spread(env.ka_rest[:], P), ALU.add).then_inc(kp_steps.sem, kp_steps.unit)
                pool.wait_ge(kp_steps.sem, kp_steps.done(t, 2))
                pool.tensor_tensor(kp[:], kp[:], k, ALU.mult).then_inc(kp_steps.sem, kp_steps.unit)
                pool.wait_ge(kp_steps.sem, kp_steps.done(t, 3))
                pool.tensor_tensor(bon[:], kp[:], r, ALU.mult).then_inc(bonus_steps.sem, bonus_steps.unit)
                pool.wait_ge(bonus_steps.sem, bonus_steps.done(t, 1))
                pool.tensor_tensor(bon[:], bon[:], per_channel(V_RK), ALU.mult).then_inc(bonus_steps.sem, bonus_steps.unit)
                pool.wait_ge(decayed.sem, decayed.done(t))
                pool.tensor_tensor(kr[:, 0, :, 1, :], r, ep[:, 0:4, 1:P + 1], ALU.mult).then_inc(prod_pool.sem, prod_pool.unit)
                pool.tensor_tensor(kr[:, 1, :, 1, :], r, en[:, 4:8, 0:P], ALU.mult).then_inc(prod_pool.sem, prod_pool.unit)
                pool.tensor_tensor(kt[:, 0], kp[:], en[:, 0:4, 1:P + 1], ALU.mult).then_inc(prod_pool.sem, prod_pool.unit)
                pool.tensor_tensor(kt[:, 1], kp[:], ep[:, 4:8, 0:P], ALU.mult).then_inc(prod_pool.sem, prod_pool.unit)


def recur(env):
    nc, io = env.nc, env.io
    E = env.event
    loaded = [E(f"rc_loaded{s}", per=4, dma=True) for s in range(2)]
    cleared = E("rc_cleared", per=2)
    scaled = E("rc_scaled", per=2)
    dn_summed = E("rc_dn_summed", per=2)
    rw_summed = E("rc_rw_summed", per=2)
    dn_o_added = E("rc_dn_o_added", per=2)
    dn_state = E("rc_dn_state", per=2)
    rw_o_added = E("rc_rw_o_added", per=2)
    rw_mid = E("rc_rw_mid", per=4)
    rw_state = E("rc_rw_state", per=2)
    DNR, RWR = 3 * DNW, 1032
    with ExitStack() as ctx:
        sb, pb = tools(nc, ctx)
        bank = pb("rc_banks", [P, 8, 512])
        dn_rec = sb("rc_dn_rec", [P, 2, 2, 3, DNH, P])
        rw_rec = sb("rc_rw_rec", [P, 2, 2, RWR])
        dn_s = sb("rc_dn_s", [P, 2, DNH, P])
        rw_s = sb("rc_rw_s", [P, 2, RCH, 64])
        block = ctx.enter_context(nc.Block())

        def steps(eng, body, before=None):
            done = 0
            for g, (t0, n) in enumerate(SEQS):
                if before:
                    before(g, done)
                with eng.Fori(0, n // 2) as i:
                    for s in range(2):
                        step = i * 2 + s
                        body(s, g, (t0 + step, t0 + n - 1 - step), done + step, done // 2 + i)
                done += n

        @block.sync
        def _(sp):
            def load(s, tiles, slot_turn):
                for d in range(2):
                    r = tiles[d] * 2 + d
                    sp.dma_start(dn_rec[:, s, d].rearrange("p x c n -> p (x c n)"),
                                              io["dn_rec"][ds(r, 1)].rearrange("a p x -> p (a x)")).then_inc(loaded[s].sem, loaded[s].unit)
                    sp.dma_start(rw_rec[:, s, d], io["rw_rec"][ds(r, 1)].rearrange("a p x -> p (a x)")).then_inc(loaded[s].sem, loaded[s].unit)
            done = 0
            for g, (t0, n) in enumerate(SEQS):
                if g == 0:
                    for s in range(2):
                        load(s, (t0 + s, t0 + n - 1 - s), 0)
                with sp.Fori(1 if g == 0 else 0, n // 2) as i:
                    for s in range(2):
                        sp.wait_ge(dn_state.sem, dn_state.done(done - 2 + i * 2 + s))
                        sp.wait_ge(rw_state.sem, rw_state.done(done - 2 + i * 2 + s))
                        load(s, (t0 + i * 2 + s, t0 + n - 1 - s - i * 2), 0)
                done += n

        @block.tensor
        def _(pe):
            def body(s, g, tiles, turn, slot_turn):
                pe.wait_ge(loaded[s].sem, loaded[s].done(slot_turn))
                for d in range(2):
                    rec = dn_rec[:, s, d]
                    for h in range(DNH):
                        pe.matmul(bank[:, 2 * d, h * P:(h + 1) * P], rec[:, 0, h, :], dn_s[:, d, h, :], start=True, stop=True)
                        mm = pe.matmul(bank[:, 2 * d + 1, h * P:(h + 1) * P], rec[:, 1, h, :], dn_s[:, d, h, :], start=True, stop=True)
                    mm.then_inc(dn_summed.sem, dn_summed.unit)
                pe.wait_ge(scaled.sem, scaled.done(turn))
                for d in range(2):
                    for h in range(RWH):
                        rows, c = slice(64 * (h % 2), 64 * (h % 2) + 64), h // 2
                        b = 4 + 2 * d + h % 2
                        state = rw_s[rows, d, c, :]
                        pe.matmul(bank[:, b, c * 64:c * 64 + 64], rw_rec[rows, s, d, c * P:(c + 1) * P], state, start=True, stop=True)
                        mm = pe.matmul(bank[rows, b, 256 + c * 64:320 + c * 64], rw_rec[rows, s, d, 512 + c * 64:576 + c * 64], state,
                                       start=True, stop=True)
                    mm.then_inc(rw_summed.sem, rw_summed.unit)
                pe.wait_ge(dn_o_added.sem, dn_o_added.done(turn))
                pe.wait_ge(dn_state.sem, dn_state.done(turn))
                pe.wait_ge(rw_o_added.sem, rw_o_added.done(turn))
                pe.wait_ge(rw_state.sem, rw_state.done(turn))

            steps(pe, body, lambda g, done: pe.wait_ge(cleared.sem, cleared.done(g)))

        @block.vector
        def _(dve):
            def clear(g, done):
                dve.memset(dn_s[:], 0.0).then_inc(cleared.sem, cleared.unit)
                dve.memset(rw_s[:], 0.0).then_inc(cleared.sem, cleared.unit)
                dve.wait_ge(cleared.sem, cleared.done(g))

            def body(s, g, tiles, turn, slot_turn):
                dve.wait_ge(loaded[s].sem, loaded[s].done(slot_turn))
                for d in range(2):
                    before = rw_rec[:, s, d, 1024:1028]
                    dve.tensor_tensor(rw_s[:, d], rw_s[:, d], spread(before, 64), ALU.mult).then_inc(scaled.sem, scaled.unit)
                for d in range(2):
                    dve.wait_ge(dn_summed.sem, dn_summed.done(turn, d + 1))
                    o = env.dn_o[:, ds(tiles[d], 1), :].rearrange("p a n -> p (a n)")
                    dve.tensor_tensor(dn_s[:, d].rearrange("p c n -> p (c n)"), bank[:, 2 * d + 1],
                                                  dn_rec[:, s, d, 2].rearrange("p c n -> p (c n)"), ALU.add).then_inc(dn_state.sem, dn_state.unit)
                    dve.tensor_tensor(o, o, bank[:, 2 * d], ALU.add).then_inc(dn_o_added.sem, dn_o_added.unit)
                for d in range(2):
                    dve.wait_ge(rw_summed.sem, rw_summed.done(turn, d + 1))
                    for x in range(2):
                        rows, b = slice(64 * x, 64 * x + 64), 4 + 2 * d + x
                        dve.tensor_tensor(rw_s[rows, d], bank[rows, b, 256:512].rearrange("p (c n) -> p c n", n=64),
                                                    rw_rec[rows, s, d, 768:1024].rearrange("p (c n) -> p c n", n=64), ALU.add).then_inc(rw_mid.sem, rw_mid.unit)
                    dve.wait_ge(rw_mid.sem, rw_mid.done(turn, 2 * d + 2))
                    dve.tensor_tensor(rw_s[:, d], rw_s[:, d], spread(rw_rec[:, s, d, 1028:1032], 64), ALU.mult).then_inc(rw_state.sem, rw_state.unit)
                    o = env.rw_o[:, ds(tiles[d], 1), :].rearrange("p a (c x n) -> p x (a c) n", c=RCH, x=2)
                    dve.tensor_tensor(o, o, bank[:, 4 + 2 * d:6 + 2 * d, 0:256].rearrange("p x (c n) -> p x c n", n=64),
                                                    ALU.add).then_inc(rw_o_added.sem, rw_o_added.unit)
                dve.wait_ge(dn_o_added.sem, dn_o_added.done(turn))
                dve.wait_ge(dn_state.sem, dn_state.done(turn))
                dve.wait_ge(rw_o_added.sem, rw_o_added.done(turn))
                dve.wait_ge(rw_state.sem, rw_state.done(turn))

            steps(dve, body, clear)


def head_out(env):
    nc, io = env.nc, env.io
    E = env.event
    rows_in = E("ho_rows_loaded", per=3, dma=True)
    z_in = E("ho_z_loaded", dma=True)
    side_in = E("ho_side_loaded", dma=True)
    z_turned = E("ho_z_turned")
    squared = E("ho_squared", per=2)
    rooted = E("ho_rooted", per=2)
    dn_steps = E("ho_dn_steps", per=6)
    rw_steps = E("ho_rw_steps", per=11)
    y_turned = E("ho_y_turned", per=2)
    y_copied = E("ho_y_copied", per=2)
    y_stored = E("ho_y_stored", dma=True)
    with ExitStack() as ctx:
        sb, pb = tools(nc, ctx)
        bank = pb("ho_banks", [P, 3, 4, P])
        norm_w = sb("ho_norm_w", [P, P])
        ln_w = sb("ho_ln_w", [P, RWW])
        ln_b = sb("ho_ln_b", [P, RWW])
        zT = sb("ho_zT", [P, 4, P])
        side = sb("ho_side", [P, 2, RWW])
        sq = sb("ho_sq", [P, 2, RWW])
        st = sb("ho_st", [P, 2, 8])
        mean = sb("ho_mean", [P, 8])
        y = sb("ho_y", [P, 2, RWW])
        yT = sb("ho_yT", [P, 8, P])
        block = ctx.enter_context(nc.Block())

        @block.sync
        def _(sp):
            sp.dma_start(norm_w[:], io["dn_norm_w"].to_broadcast([P, P])).then_inc(rows_in.sem, rows_in.unit)
            sp.dma_start(ln_w[:], io["rw_ln_w"].to_broadcast([P, RWW])).then_inc(rows_in.sem, rows_in.unit)
            sp.dma_start(ln_b[:], io["rw_ln_b"].to_broadcast([P, RWW])).then_inc(rows_in.sem, rows_in.unit)

            def load(t):
                sp.dma_start(zT[:], io["ch"][Z0:AB0, ds(t * P, P)].rearrange("(c p) t -> p c t", p=P)).then_inc(z_in.sem, z_in.unit)
                sp.dma_start(side[:].rearrange("p x n -> p (x n)"), io["rw_side"][ds(t, 1)].rearrange("a p x -> p (a x)")).then_inc(side_in.sem, side_in.unit)
            load(0)
            with sp.Fori(1, NT) as t:
                sp.wait_ge(z_turned.sem, z_turned.done(t - 1))
                sp.wait_ge(rw_steps.sem, rw_steps.done(t - 1))
                load(t)

        @block.tensor
        def _(pe):
            with pe.Fori(0, NT) as t:
                pe.wait_ge(z_in.sem, z_in.done(t))
                for c in range(4):
                    tr = pe.transpose(bank[:, 0, c, :], zT[:, c, :], env.ident[:])
                tr.then_inc(z_turned.sem, z_turned.unit)
                for b, steps in ((0, dn_steps), (1, rw_steps)):
                    pe.wait_ge(steps.sem, steps.done(t))
                    for c in range(4):
                        tr = pe.transpose(bank[:, 1 + b, c, :], y[:, b, c * P:(c + 1) * P], env.ident[:])
                    tr.then_inc(y_turned.sem, y_turned.unit)
                pe.wait_ge(y_copied.sem, y_copied.done(t))

        @block.scalar
        def _(act):
            with act.Fori(0, NT) as t:
                o = env.dn_o[:, ds(t, 1), :].rearrange("p a n -> p (a n)")
                act.activation(sq[:, 0], o, ACT.Square).then_inc(squared.sem, squared.unit)
                act.wait_ge(rw_steps.sem, rw_steps.done(t, 3))
                act.activation(sq[:, 1], y[:, 1], ACT.Square).then_inc(squared.sem, squared.unit)
                act.wait_ge(dn_steps.sem, dn_steps.done(t, 2))
                act.activation(st[:, 0, 0:4], st[:, 0, 0:4], ACT.Sqrt).then_inc(rooted.sem, rooted.unit)
                act.wait_ge(rw_steps.sem, rw_steps.done(t, 5))
                act.activation(st[:, 1], st[:, 1], ACT.Sqrt).then_inc(rooted.sem, rooted.unit)
                act.wait_ge(y_stored.sem, y_stored.done(t, 0))
                for b in range(2):
                    act.wait_ge(y_turned.sem, y_turned.done(t, b + 1))
                    act.activation(yT[:, 4 * b:4 * b + 4], bank[:, 1 + b], ACT.Identity).then_inc(y_copied.sem, y_copied.unit)
                act.wait_ge(y_copied.sem, y_copied.done(t))
                act.dma_start(io["yT"][:, ds(t * P, P)].rearrange("(c p) t -> p c t", p=P), yT[:]).then_inc(y_stored.sem, y_stored.unit)
            act.wait_ge(y_stored.sem, y_stored.done(NT - 1))

        @block.vector
        def _(dve):
            dve.wait_ge(rows_in.sem, rows_in.done())
            with dve.Fori(0, NT) as t:
                o = env.rw_o[:, ds(t, 1), :].rearrange("p a (h n) -> p (a h) n", n=64)
                yr = y[:, 1].rearrange("p (h n) -> p h n", n=64)
                dve.tensor_reduce(mean[:], o, AX, ALU.add).then_inc(rw_steps.sem, rw_steps.unit)
                dve.wait_ge(rw_steps.sem, rw_steps.done(t, 1))
                dve.tensor_scalar(mean[:], mean[:], 1.0 / 64, None, ALU.mult).then_inc(rw_steps.sem, rw_steps.unit)
                dve.wait_ge(rw_steps.sem, rw_steps.done(t, 2))
                dve.tensor_tensor(yr, o, spread(mean[:], 64), ALU.subtract).then_inc(rw_steps.sem, rw_steps.unit)
                dve.wait_ge(rw_steps.sem, rw_steps.done(t, 3))
                dve.wait_ge(squared.sem, squared.done(t, 1))
                dve.tensor_reduce(st[:, 0, 0:4], sq[:, 0].rearrange("p (h n) -> p h n", n=P), AX, ALU.add).then_inc(dn_steps.sem, dn_steps.unit)
                dve.wait_ge(dn_steps.sem, dn_steps.done(t, 1))
                dve.tensor_scalar(st[:, 0, 0:4], st[:, 0, 0:4], 1.0 / P, 1e-6, ALU.mult, ALU.add).then_inc(dn_steps.sem, dn_steps.unit)
                dve.wait_ge(dn_steps.sem, dn_steps.done(t, 2))
                dve.wait_ge(squared.sem, squared.done(t, 2))
                dve.tensor_reduce(st[:, 1], sq[:, 1].rearrange("p (h n) -> p h n", n=64), AX, ALU.add).then_inc(rw_steps.sem, rw_steps.unit)
                dve.wait_ge(rw_steps.sem, rw_steps.done(t, 4))
                dve.tensor_scalar(st[:, 1], st[:, 1], 1.0 / 64, 64e-5, ALU.mult, ALU.add).then_inc(rw_steps.sem, rw_steps.unit)
                dve.wait_ge(rw_steps.sem, rw_steps.done(t, 5))
                dve.wait_ge(rooted.sem, rooted.done(t, 1))
                dve.reciprocal(st[:, 0, 0:4], st[:, 0, 0:4]).then_inc(dn_steps.sem, dn_steps.unit)
                dve.wait_ge(dn_steps.sem, dn_steps.done(t, 3))
                yd = y[:, 0].rearrange("p (h n) -> p h n", n=P)
                od = env.dn_o[:, ds(t, 1), :].rearrange("p a (h n) -> p (a h) n", n=P)
                dve.tensor_tensor(yd, od, spread(st[:, 0, 0:4], P), ALU.mult).then_inc(dn_steps.sem, dn_steps.unit)
                dve.wait_ge(dn_steps.sem, dn_steps.done(t, 4))
                dve.tensor_tensor(yd, yd, norm_w[:].unsqueeze(1).to_broadcast([P, 4, P]), ALU.mult).then_inc(dn_steps.sem, dn_steps.unit)
                dve.wait_ge(dn_steps.sem, dn_steps.done(t, 5))
                dve.wait_ge(z_turned.sem, z_turned.done(t))
                dve.tensor_tensor(yd, yd, bank[:, 0], ALU.mult).then_inc(dn_steps.sem, dn_steps.unit)
                dve.wait_ge(dn_steps.sem, dn_steps.done(t, 6))
                dve.wait_ge(rooted.sem, rooted.done(t, 2))
                dve.reciprocal(st[:, 1], st[:, 1]).then_inc(rw_steps.sem, rw_steps.unit)
                dve.wait_ge(rw_steps.sem, rw_steps.done(t, 6))
                dve.tensor_tensor(yr, yr, spread(st[:, 1], 64), ALU.mult).then_inc(rw_steps.sem, rw_steps.unit)
                dve.wait_ge(rw_steps.sem, rw_steps.done(t, 7))
                dve.tensor_tensor(y[:, 1], y[:, 1], ln_w[:], ALU.mult).then_inc(rw_steps.sem, rw_steps.unit)
                dve.wait_ge(rw_steps.sem, rw_steps.done(t, 8))
                dve.tensor_tensor(y[:, 1], y[:, 1], ln_b[:], ALU.add).then_inc(rw_steps.sem, rw_steps.unit)
                dve.wait_ge(rw_steps.sem, rw_steps.done(t, 9))
                dve.wait_ge(side_in.sem, side_in.done(t))
                dve.tensor_tensor(y[:, 1], y[:, 1], side[:, 0], ALU.add).then_inc(rw_steps.sem, rw_steps.unit)
                dve.wait_ge(rw_steps.sem, rw_steps.done(t, 10))
                dve.tensor_tensor(y[:, 1], y[:, 1], side[:, 1], ALU.mult).then_inc(rw_steps.sem, rw_steps.unit)
                dve.wait_ge(rw_steps.sem, rw_steps.done(t, 11))
                dve.wait_ge(y_turned.sem, y_turned.done(t))


def mix_out(env):
    nc, io = env.nc, env.io
    E = env.event
    w_in = E("mx_w_loaded", per=2, dma=True)
    y_in = E("mx_y_loaded", dma=True)
    gate_in = [E(f"mx_gate_loaded{s}", per=2, dma=True) for s in range(2)]
    br_summed = E("mx_br_summed", per=NB)
    br_steps = E("mx_br_steps", per=2 * NB)
    merged_ready = E("mx_merged_ready", per=NB)
    NC8 = D // P
    with ExitStack() as ctx:
        sb, pb = tools(nc, ctx)
        merged = sb("mx_merged", [P, NC8, TOK])
        w_out = sb("mx_w_out", [P, KD, D])
        w_out_in = E("mx_w_out_loaded", dma=True)
        with ExitStack() as inner:
            sb, pb = tools(nc, inner)
            wb = sb("mx_wb", [P, 2, 4, D])
            yT = sb("mx_yT", [P, 8, TOK])
            gate = sb("mx_gate", [P, 2, 2, TOK])
            bank = pb("mx_banks", [P, 2, NB, BLK])
            block = inner.enter_context(nc.Block())

            @block.sync
            def _(sp):
                sp.dma_start(wb[:, 0], io["w_br_dn"][0].rearrange("(k p) n -> p k n", p=P)).then_inc(w_in.sem, w_in.unit)
                sp.dma_start(wb[:, 1], io["w_br_rw"][0].rearrange("(k p) n -> p k n", p=P)).then_inc(w_in.sem, w_in.unit)
                sp.dma_start(yT[:], io["yT"].rearrange("(k p) t -> p k t", p=P)).then_inc(y_in.sem, y_in.unit)

                def load(s, n):
                    for b in range(2):
                        sp.dma_start(gate[:, s, b], io["ch"][ds(G0 + b * D + n * P, P), :]).then_inc(gate_in[s].sem, gate_in[s].unit)
                load(0, 0)
                load(1, 1)
                sp.dma_start(w_out[:], io["w_out"][0].rearrange("(k p) n -> p k n", p=P)).then_inc(w_out_in.sem, w_out_in.unit)
                for n in range(2, NC8):
                    sp.wait_ge(merged_ready.sem, merged_ready.done(n - 2))
                    load(n % 2, n)

            @block.tensor
            def _(pe):
                pe.wait_ge(w_in.sem, w_in.done())
                pe.wait_ge(y_in.sem, y_in.done())
                for n in range(NC8):
                    for b in range(NB):
                        if n:
                            pe.wait_ge(br_steps.sem, br_steps.done(n - 1, 2 * b + 2))
                        for br in range(2):
                            for k in range(4):
                                mm = pe.matmul(bank[:, br, b, :], wb[:, br, k, n * P:(n + 1) * P],
                                               yT[:, 4 * br + k, b * BLK:(b + 1) * BLK], start=(k == 0), stop=(k == 3))
                        mm.then_inc(br_summed.sem, br_summed.unit)

            @block.vector
            def _(dve):
                for n in range(NC8):
                    dve.wait_ge(gate_in[n % 2].sem, gate_in[n % 2].done(n // 2))
                    for b in range(NB):
                        dve.wait_ge(br_summed.sem, br_summed.done(n, b + 1))
                        for br in range(2):
                            g = gate[:, n % 2, br, b * BLK:(b + 1) * BLK]
                            dve.tensor_tensor(g, bank[:, br, b, :], g, ALU.mult).then_inc(br_steps.sem, br_steps.unit)
                        dve.wait_ge(br_steps.sem, br_steps.done(n, 2 * b + 2))
                        cols = slice(b * BLK, (b + 1) * BLK)
                        dve.tensor_tensor(merged[:, n, cols], gate[:, n % 2, 0, cols], gate[:, n % 2, 1, cols], ALU.add).then_inc(merged_ready.sem, merged_ready.unit)

        second_norm(env, ctx, merged, w_out, w_out_in)


def second_norm(env, ctx, merged, w_out, w_out_in):
    nc, io = env.nc, env.io
    E = env.event
    rows_in = E("sn_rows_loaded", per=7, dma=True)
    router_in = E("sn_router_loaded", per=2, dma=True)
    gain_ready = E("sn_gain_ready", per=2)
    x_in = [E(f"sn_x_loaded{s}", dma=True) for s in range(2)]
    taken = E("sn_taken")
    mixed = E("sn_mixed", per=2)
    res_steps = E("sn_res_steps", per=4)
    squared = E("sn_squared")
    meaned = E("sn_meaned")
    rooted = E("sn_rooted")
    h_steps = E("sn_h_steps", per=4)
    h_turned = E("sn_h_turned", per=2)
    h_copied = E("sn_h_copied", per=2)
    routed = E("sn_routed")
    logits_kept = E("sn_logits_kept")
    x1_stored = E("sn_x1_stored", dma=True)
    h2_stored = E("sn_h2_stored", dma=True)
    with ExitStack() as inner:
        sb, pb = tools(nc, inner)
        gate1 = sb("sn_gate1", [P, 2, D])
        shift = sb("sn_shift", [P, 2, D])
        gain = sb("sn_gain", [P, 2, D])
        norm2 = sb("sn_norm2", [P, D])
        router = sb("sn_router", [P, KD, NG + NE])
        x = [sb(f"sn_x{s}", [P, D]) for s in range(2)]
        mT = sb("sn_mT", [P, KD, P])
        x1 = sb("sn_res", [P, D])
        h2 = sb("sn_h2", [P, D])
        h2T = sb("sn_h2T", [P, KD, P])
        sq = sb("sn_sq", [P, D])
        ss = sb("sn_ss", [P, 4])
        mix = pb("sn_mix", [P, 2, BLK])
        turned = pb("sn_turned", [P, 2, 4, P])
        log = pb("sn_log", [P, NG + NE])
        block = inner.enter_context(nc.Block())
        part = io["ada_rows"].rearrange("g (s n) -> s g n", s=6)

        @block.sync
        def _(sp):
            for g in range(2):
                for dst, which in ((gate1, 2), (shift, 3), (gain, 4)):
                    sp.dma_start(dst[:, g], part[which, g:g + 1].to_broadcast([P, D])).then_inc(rows_in.sem, rows_in.unit)
            sp.dma_start(norm2[:], io["norm2"].to_broadcast([P, D])).then_inc(rows_in.sem, rows_in.unit)
            sp.dma_start(router[:, :, 0:NG], io["moe_w_group"][0].rearrange("(k p) e -> p k e", p=P)).then_inc(router_in.sem, router_in.unit)
            sp.dma_start(router[:, :, NG:], io["moe_w_expert"][0].rearrange("(k p) e -> p k e", p=P)).then_inc(router_in.sem, router_in.unit)
            for s in range(2):
                sp.dma_start(x[s][:], io["x_prompt"][0, s * P:(s + 1) * P, :]).then_inc(x_in[s].sem, x_in[s].unit)

            def store(t):
                sp.wait_ge(res_steps.sem, res_steps.done(t))
                sp.dma_start(io["x1"][ds(t * P, P), :], x1[:]).then_inc(x1_stored.sem, x1_stored.unit)
                sp.wait_ge(h_steps.sem, h_steps.done(t))
                sp.dma_start(io["h2"][ds(t * P, P), :], h2[:]).then_inc(h2_stored.sem, h2_stored.unit)

            for g, (t0, n) in enumerate(SEQS):
                src = io["x_prompt"][0] if g == 0 else io["x_sample"][0]
                with sp.Fori(1 if g == 0 else 0, n // 2) as i:
                    for s in range(2):
                        sp.wait_ge(res_steps.sem, res_steps.done(t0 + i * 2 + s - 2))
                        sp.dma_start(x[s][:], src[ds((i * 2 + s) * P, P), :]).then_inc(x_in[s].sem, x_in[s].unit)
                        store(t0 + i * 2 + s - 2)
            store(NT - 2)
            store(NT - 1)
            sp.wait_ge(x1_stored.sem, x1_stored.done(NT - 1))
            sp.wait_ge(h2_stored.sem, h2_stored.done(NT - 1))

        @block.tensor
        def _(pe):
            pe.wait_ge(router_in.sem, router_in.done())
            pe.wait_ge(w_out_in.sem, w_out_in.done())
            with pe.Fori(0, NT) as t:
                pe.wait_ge(taken.sem, taken.done(t))
                for half in range(2):
                    for k in range(KD):
                        mm = pe.matmul(mix[:, half, :], mT[:, k, :], w_out[:, k, half * BLK:(half + 1) * BLK],
                                       start=(k == 0), stop=(k == KD - 1))
                    mm.then_inc(mixed.sem, mixed.unit)
                pe.wait_ge(h_steps.sem, h_steps.done(t))
                for half in range(2):
                    for k in range(4):
                        tr = pe.transpose(turned[:, half, k, :], h2[:, (4 * half + k) * P:(4 * half + k + 1) * P], env.ident[:])
                    tr.then_inc(h_turned.sem, h_turned.unit)
                pe.wait_ge(h_copied.sem, h_copied.done(t))
                pe.wait_ge(logits_kept.sem, logits_kept.done(t, 0))
                for k in range(KD):
                    mm = pe.matmul(log[:], h2T[:, k, :], router[:, k, :], start=(k == 0), stop=(k == KD - 1))
                mm.then_inc(routed.sem, routed.unit)

        @block.scalar
        def _(act):
            with act.Fori(0, NT) as t:
                act.wait_ge(mixed.sem, mixed.done(t, 0))
                act.activation(mT[:], merged[:, :, ds(t * P, P)], ACT.Identity).then_inc(taken.sem, taken.unit)
                act.wait_ge(res_steps.sem, res_steps.done(t))
                act.activation(sq[:], x1[:], ACT.Square, accum_out=ss[:, 0:1]).then_inc(squared.sem, squared.unit)
                act.wait_ge(meaned.sem, meaned.done(t))
                act.activation(ss[:, 2:3], ss[:, 1:2], ACT.Sqrt).then_inc(rooted.sem, rooted.unit)
                for half in range(2):
                    act.wait_ge(h_turned.sem, h_turned.done(t, half + 1))
                    if half == 0:
                        act.wait_ge(routed.sem, routed.done(t, 0))
                    act.activation(h2T[:, 4 * half:4 * half + 4], turned[:, half], ACT.Identity).then_inc(h_copied.sem, h_copied.unit)

        @block.vector
        def _(dve):
            dve.wait_ge(rows_in.sem, rows_in.done())
            dve.tensor_scalar(gain[:], gain[:], 1.0, None, ALU.add).then_inc(gain_ready.sem, gain_ready.unit)
            dve.wait_ge(gain_ready.sem, gain_ready.done(0, 1))
            dve.tensor_tensor(gain[:], gain[:], norm2[:].unsqueeze(1).to_broadcast([P, 2, D]), ALU.mult).then_inc(gain_ready.sem, gain_ready.unit)
            dve.wait_ge(gain_ready.sem, gain_ready.done(0, 2))
            for g, (t0, n) in enumerate(SEQS):
                with dve.Fori(0, n // 2) as i:
                    for s in range(2):
                        t = t0 + i * 2 + s
                        dve.wait_ge(x_in[s].sem, x_in[s].done(t0 // 2 + i))
                        dve.wait_ge(x1_stored.sem, x1_stored.done(t, 0))
                        for half in range(2):
                            cols = slice(half * BLK, (half + 1) * BLK)
                            dve.wait_ge(mixed.sem, mixed.done(t, half + 1))
                            dve.tensor_tensor(x1[:, cols], mix[:, half], gate1[:, g, cols], ALU.mult).then_inc(res_steps.sem, res_steps.unit)
                        dve.wait_ge(res_steps.sem, res_steps.done(t, 2))
                        for half in range(2):
                            cols = slice(half * BLK, (half + 1) * BLK)
                            dve.tensor_tensor(x1[:, cols], x1[:, cols], x[s][:, cols], ALU.add).then_inc(res_steps.sem, res_steps.unit)
                        dve.wait_ge(squared.sem, squared.done(t))
                        dve.tensor_scalar(ss[:, 1:2], ss[:, 0:1], 1.0 / D, 1e-6, ALU.mult, ALU.add).then_inc(meaned.sem, meaned.unit)
                        dve.wait_ge(rooted.sem, rooted.done(t))
                        dve.reciprocal(ss[:, 3:4], ss[:, 2:3]).then_inc(h_steps.sem, h_steps.unit)
                        dve.wait_ge(h_steps.sem, h_steps.done(t, 1))
                        dve.wait_ge(h2_stored.sem, h2_stored.done(t, 0))
                        dve.tensor_scalar(h2[:], x1[:], ss[:, 3:4], None, ALU.mult).then_inc(h_steps.sem, h_steps.unit)
                        dve.wait_ge(h_steps.sem, h_steps.done(t, 2))
                        dve.tensor_tensor(h2[:], h2[:], gain[:, g], ALU.mult).then_inc(h_steps.sem, h_steps.unit)
                        dve.wait_ge(h_steps.sem, h_steps.done(t, 3))
                        dve.tensor_tensor(h2[:], h2[:], shift[:, g], ALU.add).then_inc(h_steps.sem, h_steps.unit)
                        dve.wait_ge(routed.sem, routed.done(t))
                        dve.tensor_copy(env.logits[:, ds(t, 1), :].rearrange("p a e -> p (a e)"), log[:]).then_inc(logits_kept.sem, logits_kept.unit)


BIG = 1e30
MORE = TOK // P - 1


def route(env):
    nc, io = env.nc, env.io
    E = env.event
    bias_in = E("rt_bias_loaded", per=2, dma=True)
    pool_steps = E("rt_pool_steps", per=NPG + MORE + 4)
    zeroed = E("rt_zeroed", dma=True)
    dve_steps = E("rt_dve_steps", per=1)
    exp_in = E("rt_exp_in", per=2)
    exp_done = E("rt_exp_done", per=2)
    pairs_ready = E("rt_pairs_ready")
    ranked = E("rt_ranked")
    places_ready = E("rt_places_ready")
    scattered = E("rt_scattered", per=2 * NT, dma=True)
    table_in = E("rt_table_loaded", dma=True)
    with ExitStack() as ctx:
        sb, pb = tools(nc, ctx)
        bias = sb("rt_bias", [P, NG + NE])
        order = sb("rt_order", [P, NPG])
        steps128 = sb("rt_steps128", [P, MORE])
        token = sb("rt_token", [P, NT], I32)
        zero = sb("rt_zero", [P, NBLOCKS + 1], I32)
        lg = sb("rt_lg", [P, NT, NG + NE])
        eq = sb("rt_eq", [P, NT, NPG])
        top = sb("rt_top", [P, NT])
        first = sb("rt_first", [P, NT])
        group = sb("rt_group", [P, NT, NG])
        gprob = sb("rt_gprob", [P, NT])
        gexp = sb("rt_gexp", [P, NT, NG])
        in_group = sb("rt_in_group", [P, NT, NPG])
        pick = [sb(f"rt_pick{k}", [P, NT, NPG]) for k in range(2)]
        tops = [sb(f"rt_tops{k}", [P, NT]) for k in range(2)]
        wide = sb("rt_wide", [P, NT, NG, NPG])
        pair = [sb(f"rt_pair{k}", [P, NT, NG, NPG]) for k in range(2)]
        both = sb("rt_both", [P, NT * NE])
        before = sb("rt_before", [P, NT + 1, NE])
        more = sb("rt_more", [P, NE, MORE])
        blocks = sb("rt_blocks", [P, NE])
        ends = sb("rt_ends", [P, NE + 2])
        start = sb("rt_start", [P, NE])
        place = sb("rt_place", [P, NT, NE])
        placef = sb("rt_placef", [P, 2, NT])
        rank_ps = pb("rt_rank_ps", [P, NT * NE])
        total_ps = pb("rt_total_ps", [P, NT * NE])
        block = ctx.enter_context(nc.Block())

        @block.sync
        def _(sp):
            sp.dma_start(bias[:, 0:NG], io["moe_b_group"].to_broadcast([P, NG])).then_inc(bias_in.sem, bias_in.unit)
            sp.dma_start(bias[:, NG:], io["moe_b_expert"].to_broadcast([P, NE])).then_inc(bias_in.sem, bias_in.unit)
            sp.wait_ge(pool_steps.sem, pool_steps.done(0, 1))
            sp.dma_start(io["slot_tok"].rearrange("(p b) o -> p (b o)", p=P), zero[:]).then_inc(zeroed.sem, zeroed.unit)
            sp.wait_ge(zeroed.sem, zeroed.done())
            sp.wait_ge(scattered.sem, scattered.done())
            sp.dma_start(env.slot_tok[:], io["slot_tok"].rearrange("(b p) o -> p (b o)", p=P), allow_slow_non_contiguous=True).then_inc(table_in.sem, table_in.unit)
            sp.wait_ge(table_in.sem, table_in.done())

        @block.gpsimd
        def _(pool):
            pool.memset(zero[:], 0).then_inc(pool_steps.sem, pool_steps.unit)
            for i in range(NPG):
                pool.memset(order[:, i:i + 1], float(NPG - i)).then_inc(pool_steps.sem, pool_steps.unit)
            for i in range(MORE):
                pool.memset(steps128[:, i:i + 1], float(P * (i + 1))).then_inc(pool_steps.sem, pool_steps.unit)
            pool.memset(before[:, 0, :], 0.0).then_inc(pool_steps.sem, pool_steps.unit)
            pool.memset(ends[:, 0:1], 0.0).then_inc(pool_steps.sem, pool_steps.unit)
            pool.iota(token[:], pattern=[[P, NT]], base=0, channel_multiplier=1).then_inc(pool_steps.sem, pool_steps.unit)
            pool.wait_ge(pool_steps.sem, pool_steps.done())
            pool.wait_ge(zeroed.sem, zeroed.done())
            pool.wait_ge(places_ready.sem, places_ready.done())
            for k in range(2):
                for t in range(NT):
                    pool.indirect_dma_start(io["slot_tok"], bass.IndirectOffsetOnAxis(ap=env.places[:, k, t:t + 1], axis=0),
                                                         token[:, t:t + 1], None).then_inc(scattered.sem, scattered.unit)

        @block.scalar
        def _(act):
            act.wait_ge(exp_in.sem, exp_in.done(0, 1))
            act.activation(gexp[:], gexp[:], ACT.Exp).then_inc(exp_done.sem, exp_done.unit)
            act.wait_ge(exp_in.sem, exp_in.done(0, 2))
            act.activation(tops[1][:], tops[1][:], ACT.Exp).then_inc(exp_done.sem, exp_done.unit)

        @block.tensor
        def _(pe):
            pe.wait_ge(pairs_ready.sem, pairs_ready.done())
            pe.matmul(rank_ps[:], env.upper[:], both[:], start=True, stop=True)
            pe.matmul(total_ps[:], env.ones[:], both[:], start=True, stop=True).then_inc(ranked.sem, ranked.unit)

        @block.vector
        def _(dve):
            def over(v, n):
                return spread(v, n)

            def first_max(values, n, top_out, onehot):
                ranks = order[:, NPG - n:NPG].unsqueeze(1).to_broadcast([P, NT, n])
                dve.tensor_reduce(top_out[:], values, AX, ALU.max).then_inc(dve_steps.sem, dve_steps.unit)
                dve.wait_ge(dve_steps.sem, dve_steps.next())
                dve.tensor_tensor(eq[:, :, 0:n], values, over(top_out[:], n), ALU.is_equal).then_inc(dve_steps.sem, dve_steps.unit)
                dve.wait_ge(dve_steps.sem, dve_steps.next())
                dve.tensor_tensor(eq[:, :, 0:n], eq[:, :, 0:n], ranks, ALU.mult).then_inc(dve_steps.sem, dve_steps.unit)
                dve.wait_ge(dve_steps.sem, dve_steps.next())
                dve.tensor_reduce(first[:], eq[:, :, 0:n], AX, ALU.max).then_inc(dve_steps.sem, dve_steps.unit)
                dve.wait_ge(dve_steps.sem, dve_steps.next())
                dve.tensor_tensor(onehot, ranks, over(first[:], n), ALU.is_equal).then_inc(dve_steps.sem, dve_steps.unit)
                dve.wait_ge(dve_steps.sem, dve_steps.next())

            dve.wait_ge(bias_in.sem, bias_in.done())
            dve.wait_ge(pool_steps.sem, pool_steps.done())
            dve.tensor_tensor(lg[:], env.logits[:], bias[:].unsqueeze(1).to_broadcast([P, NT, NG + NE]), ALU.add).then_inc(dve_steps.sem, dve_steps.unit)
            dve.wait_ge(dve_steps.sem, dve_steps.next())
            first_max(lg[:, :, 0:NG], NG, top, group[:])
            dve.tensor_tensor(gexp[:], lg[:, :, 0:NG], over(top[:], NG), ALU.subtract).then_inc(dve_steps.sem, dve_steps.unit)
            dve.wait_ge(dve_steps.sem, dve_steps.next())
            dve.tensor_tensor(wide[:], lg[:, :, NG:].rearrange("p t (g e) -> p t g e", g=NG), spread(group[:], NPG, 3), ALU.mult).then_inc(exp_in.sem, exp_in.unit)
            dve.wait_ge(exp_in.sem, exp_in.done(0, 1))
            dve.tensor_reduce(in_group[:], wide[:].rearrange("p t g e -> p t e g"), AX, ALU.add).then_inc(dve_steps.sem, dve_steps.unit)
            dve.wait_ge(dve_steps.sem, dve_steps.next())
            first_max(in_group[:], NPG, tops[0], pick[0][:])
            dve.scalar_tensor_tensor(in_group[:], pick[0][:], -BIG, in_group[:], ALU.mult, ALU.add).then_inc(dve_steps.sem, dve_steps.unit)
            dve.wait_ge(dve_steps.sem, dve_steps.next())
            first_max(in_group[:], NPG, tops[1], pick[1][:])
            dve.tensor_tensor(tops[1][:], tops[1][:], tops[0][:], ALU.subtract).then_inc(exp_in.sem, exp_in.unit)
            for k in range(2):
                dve.tensor_tensor(pair[k][:], spread(group[:], NPG, 3), spread(pick[k][:], NG, 2), ALU.mult).then_inc(dve_steps.sem, dve_steps.unit)
                dve.wait_ge(dve_steps.sem, dve_steps.next())
            dve.tensor_tensor(both[:], pair[0][:].rearrange("p t g e -> p (t g e)"),
                                             pair[1][:].rearrange("p t g e -> p (t g e)"), ALU.add).then_inc(pairs_ready.sem, pairs_ready.unit)
            dve.wait_ge(exp_done.sem, exp_done.done())
            dve.tensor_reduce(gprob[:], gexp[:], AX, ALU.add).then_inc(dve_steps.sem, dve_steps.unit)
            dve.wait_ge(dve_steps.sem, dve_steps.next())
            dve.reciprocal(gprob[:], gprob[:]).then_inc(dve_steps.sem, dve_steps.unit)
            dve.wait_ge(dve_steps.sem, dve_steps.next())
            dve.tensor_scalar(tops[0][:], tops[1][:], 1.0, None, ALU.add).then_inc(dve_steps.sem, dve_steps.unit)
            dve.wait_ge(dve_steps.sem, dve_steps.next())
            dve.reciprocal(tops[0][:], tops[0][:]).then_inc(dve_steps.sem, dve_steps.unit)
            dve.wait_ge(dve_steps.sem, dve_steps.next())
            dve.tensor_tensor(env.weights[:, 0], tops[0][:], gprob[:], ALU.mult).then_inc(dve_steps.sem, dve_steps.unit)
            dve.wait_ge(dve_steps.sem, dve_steps.next())
            dve.tensor_tensor(env.weights[:, 1], env.weights[:, 0], tops[1][:], ALU.mult).then_inc(dve_steps.sem, dve_steps.unit)
            dve.wait_ge(dve_steps.sem, dve_steps.next())
            dve.wait_ge(ranked.sem, ranked.done())
            totals = total_ps[:].rearrange("p (t e) -> p t e", e=NE)
            for t in range(NT):
                dve.tensor_tensor(before[:, t + 1], before[:, t], totals[:, t], ALU.add).then_inc(dve_steps.sem, dve_steps.unit)
                dve.wait_ge(dve_steps.sem, dve_steps.next())
            dve.tensor_tensor(more[:], spread(before[:, NT], MORE), steps128[:].unsqueeze(1).to_broadcast([P, NE, MORE]), ALU.is_gt).then_inc(dve_steps.sem, dve_steps.unit)
            dve.wait_ge(dve_steps.sem, dve_steps.next())
            dve.tensor_reduce(blocks[:], more[:], AX, ALU.add).then_inc(dve_steps.sem, dve_steps.unit)
            dve.wait_ge(dve_steps.sem, dve_steps.next())
            dve.tensor_scalar(blocks[:], blocks[:], 1.0, None, ALU.add).then_inc(dve_steps.sem, dve_steps.unit)
            dve.wait_ge(dve_steps.sem, dve_steps.next())
            dve.tensor_tensor_scan(ends[:, 1:NE + 1], env.ones[:, 0:NE], blocks[:], 0.0, ALU.mult, ALU.add).then_inc(dve_steps.sem, dve_steps.unit)
            dve.wait_ge(dve_steps.sem, dve_steps.next())
            dve.tensor_scalar(ends[:, NE + 1:], ends[:, NE:NE + 1], -1.0, float(NBLOCKS + 1), ALU.mult, ALU.add).then_inc(dve_steps.sem, dve_steps.unit)
            dve.wait_ge(dve_steps.sem, dve_steps.next())
            dve.tensor_copy(env.first_block[:], ends[:]).then_inc(dve_steps.sem, dve_steps.unit)
            dve.wait_ge(dve_steps.sem, dve_steps.next())
            dve.tensor_scalar(start[:], ends[:, 0:NE], float(P), None, ALU.mult).then_inc(dve_steps.sem, dve_steps.unit)
            dve.wait_ge(dve_steps.sem, dve_steps.next())
            dve.tensor_tensor(place[:], rank_ps[:].rearrange("p (t e) -> p t e", e=NE), before[:, 0:NT], ALU.add).then_inc(dve_steps.sem, dve_steps.unit)
            dve.wait_ge(dve_steps.sem, dve_steps.next())
            dve.tensor_tensor(place[:], place[:], start[:].unsqueeze(1).to_broadcast([P, NT, NE]), ALU.add).then_inc(dve_steps.sem, dve_steps.unit)
            dve.wait_ge(dve_steps.sem, dve_steps.next())
            for k in range(2):
                w = wide[:].rearrange("p t g e -> p t (g e)")
                dve.tensor_tensor(w, place[:], pair[k][:].rearrange("p t g e -> p t (g e)"), ALU.mult).then_inc(dve_steps.sem, dve_steps.unit)
                dve.wait_ge(dve_steps.sem, dve_steps.next())
                dve.tensor_reduce(placef[:, k], w, AX, ALU.add).then_inc(dve_steps.sem, dve_steps.unit)
                dve.wait_ge(dve_steps.sem, dve_steps.next())
            dve.tensor_copy(env.places[:], placef[:]).then_inc(places_ready.sem, places_ready.unit)


def experts(env):
    nc, io = env.nc, env.io
    E = env.event
    w_in = [E(f"ex_w_loaded{s}", per=3, dma=True) for s in range(2)]
    picked = E("ex_picked")
    settled = E("ex_settled")
    gathered = E("ex_gathered", dma=True)
    x_turned = E("ex_x_turned")
    x_copied = E("ex_x_copied")
    gu_summed = E("ex_gu_summed")
    silued = E("ex_silued")
    hid_ready = E("ex_hid_ready")
    hid_turned = E("ex_hid_turned")
    hid_copied = E("ex_hid_copied")
    y_summed = E("ex_y_summed")
    y_act = E("ex_y_act")
    y_dve = E("ex_y_dve")
    y_stored = E("ex_y_stored", dma=True)
    zero_ready = E("ex_zero_ready")
    rest_zeroed = E("ex_rest_zeroed", dma=True)
    KF = FF // P
    with ExitStack() as ctx:
        sb, pb = tools(nc, ctx)
        w_up = [sb(f"ex_w_up{s}", [P, 2, KD, FF]) for s in range(2)]
        w_down = [sb(f"ex_w_down{s}", [P, KF, D]) for s in range(2)]
        x = sb("ex_x", [P, D])
        idx = sb("ex_idx", [P, 1], I32)
        xT = sb("ex_xT", [P, KD, P])
        sg = sb("ex_sg", [P, FF])
        hid = sb("ex_hid", [P, FF])
        hidT = sb("ex_hidT", [P, KF, P])
        y = sb("ex_y", [P, 2, BLK])
        zero = sb("ex_zero", [P, D])
        gu = pb("ex_gu", [P, 2, FF])
        tx = pb("ex_tx", [P, KD, P])
        th = pb("ex_th", [P, KF, P])
        yp = pb("ex_yp", [P, 2, BLK])
        block = ctx.enter_context(nc.Block())

        def bound(eng, e):
            at = env.first_block[0:1, ds(e, 1)] if not isinstance(e, int) else env.first_block[0:1, e:e + 1]
            return eng.value_load(at, min_val=0, max_val=NBLOCKS)

        @block.sync
        def _(sp):
            def load(s, e):
                for dst, name in ((w_up[s][:, 0], "moe_w_gate"), (w_up[s][:, 1], "moe_w_up")):
                    sp.dma_start(dst, io[name][0, ds(e, 1)].rearrange("a (p k) f -> (a p) k f", k=KD)).then_inc(w_in[s].sem, w_in[s].unit)
                sp.dma_start(w_down[s][:], io["moe_w_down"][0, ds(e, 1)].rearrange("a (p k) n -> (a p) k n", k=KF)).then_inc(w_in[s].sem, w_in[s].unit)
            load(0, 0)
            sp.wait_ge(zero_ready.sem, zero_ready.done())
            rest = bound(sp, NE + 1)
            with sp.Fori(0, rest) as b:
                sp.dma_start(io["yslots"][ds((NBLOCKS - b) * P, P), :], zero[:]).then_inc(rest_zeroed.sem, rest_zeroed.unit)
            sp.wait_ge(rest_zeroed.sem, rest_zeroed.done(rest, 0))
            load(1, 1)
            with sp.Fori(1, NE // 2) as i:
                for s in range(2):
                    sp.wait_ge(y_summed.sem, y_summed.done(bound(sp, i * 2 + s - 1), 0))
                    load(s, i * 2 + s)

        @block.gpsimd
        def _(pool):
            pool.memset(zero[:], 0.0).then_inc(zero_ready.sem, zero_ready.unit)
            with pool.Fori(0, bound(pool, NE) + 1) as b:
                pool.wait_ge(x_turned.sem, x_turned.done(b, 0))
                pool.wait_ge(settled.sem, settled.done(b, 0))
                pool.tensor_copy(idx[:], env.slot_tok[:, ds(b, 1)]).then_inc(picked.sem, picked.unit)
                pool.wait_ge(picked.sem, picked.done(b))
                settle_pool(pool, env).then_inc(settled.sem, settled.unit)
                pool.indirect_dma_start(x[:], None, io["h2"], bass.IndirectOffsetOnAxis(ap=idx[:, 0:1], axis=0)).then_inc(gathered.sem, gathered.unit)
            total = bound(pool, NE)
            pool.wait_ge(settled.sem, settled.done(total))
            pool.wait_ge(gathered.sem, gathered.done(total))
            settle_pool(pool, env)

        @block.tensor
        def _(pe):
            def turn_x(b):
                pe.wait_ge(gathered.sem, gathered.done(b))
                for k in range(KD):
                    tr = pe.transpose(tx[:, k, :], x[:].rearrange("t (p k) -> t k p", k=KD)[:, k, :], env.ident[:])
                tr.then_inc(x_turned.sem, x_turned.unit)

            turn_x(0)
            with pe.Fori(0, NE // 2) as i:
                for s in range(2):
                    first, end = bound(pe, i * 2 + s), bound(pe, i * 2 + s + 1)
                    with pe.Fori(first, end) as b:
                        pe.wait_ge(w_in[s].sem, w_in[s].done(i))
                        pe.wait_ge(x_copied.sem, x_copied.done(b))
                        for u in range(2):
                            for k in range(KD):
                                mm = pe.matmul(gu[:, u, :], xT[:, k, :], w_up[s][:, u, k, :], start=(k == 0), stop=(k == KD - 1))
                        mm.then_inc(gu_summed.sem, gu_summed.unit)
                        turn_x(b + 1)
                        pe.wait_ge(hid_ready.sem, hid_ready.done(b))
                        for k in range(KF):
                            tr = pe.transpose(th[:, k, :], hid[:].rearrange("t (p k) -> t k p", k=KF)[:, k, :], env.ident[:])
                        tr.then_inc(hid_turned.sem, hid_turned.unit)
                        pe.wait_ge(hid_copied.sem, hid_copied.done(b))
                        pe.wait_ge(y_act.sem, y_act.done(b, 0))
                        pe.wait_ge(y_dve.sem, y_dve.done(b, 0))
                        for half in range(2):
                            for k in range(KF):
                                mm = pe.matmul(yp[:, half, :], hidT[:, k, :], w_down[s][:, k, half * BLK:(half + 1) * BLK],
                                               start=(k == 0), stop=(k == KF - 1))
                        mm.then_inc(y_summed.sem, y_summed.unit)

        @block.scalar
        def _(act):
            act.wait_ge(x_turned.sem, x_turned.done(0))
            act.activation(xT[:], tx[:], ACT.Identity).then_inc(x_copied.sem, x_copied.unit)
            total = bound(act, NE)
            with act.Fori(0, total) as b:
                act.wait_ge(gu_summed.sem, gu_summed.done(b))
                act.activation(sg[:], gu[:, 0, :], ACT.Silu).then_inc(silued.sem, silued.unit)
                act.wait_ge(x_turned.sem, x_turned.done(b + 1))
                act.activation(xT[:], tx[:], ACT.Identity).then_inc(x_copied.sem, x_copied.unit)
                act.wait_ge(y_summed.sem, y_summed.done(b))
                act.wait_ge(y_stored.sem, y_stored.done(b, 0))
                act.activation(y[:, 0], yp[:, 0], ACT.Identity).then_inc(y_act.sem, y_act.unit)
                act.wait_ge(y_act.sem, y_act.done(b))
                act.wait_ge(y_dve.sem, y_dve.done(b))
                act.dma_start(io["yslots"][ds(b * P, P), :], y[:].rearrange("p x n -> p (x n)")).then_inc(y_stored.sem, y_stored.unit)
            act.wait_ge(y_stored.sem, y_stored.done(total, 0))
            act.activation(env.settled[:, 1:2], env.ones[:, 0:1], ACT.Identity)

        @block.vector
        def _(dve):
            with dve.Fori(0, bound(dve, NE)) as b:
                dve.wait_ge(silued.sem, silued.done(b))
                dve.tensor_tensor(hid[:], sg[:], gu[:, 1, :], ALU.mult).then_inc(hid_ready.sem, hid_ready.unit)
                dve.wait_ge(hid_turned.sem, hid_turned.done(b))
                dve.tensor_copy(hidT[:], th[:]).then_inc(hid_copied.sem, hid_copied.unit)
                dve.wait_ge(y_summed.sem, y_summed.done(b))
                dve.wait_ge(y_stored.sem, y_stored.done(b, 0))
                dve.tensor_copy(y[:, 1], yp[:, 1]).then_inc(y_dve.sem, y_dve.unit)


def combine(env):
    nc, io = env.nc, env.io
    E = env.event
    rows_in = E("cb_rows_loaded", per=3, dma=True)
    picked = E("cb_picked")
    settled = E("cb_settled")
    got = [E(f"cb_got{s}", per=2, dma=True) for s in range(2)]
    x_in = [E(f"cb_x_loaded{s}", dma=True) for s in range(2)]
    mix_steps = E("cb_mix_steps", per=4)
    squared = E("cb_squared")
    meaned = E("cb_meaned")
    rooted = E("cb_rooted")
    norm_steps = E("cb_norm_steps", per=3)
    stored = [E(f"cb_stored{s}", dma=True) for s in range(2)]
    with ExitStack() as ctx:
        sb, pb = tools(nc, ctx)
        gate2 = sb("cb_gate2", [P, 2, D])
        final = sb("cb_final", [P, D])
        idx = [sb(f"cb_idx{s}", [P, 2], I32) for s in range(2)]
        got_rows = [sb(f"cb_rows{s}", [P, 2, D]) for s in range(2)]
        x1 = [sb(f"cb_x1{s}", [P, D]) for s in range(2)]
        sq = sb("cb_sq", [P, D])
        ss = sb("cb_ss", [P, 4])
        out = [sb(f"cb_out{s}", [P, D]) for s in range(2)]
        block = ctx.enter_context(nc.Block())

        @block.sync
        def _(sp):
            for g in range(2):
                sp.dma_start(gate2[:, g], io["ada_rows"][g:g + 1, 5 * D:6 * D].to_broadcast([P, D])).then_inc(rows_in.sem, rows_in.unit)
            sp.dma_start(final[:], io["final_norm"].rearrange("(o d) -> o d", o=1).to_broadcast([P, D])).then_inc(rows_in.sem, rows_in.unit)
            with sp.Fori(0, NT // 2) as i:
                for s in range(2):
                    sp.wait_ge(norm_steps.sem, norm_steps.done(i * 2, 0))
                    sp.dma_start(x1[s][:], io["x1"][ds((i * 2 + s) * P, P), :]).then_inc(x_in[s].sem, x_in[s].unit)

        @block.gpsimd
        def _(pool):
            with pool.Fori(0, NT // 2) as i:
                for s in range(2):
                    t = i * 2 + s
                    pool.wait_ge(norm_steps.sem, norm_steps.done(i * 2, 0))
                    pool.wait_ge(settled.sem, settled.done(t, 0))
                    pool.tensor_copy(idx[s][:], env.places[:, :, ds(t, 1)].rearrange("p k a -> p (k a)")).then_inc(picked.sem, picked.unit)
                    pool.wait_ge(picked.sem, picked.done(t))
                    settle_pool(pool, env).then_inc(settled.sem, settled.unit)
                    for k in range(2):
                        pool.indirect_dma_start(got_rows[s][:, k], None, io["yslots"],
                                                          bass.IndirectOffsetOnAxis(ap=idx[s][:, k:k + 1], axis=0)).then_inc(got[s].sem, got[s].unit)

        @block.scalar
        def _(act):
            for g, (t0, n) in enumerate(SEQS):
                with act.Fori(0, n // 2) as i:
                    for s in range(2):
                        t = t0 + i * 2 + s
                        act.wait_ge(mix_steps.sem, mix_steps.done(t))
                        act.activation(sq[:], x1[s][:], ACT.Square, accum_out=ss[:, 0:1]).then_inc(squared.sem, squared.unit)
                        act.wait_ge(meaned.sem, meaned.done(t))
                        act.activation(ss[:, 2:3], ss[:, 1:2], ACT.Sqrt).then_inc(rooted.sem, rooted.unit)
                        act.wait_ge(norm_steps.sem, norm_steps.done(t))
                        dst = io["y_prompt"][0] if g == 0 else io["y_sample"][0]
                        act.dma_start(dst[ds((i * 2 + s) * P, P), :], out[s][:]).then_inc(stored[s].sem, stored[s].unit)
            for s in range(2):
                act.wait_ge(stored[s].sem, stored[s].done(NT // 2 - 1))

        @block.vector
        def _(dve):
            dve.wait_ge(rows_in.sem, rows_in.done())
            for g, (t0, n) in enumerate(SEQS):
                with dve.Fori(0, n // 2) as i:
                    for s in range(2):
                        t = t0 + i * 2 + s
                        half_turn = t0 // 2 + i
                        rows = got_rows[s]
                        dve.wait_ge(got[s].sem, got[s].done(half_turn))
                        dve.tensor_scalar(rows[:, 0], rows[:, 0], env.weights[:, 0, ds(t, 1)], None, ALU.mult).then_inc(mix_steps.sem, mix_steps.unit)
                        dve.wait_ge(mix_steps.sem, mix_steps.done(t, 1))
                        dve.scalar_tensor_tensor(rows[:, 0], rows[:, 1], env.weights[:, 1, ds(t, 1)], rows[:, 0],
                                                              ALU.mult, ALU.add).then_inc(mix_steps.sem, mix_steps.unit)
                        dve.wait_ge(mix_steps.sem, mix_steps.done(t, 2))
                        dve.tensor_tensor(rows[:, 0], rows[:, 0], gate2[:, g], ALU.mult).then_inc(mix_steps.sem, mix_steps.unit)
                        dve.wait_ge(mix_steps.sem, mix_steps.done(t, 3))
                        dve.wait_ge(x_in[s].sem, x_in[s].done(half_turn))
                        dve.tensor_tensor(x1[s][:], rows[:, 0], x1[s][:], ALU.add).then_inc(mix_steps.sem, mix_steps.unit)
                        dve.wait_ge(squared.sem, squared.done(t))
                        dve.tensor_scalar(ss[:, 1:2], ss[:, 0:1], 1.0 / D, 1e-6, ALU.mult, ALU.add).then_inc(meaned.sem, meaned.unit)
                        dve.wait_ge(rooted.sem, rooted.done(t))
                        dve.reciprocal(ss[:, 3:4], ss[:, 2:3]).then_inc(norm_steps.sem, norm_steps.unit)
                        dve.wait_ge(norm_steps.sem, norm_steps.done(t, 1))
                        dve.wait_ge(stored[s].sem, stored[s].done(half_turn, 0))
                        dve.tensor_scalar(out[s][:], x1[s][:], ss[:, 3:4], None, ALU.mult).then_inc(norm_steps.sem, norm_steps.unit)
                        dve.wait_ge(norm_steps.sem, norm_steps.done(t, 2))
                        dve.tensor_tensor(out[s][:], out[s][:], final[:], ALU.mult).then_inc(norm_steps.sem, norm_steps.unit)


SCRATCH = {
    "ada_rows": ((2, 6 * D), F32),
    "ch": ((IN_COLS, TOK), F32),
    "dn_rec": ((NT * 2, P, 3 * DNH * P), F32),
    "rw_rec": ((NT * 2, P, 1032), F32),
    "rw_side": ((NT, P, 2 * RWW), F32),
    "yT": ((DNW + RWW, TOK), F32),
    "x1": ((TOK, D), F32),
    "h2": ((TOK, D), F32),
    "slot_tok": (((NBLOCKS + 1) * P, 1), I32),
    "yslots": ((SLOTS + P, D), F32),
}
OUTPUTS = {"y_prompt": ((1, SEQ[0], D), F32), "y_sample": ((1, SEQ[1], D), F32)}


def program(nc, io):
    with ExitStack() as ctx:
        env = Env(nc, ctx, io)
        constants(env)
        ada(env)
        with ExitStack() as stage:
            norm_in(env, stage)
            project(env)
        env.recycle()
        with ExitStack() as stage:
            env.dn_o = stage.enter_context(nc.sbuf_tensor("dn_o", [P, NT, DNW], F32))
            env.rw_o = stage.enter_context(nc.sbuf_tensor("rw_o", [P, NT, RWW], F32))
            delta(env)
            env.recycle()
            rwkv(env)
            env.recycle()
            recur(env)
            head_out(env)
        env.logits = env.keep("logits", [P, NT, NG + NE])
        mix_out(env)
        env.recycle()
        routed(env)
        route(env)
        experts(env)
        combine(env)


def routed(env):
    env.places = env.keep("places", [P, 2, NT], I32)
    env.weights = env.keep("weights", [P, 2, NT])
    env.first_block = env.keep("first_block", [P, NE + 2], I32)
    env.slot_tok = env.keep("slot_tok_cols", [P, NBLOCKS + 1], I32)


INPUTS = ("x_prompt", "x_sample", "c_prompt", "c_sample", "w_ada", "b_ada", "norm1", "norm2", "w_in",
          "dn_conv_w", "dn_a_log", "dn_dt_bias", "dn_norm_w", "rw_mu", "rw_w0", "rw_w2", "rw_a0", "rw_a2",
          "rw_g2", "rw_k_k", "rw_k_a", "rw_r_k", "rw_ln_w", "rw_ln_b", "w_br_dn", "w_br_rw", "w_out",
          "moe_w_group", "moe_b_group", "moe_w_expert", "moe_b_expert", "moe_w_gate", "moe_w_up",
          "moe_w_down", "final_norm")


def kernel(**inputs):
    import numpy as np
    import concourse.bacc as bacc
    from concourse import mybir
    from concourse.bass_utils import run_bass_kernel_spmd as run

    nc = bacc.Bacc("TRN2", target_bir_lowering=False, num_devices=1)
    arrays, io = {}, {}
    for name in INPUTS:
        a = np.ascontiguousarray(inputs[name])
        arrays[f"in_{name}"] = a
        io[name] = nc.dram_tensor(f"in_{name}", a.shape, mybir.dt.from_np(a.dtype), kind="ExternalInput").ap()
    for name, (shape, dt) in SCRATCH.items():
        io[name] = nc.dram_tensor(f"scratch_{name}", shape, dt).ap()
    for name, (shape, dt) in OUTPUTS.items():
        io[name] = nc.dram_tensor(f"out_{name}", shape, dt, kind="ExternalOutput").ap()
    program(nc, io)
    r = run(nc, [arrays], core_ids=[0])
    return tuple(r.results[0][f"out_{name}"] for name in OUTPUTS)
```

```python
import math
from contextlib import ExitStack

import concourse.bass as bass
from concourse import mybir

ALU = mybir.AluOpType
ACT = mybir.ActivationFunctionType
F32 = mybir.dt.float32
I32 = mybir.dt.int32
U32 = mybir.dt.uint32
AX = mybir.AxisListType.X
ds = bass.ds

P = 128
D = 1024
KD = D // P
SEQ = (1024, 512)
TOK = sum(SEQ)
NT = TOK // P
SEQS = ((0, SEQ[0] // P), (SEQ[0] // P, SEQ[1] // P))
BLK = 512
NB = TOK // BLK
DNH, DNW = 4, 512
RWH, RWW = 8, 512
DN_CONV = 5
QKV_T = 3 * DNW // P
Z0 = 3 * DNW
AB0 = 4 * DNW
RW0 = AB0 + 4 * DNH
RW_COLS = 3 * RWW + 128 + 64 + 128
RW_T = RW_COLS // P
G0 = RW0 + RW_COLS
IN_COLS = G0 + 2 * D
LEVELS = 7
NG, NPG, NE = 4, 8, 32
FF = 512
NBLOCKS = 2 * TOK // P + NE
SLOTS = NBLOCKS * P
BIG = 1e30
HALF_DECAY = -math.exp(-0.5)


class Event:

    def __init__(self, sem, per=1, base=0, unit=1):
        self.sem, self.per, self.base, self.unit = sem, per, base, unit
        self.counted = 0

    def done(self, turn=0, k=None):
        k = self.per if k is None else k
        return turn * (self.per * self.unit) + (self.base + k) * self.unit

    def next(self):
        self.counted += 1
        return self.counted


class Env:

    def __init__(self, nc, ctx, io):
        self.nc, self.ctx, self.io = nc, ctx, io
        self.sems = []

    def sem(self, name):
        self.sems.append(self.nc.alloc_semaphore(name))
        return self.sems[-1]

    def recycle(self):
        self.nc.all_engine_barrier()
        self.nc.clear_and_free_semaphores(self.sems)
        self.nc.all_engine_barrier()
        self.sems = []

    def event(self, name, per=1, base=0, dma=False):
        return Event(self.sem(name), per, base, 16 if dma else 1)

    def keep(self, name, shape, dt=F32):
        return self.ctx.enter_context(self.nc.sbuf_tensor(name, shape, dt))


def tools(nc, ctx):
    def sb(name, shape, dt=F32):
        return ctx.enter_context(nc.sbuf_tensor(name, shape, dt))

    def pb(name, shape, dt=F32):
        return ctx.enter_context(nc.psum_tensor(name, shape, dt))

    return sb, pb


def settle_pool(pool, env):
    return pool.tensor_tensor(env.settled[:, 0:1], env.ones[:, 0:1], env.ones[:, 0:1], ALU.mult)


def spread(ap, n, axis=2):
    shape = list(ap.shape)
    shape.insert(axis, n)
    return ap.unsqueeze(axis).to_broadcast(shape)


V_CONV, V_MU, V_W0, V_A0, V_KK, V_KA, V_RK = 0, 60, 75, 83, 87, 91, 95
V_ROWS = 99


def constants(env):
    nc, io = env.nc, env.io
    env.ident = env.keep("ident", [P, P])
    env.ones = env.keep("ones", [P, P])
    env.settled = env.keep("settled", [P, 2])
    env.headones = env.keep("headones", [P, P])
    env.upper_incl = env.keep("upper_incl", [P, P])
    env.upper = env.keep("upper", [P, P])
    env.lower_incl = env.keep("lower_incl", [P, P])
    env.lower = env.keep("lower", [P, P])
    env.lower_level = env.keep("lower_level", [P, LEVELS, P])
    env.upper_level = env.keep("upper_level", [P, LEVELS, P])
    env.vec = env.keep("vec", [P, V_ROWS + 1])
    env.conv_w = env.keep("conv_w", [P, QKV_T * DN_CONV])
    env.mu_keep = env.keep("mu_keep", [P, RW_T + 1])
    env.mu_half = env.keep("mu_half", [P, RW_T + 1])
    env.ka_rest = env.keep("ka_rest", [P, 4])
    made = env.event("constants_made")
    rows_in = env.event("vec_rows_loaded", per=8, dma=True)
    turned = env.event("vec_turned")
    copied = env.event("vec_copied")
    rows_clear = env.event("vec_rows_clear")

    with ExitStack() as ctx:
        sb, pb = tools(nc, ctx)
        rows = sb("vec_rows", [P, P])
        turned_ps = pb("vec_ps", [P, P])
        block = ctx.enter_context(nc.Block())

        @block.gpsimd
        def _(pool):
            pool.memset(env.ones[:], 1.0).then_inc(made.sem, made.unit)
            pool.wait_ge(made.sem, made.next())
            pool.memset(env.ident[:], 0.0).then_inc(made.sem, made.unit)
            pool.wait_ge(made.sem, made.next())
            pool.affine_select(out=env.ident[:], in_=env.ident[:], compare_op=ALU.not_equal, fill=1.0,
                                    base=0, pattern=[[-1, P]], channel_multiplier=1).then_inc(made.sem, made.unit)
            pool.wait_ge(made.sem, made.next())

        @block.sync
        def _(sp):
            sp.wait_ge(rows_clear.sem, rows_clear.done())
            conv = io["dn_conv_w"].rearrange("o k (t p) -> (o k t) p", p=P)
            sp.dma_start(rows[V_CONV:V_CONV + 60, :], conv).then_inc(rows_in.sem, rows_in.unit)
            mu = io["rw_mu"]
            sp.dma_start(rows[V_MU:V_MU + RW_T, :],
                                    mu[:, 0:RW_T * P].rearrange("o (t p) -> (o t) p", p=P)).then_inc(rows_in.sem, rows_in.unit)
            sp.dma_start(rows[V_MU + RW_T:V_MU + RW_T + 1, 0:RW_COLS - RW_T * P], mu[:, RW_T * P:RW_COLS]).then_inc(rows_in.sem, rows_in.unit)
            sp.dma_start(rows[V_W0:V_W0 + 8, :], io["rw_w0"].rearrange("o d (t p) -> (o d t) p", p=P)).then_inc(rows_in.sem, rows_in.unit)
            for at, name in ((V_A0, "rw_a0"), (V_KK, "rw_k_k"), (V_KA, "rw_k_a")):
                sp.dma_start(rows[at:at + 4, :], io[name].rearrange("o (t p) -> (o t) p", p=P)).then_inc(rows_in.sem, rows_in.unit)
            sp.dma_start(rows[V_RK:V_RK + 4, :],
                                    io["rw_r_k"].rearrange("o (t h) c -> (o t) (h c)", h=2)).then_inc(rows_in.sem, rows_in.unit)

        @block.tensor
        def _(pe):
            pe.wait_ge(made.sem, made.done(0, 3))
            pe.wait_ge(rows_in.sem, rows_in.done())
            pe.transpose(turned_ps[:, 0:V_ROWS + 1], rows[0:V_ROWS + 1, :], env.ident[0:V_ROWS + 1, 0:V_ROWS + 1]).then_inc(turned.sem, turned.unit)

        @block.vector
        def _(dve):
            dve.memset(rows[:], 0.0).then_inc(rows_clear.sem, rows_clear.unit)
            dve.wait_ge(turned.sem, turned.done())
            v = env.vec
            dve.tensor_copy(v[:], turned_ps[:, 0:V_ROWS + 1]).then_inc(copied.sem, copied.unit)
            dve.wait_ge(copied.sem, copied.done())
            dve.tensor_copy(env.conv_w[:].rearrange("p (t k) -> p t k", k=DN_CONV),
                            v[:, V_CONV:V_CONV + 60].rearrange("p (k t) -> p t k", t=QKV_T))
            mu = v[:, V_MU:V_MU + RW_T + 1]
            dve.tensor_scalar(env.mu_keep[:], mu, -1.0, 1.0, ALU.mult, ALU.add)
            dve.tensor_scalar(env.mu_half[:], mu, 0.5, None, ALU.mult)
            dve.tensor_scalar(env.ka_rest[:], v[:, V_KA:V_KA + 4], -1.0, 1.0, ALU.mult, ALU.add)


def triangles(pool, env, made):

    def keep_where(out, base, per_row, pattern):
        pool.affine_select(out=out, in_=out, compare_op=ALU.is_ge, fill=0.0, base=base,
                                pattern=pattern, channel_multiplier=per_row).then_inc(made.sem, made.unit)
        pool.wait_ge(made.sem, made.next())

    for m, base, per_row in ((env.upper_incl, 0, -1), (env.upper, -1, -1),
                             (env.lower_incl, 0, 1), (env.lower, -1, 1)):
        pool.memset(m[:], 1.0).then_inc(made.sem, made.unit)
        pool.wait_ge(made.sem, made.next())
        keep_where(m[:], base, per_row, [[-per_row, P]])
    pool.memset(env.headones[:], 1.0).then_inc(made.sem, made.unit)
    pool.wait_ge(made.sem, made.next())
    by_head = env.headones[:].rearrange("p (b c) -> p b c", c=64)
    keep_where(by_head, 0, 1, [[-64, 2], [0, 64]])
    keep_where(by_head, 63, -1, [[64, 2], [0, 64]])
    for m, row_half, col_zero in ((env.lower_level, 1, 1), (env.upper_level, 0, 0)):
        pool.memset(m[:], 1.0).then_inc(made.sem, made.unit)
        pool.wait_ge(made.sem, made.next())
        for l in range(LEVELS):
            s = 1 << l
            v = m[:, l, :].rearrange("p (b h c) -> p b h c", h=2, c=s)
            pool.memset(v[:, :, col_zero, :], 0.0).then_inc(made.sem, made.unit)
            pool.wait_ge(made.sem, made.next())
            v = m[:, l, :].rearrange("p (b c) -> p b c", c=2 * s)
            keep_where(v, -s * row_half, 1, [[-2 * s, P // (2 * s)], [0, 2 * s]])
            keep_where(v, s * (row_half + 1) - 1, -1, [[2 * s, P // (2 * s)], [0, 2 * s]])


def ada_and_norm(env, ctx):
    nc, io = env.nc, env.io
    E = env.event
    NC = 6 * D // BLK
    assert NC == NT
    env.hT = ctx.enter_context(nc.sbuf_tensor("hT", [P, KD, TOK], F32))
    c_in = E("ada_c_loaded", per=3, dma=True)
    c_ready = E("ada_c_ready")
    w_in = [E(f"ada_w_loaded{s}", dma=True) for s in range(2)]
    x_in = [E(f"n1_x_loaded{s}", dma=True) for s in range(2)]
    summed = E("ada_summed")
    added = E("ada_added")
    stored = E("ada_stored", dma=True)
    norm_in = E("n1_norm_loaded", dma=True)
    cols_in = E("n1_cols_loaded", per=4, dma=True)
    gain_ready = E("n1_gain_ready", per=2)
    squared = E("n1_squared")
    meaned = E("n1_meaned")
    rooted = E("n1_rooted")
    inverted = E("n1_inverted")
    scaled = E("n1_scaled")
    turned = E("n1_turned")
    copied = E("n1_copied")
    made = E("masks_made")
    with ExitStack() as inner:
        sb, pb = tools(nc, inner)
        c_raw = sb("ada_c_raw", [P, 2, KD])
        c_act = sb("ada_c", [P, 2, KD])
        bias = sb("ada_bias", [2, 6 * D])
        w = sb("ada_w", [P, 2, KD, BLK])
        out = sb("ada_out", [2, 6 * D])
        ps = [pb(f"ada_ps{s}", [2, BLK]) for s in range(2)]
        norm1 = sb("n1_norm", [P, KD])
        shift = sb("n1_shift", [P, 2, KD])
        scale = sb("n1_scale", [P, 2, KD])
        gain = sb("n1_gain", [P, 2, KD])
        x = [sb(f"n1_x{s}", [P, D]) for s in range(2)]
        sq = sb("n1_sq", [P, D])
        st = sb("n1_st", [P, 4])
        xn = sb("n1_xn", [P, D])
        xT = [pb(f"n1_xT{s}", [P, KD, P]) for s in range(2)]
        w_view = io["w_ada"].rearrange("o (p k) n -> (o p) k n", k=KD)
        part = io["ada_rows"].rearrange("g (s p k) -> s g p k", s=6, k=KD)
        block = inner.enter_context(nc.Block())

        @block.sync
        def _(sp):
            sp.dma_start(c_raw[:, 0, :], io["c_prompt"].rearrange("o (p k) -> (o p) k", k=KD)).then_inc(c_in.sem, c_in.unit)
            sp.dma_start(c_raw[:, 1, :], io["c_sample"].rearrange("o (p k) -> (o p) k", k=KD)).then_inc(c_in.sem, c_in.unit)
            sp.dma_start(bias[:], io["b_ada"].to_broadcast([2, 6 * D])).then_inc(c_in.sem, c_in.unit)
            for s in range(2):
                sp.dma_start(x[s][:], io["x_prompt"][0, s * P:(s + 1) * P, :]).then_inc(x_in[s].sem, x_in[s].unit)
                sp.dma_start(w[:, s], w_view[:, :, s * BLK:(s + 1) * BLK]).then_inc(w_in[s].sem, w_in[s].unit)
            sp.dma_start(norm1[:], io["norm1"].rearrange("o (p k) -> (o p) k", k=KD)).then_inc(norm_in.sem, norm_in.unit)
            for g, (t0, n) in enumerate(SEQS):
                src = io["x_prompt"][0] if g == 0 else io["x_sample"][0]
                with sp.Fori(1 if g == 0 else 0, n // 2) as i:
                    for s in range(2):
                        t = t0 + i * 2 + s
                        sp.wait_ge(scaled.sem, scaled.done(t - 2))
                        sp.dma_start(x[s][:], src[ds((i * 2 + s) * P, P), :]).then_inc(x_in[s].sem, x_in[s].unit)
                        sp.wait_ge(summed.sem, summed.done(t - 2))
                        sp.dma_start(w[:, s], w_view[:, :, ds(t * BLK, BLK)]).then_inc(w_in[s].sem, w_in[s].unit)
            sp.wait_ge(added.sem, added.done(NC - 1))
            sp.dma_start(io["ada_rows"], out[:]).then_inc(stored.sem, stored.unit)
            sp.wait_ge(stored.sem, stored.done())
            for g in range(2):
                sp.dma_start(shift[:, g, :], part[0, g]).then_inc(cols_in.sem, cols_in.unit)
                sp.dma_start(scale[:, g, :], part[1, g]).then_inc(cols_in.sem, cols_in.unit)

        @block.scalar
        def _(act):
            act.wait_ge(c_in.sem, c_in.done())
            act.activation(c_act[:], c_raw[:], ACT.Silu).then_inc(c_ready.sem, c_ready.unit)
            with act.Fori(0, NT // 2) as i:
                for s in range(2):
                    t = i * 2 + s
                    act.wait_ge(x_in[s].sem, x_in[s].done(i))
                    act.activation(sq[:], x[s][:], ACT.Square, accum_out=st[:, 0:1]).then_inc(squared.sem, squared.unit)
                    act.wait_ge(meaned.sem, meaned.done(t))
                    act.activation(st[:, 2:3], st[:, 1:2], ACT.Sqrt).then_inc(rooted.sem, rooted.unit)
            act.wait_ge(gain_ready.sem, gain_ready.done())
            act.wait_ge(copied.sem, copied.done(NT - 1))
            for k in range(KD // 2, KD):
                for g, (t0, n) in enumerate(SEQS):
                    h = env.hT[:, k, t0 * P:(t0 + n) * P]
                    act.activation(h, h, ACT.Identity, bias=shift[:, g, k:k + 1], scale=gain[:, g, k:k + 1])

        @block.gpsimd
        def _(pool):
            triangles(pool, env, made)

        @block.tensor
        def _(pe):
            pe.wait_ge(c_ready.sem, c_ready.done())
            with pe.Fori(0, NC // 2) as i:
                for s in range(2):
                    t = i * 2 + s
                    pe.wait_ge(scaled.sem, scaled.done(t))
                    pe.wait_ge(copied.sem, copied.done(t - 1, 0) if s else copied.done(t, 0))
                    for k in range(KD):
                        mm = pe.transpose(xT[s][:, k, :], xn[:].rearrange("t (p k) -> t k p", k=KD)[:, k, :], env.ident[:])
                    mm.then_inc(turned.sem, turned.unit)
                    pe.wait_ge(w_in[s].sem, w_in[s].done(i))
                    pe.wait_ge(added.sem, added.done(i * 2, 0))
                    for k in range(KD):
                        mm = pe.matmul(ps[s][:], c_act[:, :, k], w[:, s, k, :], start=(k == 0), stop=(k == KD - 1))
                    mm.then_inc(summed.sem, summed.unit)

        @block.vector
        def _(dve):
            with dve.Fori(0, NC // 2) as i:
                for s in range(2):
                    t = i * 2 + s
                    dve.wait_ge(squared.sem, squared.done(t))
                    dve.tensor_scalar(st[:, 1:2], st[:, 0:1], 1.0 / D, 1e-6, ALU.mult, ALU.add).then_inc(meaned.sem, meaned.unit)
                    dve.wait_ge(rooted.sem, rooted.done(t))
                    dve.reciprocal(st[:, 3:4], st[:, 2:3]).then_inc(inverted.sem, inverted.unit)
                    dve.wait_ge(inverted.sem, inverted.done(t))
                    dve.tensor_scalar(xn[:], x[s][:], st[:, 3:4], None, ALU.mult).then_inc(scaled.sem, scaled.unit)
                    dve.wait_ge(turned.sem, turned.done(t))
                    dve.tensor_copy(env.hT[:, :, ds(t * P, P)], xT[s][:]).then_inc(copied.sem, copied.unit)
                    dve.wait_ge(summed.sem, summed.done(t))
                    cols = ds(t * BLK, BLK)
                    dve.tensor_tensor(out[:, cols], ps[s][:], bias[:, cols], ALU.add).then_inc(added.sem, added.unit)
            dve.wait_ge(cols_in.sem, cols_in.done())
            dve.wait_ge(norm_in.sem, norm_in.done())
            dve.tensor_scalar(scale[:], scale[:], 1.0, None, ALU.add).then_inc(gain_ready.sem, gain_ready.unit)
            dve.wait_ge(gain_ready.sem, gain_ready.done(0, 1))
            dve.tensor_tensor(gain[:], scale[:], norm1[:].unsqueeze(1).to_broadcast([P, 2, KD]), ALU.mult).then_inc(gain_ready.sem, gain_ready.unit)
            dve.wait_ge(gain_ready.sem, gain_ready.done())
            dve.wait_ge(copied.sem, copied.done(NT - 1))
            for k in range(KD // 2):
                for g, (t0, n) in enumerate(SEQS):
                    h = env.hT[:, k, t0 * P:(t0 + n) * P]
                    dve.tensor_scalar(h, h, gain[:, g, k:k + 1], shift[:, g, k:k + 1], ALU.mult, ALU.add)


def project(env):
    nc, io = env.nc, env.io
    kinds = (("conv", 0, QKV_T, P), ("silu", Z0, DNW // P, P), ("shift", RW0, RW_T, P),
             ("sigmoid", G0, 2 * D // P, P), ("shift", RW0 + RW_T * P, 1, RW_COLS - RW_T * P),
             ("copy", AB0, 1, 4 * DNH))
    w_in = [env.event(f"pj_w_loaded{s}", dma=True) for s in range(2)]
    summed = env.event("pj_summed")
    drained = env.event("pj_drained", per=2)
    padded = env.event("pj_padded")
    tapped = env.event("pj_tapped", per=5)
    shaped = env.event("pj_shaped", per=3)
    ready = env.event("pj_ready")
    stored = [env.event(f"pj_stored{s}", per=2, dma=True) for s in range(2)]
    GAP = 4
    S0 = 2 + SEQ[0] + GAP
    WIDE = S0 + SEQ[1] + 2
    OUTW = WIDE - GAP
    OUT1 = S0 - 2
    w_view = io["w_in"].rearrange("o (p k) n -> (o p) k n", k=KD)

    with ExitStack() as ctx:
        sb, pb = tools(nc, ctx)
        w = [sb(f"pj_w{s}", [P, KD, P]) for s in range(2)]
        raw = [sb(f"pj_raw{s}", [P, WIDE]) for s in range(2)]
        mid = sb("pj_mid", [P, OUTW])
        out = [sb(f"pj_out{s}", [P, OUTW]) for s in range(2)]
        ps = [pb(f"pj_ps{s}", [P, NB, BLK]) for s in range(2)]
        block = ctx.enter_context(nc.Block())

        runs, n = [], 0
        for kind, c0, tiles, width in kinds:
            runs.append((kind, c0, tiles, width, n))
            n += tiles
        total = n

        @block.sync
        def _(sp):
            for kind, c0, tiles, width, n0 in runs:
                if tiles == 1:
                    s = n0 % 2
                    sp.wait_ge(summed.sem, summed.done(n0 - 2))
                    sp.dma_start(w[s][:, :, 0:width], w_view[:, :, c0:c0 + width]).then_inc(w_in[s].sem, w_in[s].unit)
                    continue
                if n0 == 0:
                    for s in range(2):
                        sp.dma_start(w[s][:], w_view[:, :, c0 + s * P:c0 + (s + 1) * P]).then_inc(w_in[s].sem, w_in[s].unit)
                with sp.Fori(1 if n0 == 0 else 0, tiles // 2) as i:
                    for s in range(2):
                        sp.wait_ge(summed.sem, summed.done(n0 - 2 + i * 2 + s))
                        sp.dma_start(w[s][:], w_view[:, :, ds(c0 + (i * 2 + s) * P, P)]).then_inc(w_in[s].sem, w_in[s].unit)

        @block.tensor
        def _(pe):
            for kind, c0, tiles, width, n0 in runs:
                def tile(s, i, n, wait_drained=True):
                    pe.wait_ge(w_in[s].sem, w_in[s].done(i))
                    if wait_drained:
                        pe.wait_ge(drained.sem, drained.done(n - 2))
                    for b in range(NB):
                        for k in range(KD):
                            mm = pe.matmul(ps[s][0:width, b, :], w[s][:, k, 0:width], env.hT[:, k, b * BLK:(b + 1) * BLK],
                                           start=(k == 0), stop=(k == KD - 1))
                    mm.then_inc(summed.sem, summed.unit)
                if tiles == 1:
                    tile(n0 % 2, n0 // 2, n0)
                    continue
                if n0 == 0:
                    tile(0, 0, 0, False)
                    tile(1, 0, 1, False)
                with pe.Fori(1 if n0 == 0 else 0, tiles // 2) as i:
                    for s in range(2):
                        tile(s, n0 // 2 + i, n0 + i * 2 + s)

        def columns(t):
            return (t[:, 0:SEQ[0]], t[:, OUT1:OUT1 + SEQ[1]])

        @block.scalar
        def _(act):
            act.wait_ge(padded.sem, padded.done(0, 2))
            shaped_base = 0
            for kind, c0, tiles, width, n0 in runs:
                def tile(s, i, n, c, m, first=False):
                    act.wait_ge(summed.sem, summed.done(n))
                    rows = slice(0, width)
                    flat = ps[s][rows].rearrange("p b t -> p (b t)")
                    if not first:
                        act.wait_ge(stored[s].sem, stored[s].done(i - 1))
                    if kind in ("conv", "shift"):
                        targets = (raw[s][rows, 2:2 + SEQ[0]], raw[s][rows, S0:S0 + SEQ[1]])
                        func = ACT.Identity
                    else:
                        targets = columns(out[s][rows])
                        func = {"silu": ACT.Silu, "sigmoid": ACT.Sigmoid, "copy": ACT.Identity}[kind]
                    for dst, src in zip(targets, (flat[:, 0:SEQ[0]], flat[:, SEQ[0]:TOK])):
                        act.activation(dst, src, func).then_inc(drained.sem, drained.unit)
                    if kind == "conv":
                        act.wait_ge(tapped.sem, tapped.done(n))
                        act.activation(out[s][:], mid[:], ACT.Silu).then_inc(ready.sem, ready.unit)
                        act.wait_ge(ready.sem, ready.done(n))
                    elif kind == "shift":
                        act.wait_ge(shaped.sem, shaped.done(m))
                    else:
                        act.wait_ge(drained.sem, drained.done(n))
                    dst = io["ch"][ds(c0 + c * P, width), :]
                    for (a, b), src in zip(((0, SEQ[0]), (SEQ[0], TOK)), columns(out[s][0:width])):
                        act.dma_start(dst[:, a:b], src).then_inc(stored[s].sem, stored[s].unit)
                if tiles == 1:
                    tile(n0 % 2, n0 // 2, n0, 0, shaped_base)
                else:
                    if n0 == 0:
                        tile(0, 0, 0, 0, 0, True)
                        tile(1, 0, 1, 1, 1, True)
                    with act.Fori(1 if n0 == 0 else 0, tiles // 2) as i:
                        for s in range(2):
                            tile(s, n0 // 2 + i, n0 + i * 2 + s, i * 2 + s, shaped_base + i * 2 + s)
                if kind == "shift":
                    shaped_base += tiles
            for s in range(2):
                act.wait_ge(stored[s].sem, stored[s].done((total - 1 - s) // 2))

        @block.vector
        def _(dve):
            for s in range(2):
                dve.memset(raw[s][:], 0.0).then_inc(padded.sem, padded.unit)
            shaped_base = 0
            for kind, c0, tiles, width, n0 in runs:
                if kind not in ("conv", "shift"):
                    continue
                rows = slice(0, width)

                def conv(s, n, c):
                    dve.wait_ge(drained.sem, drained.done(n))
                    taps = env.conv_w
                    dve.tensor_scalar(mid[:], raw[s][:, 0:OUTW], taps[:, ds(c * DN_CONV, 1)], None, ALU.mult).then_inc(tapped.sem, tapped.unit)
                    for k in range(1, DN_CONV):
                        dve.wait_ge(tapped.sem, tapped.done(n, k))
                        dve.scalar_tensor_tensor(mid[:], raw[s][:, k:k + OUTW], taps[:, ds(c * DN_CONV + k, 1)],
                                                           mid[:], ALU.mult, ALU.add).then_inc(tapped.sem, tapped.unit)

                def shift(s, n, m, c):
                    dve.wait_ge(drained.sem, drained.done(n))
                    x = raw[s][rows]
                    dve.tensor_tensor(mid[rows], x[:, 1:1 + OUTW], x[:, 3:3 + OUTW], ALU.add).then_inc(shaped.sem, shaped.unit)
                    dve.tensor_scalar(out[s][rows], x[:, 2:2 + OUTW], env.mu_keep[rows, ds(c, 1)], None, ALU.mult).then_inc(shaped.sem, shaped.unit)
                    dve.wait_ge(shaped.sem, shaped.done(m, 2))
                    dve.scalar_tensor_tensor(out[s][rows], mid[rows], env.mu_half[rows, ds(c, 1)], out[s][rows],
                                                       ALU.mult, ALU.add).then_inc(shaped.sem, shaped.unit)

                if kind == "conv":
                    conv(0, 0, 0)
                    dve.wait_ge(ready.sem, ready.done(0))
                    conv(1, 1, 1)
                    with dve.Fori(1, tiles // 2) as i:
                        for s in range(2):
                            dve.wait_ge(ready.sem, ready.done(i * 2 + s - 1))
                            conv(s, i * 2 + s, i * 2 + s)
                    dve.wait_ge(ready.sem, ready.done(tiles - 1))
                elif tiles == 1:
                    shift(n0 % 2, n0, shaped_base, RW_T)
                    shaped_base += 1
                else:
                    with dve.Fori(0, tiles // 2) as i:
                        for s in range(2):
                            shift(s, n0 + i * 2 + s, shaped_base + i * 2 + s, i * 2 + s)
                            dve.wait_ge(shaped.sem, shaped.done(shaped_base + i * 2 + s))
                    shaped_base += tiles


HALF = DNH * P


class Solver:

    def __init__(self, env, name, sb, sum_p, sum_x, at=None):
        self.a = sb(f"{name}_a", [P, 4, P])
        self.at = sb(f"{name}_at", [P, 4, P]) if at is None else at
        self.x = sb(f"{name}_x", [P, 2, 4, P])
        self.p = sb(f"{name}_p", [P, 4, P])
        self.sum_p, self.sum_x = sum_p, sum_x
        self.x_ready = env.event(f"{name}_x_ready", per=2 + LEVELS - 1)
        self.xt_started = env.event(f"{name}_xt_started", per=2)
        self.p_summed = env.event(f"{name}_p_summed", per=LEVELS - 1)
        self.p_masked = env.event(f"{name}_p_masked", per=LEVELS - 1)
        self.x_summed = env.event(f"{name}_x_summed", per=LEVELS - 1)

    @property
    def xt(self):
        return self.x[:, 1]

    def start(self, dve, turn, ident, mask):
        dve.tensor_tensor(self.x[:, 0], self.a[:], mask[:, 0:1, :].to_broadcast([P, 4, P]), ALU.mult).then_inc(self.x_ready.sem, self.x_ready.unit)
        dve.wait_ge(self.x_ready.sem, self.x_ready.done(turn, 1))
        dve.tensor_tensor(self.x[:, 0], self.x[:, 0], ident[:].unsqueeze(1).to_broadcast([P, 4, P]), ALU.add).then_inc(self.x_ready.sem, self.x_ready.unit)

    def start_t(self, pool, turn, ident, mask_t):
        pool.tensor_tensor(self.x[:, 1], self.at[:], mask_t[:, 0:1, :].to_broadcast([P, 4, P]), ALU.mult).then_inc(self.xt_started.sem, self.xt_started.unit)
        pool.wait_ge(self.xt_started.sem, self.xt_started.done(turn, 1))
        pool.tensor_tensor(self.x[:, 1], self.x[:, 1], ident[:].unsqueeze(1).to_broadcast([P, 4, P]), ALU.add).then_inc(self.xt_started.sem, self.xt_started.unit)

    def multiply_p(self, pe, turn, level):
        pe.wait_ge(self.x_ready.sem, self.x_ready.done(turn, 1 + level))
        for c in range(4):
            mm = pe.matmul(self.sum_p[:, c, :], self.at[:, c, :], self.x[:, 0, c, :], start=True, stop=True)
        mm.then_inc(self.p_summed.sem, self.p_summed.unit)

    def mask_p(self, dve, turn, level, mask):
        dve.wait_ge(self.p_summed.sem, self.p_summed.done(turn, level))
        dve.tensor_tensor(self.p[:], self.sum_p, mask[:, level:level + 1, :].to_broadcast([P, 4, P]), ALU.mult).then_inc(self.p_masked.sem, self.p_masked.unit)

    def multiply_x(self, pe, turn, level):
        pe.wait_ge(self.p_masked.sem, self.p_masked.done(turn, level))
        if level == 1:
            pe.wait_ge(self.xt_started.sem, self.xt_started.done(turn))
        for c in range(4):
            if level < LEVELS - 1:
                pe.matmul(self.sum_x[:, 0, c, :], self.x[:, 1, c, :], self.p[:, c, :], start=True, stop=True)
            mm = pe.matmul(self.sum_x[:, 1, c, :], self.p[:, c, :], self.x[:, 1, c, :], start=True, stop=True)
        mm.then_inc(self.x_summed.sem, self.x_summed.unit)

    def add_x(self, dve, turn, level):
        dve.wait_ge(self.x_summed.sem, self.x_summed.done(turn, level))
        which = slice(0, 2) if level < LEVELS - 1 else slice(1, 2)
        v = self.x[:, which].rearrange("p x c n -> p (x c) n")
        dve.tensor_tensor(v, v, self.sum_x[:, which].rearrange("p x c n -> p (x c) n"), ALU.add).then_inc(self.x_ready.sem, self.x_ready.unit)

    def solved(self, eng, turn):
        eng.wait_ge(self.x_ready.sem, self.x_ready.done(turn))


def solve_products(pe, solvers, turn, meanwhile=None):
    for level in range(1, LEVELS):
        for s in solvers:
            s.multiply_p(pe, turn, level)
        if meanwhile:
            meanwhile(level)
        for s in solvers:
            s.multiply_x(pe, turn, level)


def solve_sums(dve, solvers, turn, masks, meanwhile=None):
    for level in range(1, LEVELS):
        for s, m in zip(solvers, masks):
            s.mask_p(dve, turn, level, m)
        if meanwhile:
            meanwhile(level)
        for s in solvers:
            s.add_x(dve, turn, level)


def delta(env):
    nc, io = env.nc, env.io
    E = env.event
    qkv_in = E("dn_qkv_loaded", per=2, dma=True)
    rows_in = E("dn_rows_loaded", per=2, dma=True)
    neg_a_ready = E("dn_neg_a_ready")
    taken = E("dn_taken")
    qk_turned = E("dn_qk_turned")
    qk_read = E("dn_qk_read", per=2)
    ab_read = E("dn_ab_read")
    v_read = E("dn_v_read")
    norm_steps = E("dn_norm_steps", per=4)
    rooted = E("dn_rooted")
    k_ready = E("dn_k_ready", per=2)
    gate_steps = E("dn_gate_steps", per=5)
    gate_act = E("dn_gate_act", per=3)
    rows_summed = E("dn_rows_summed")
    summed_g = E("dn_g_summed")
    g_copied = E("dn_g_copied", per=3)
    decay_steps = E("dn_decay_steps", per=5)
    decayed = E("dn_decayed", per=2)
    small_exp = E("dn_small_exp", per=3)
    turned_kq = E("dn_kq_turned")
    kq_copied = E("dn_kq_copied", per=2)
    crossed = E("dn_crossed")
    masked = E("dn_masked")
    far_ready = E("dn_far_ready", per=4)
    scaled = E("dn_scaled", per=11)
    a_ready = E("dn_a_ready", per=4)
    at_turned = E("dn_at_turned")
    at_copied = E("dn_at_copied", per=2)
    w_summed = E("dn_w_summed", per=2)
    w_copied = E("dn_w_copied", per=2)
    out_summed = E("dn_out_summed", per=3)
    o_kept = E("dn_o_kept")
    out_ready = E("dn_out_ready", per=5)
    rec_stored = E("dn_rec_stored", per=2, dma=True)

    with ExitStack() as ctx:
        sb, pb = tools(nc, ctx)
        bank = pb("dn_banks", [P, 8, 4, P])
        qkvT = sb("dn_qkvT", [P, QKV_T, P])
        abT = sb("dn_abT", [4 * DNH, P])
        dt_bias = sb("dn_dt_bias", [P, 8])
        neg_a = sb("dn_neg_a", [P, 8])
        sq = sb("dn_sq", [P, 8, P])
        ss = sb("dn_ss", [P, 8])
        root = sb("dn_root", [P, 8])
        rnorm = sb("dn_rnorm", [P, 8])
        v = sb("dn_v", [P, DNH, P])
        raw = sb("dn_raw", [P, 8, P])
        far = sb("dn_far", [P, 2, P])
        far_q = sb("dn_far_q", [P, 2, P])
        qk = sb("dn_qk", [P, 2, DNH, P])
        qkT = sb("dn_qkT", [P, 2, DNH, P])
        ab = sb("dn_ab", [P, 16])
        soft = sb("dn_soft", [P, 4, 8])
        la = sb("dn_la", [P, 8])
        beta = sb("dn_beta", [P, 8])
        g = sb("dn_g", [P, 16])
        tail = sb("dn_tail", [P, 8])
        eg = sb("dn_eg", [P, 8])
        etail = sb("dn_etail", [P, 8])
        etot = sb("dn_etot", [P, 8])
        neg_beta = sb("dn_neg_beta", [P, 8])
        neg_beg = sb("dn_neg_beg", [P, 8])
        diff = sb("dn_diff", [P, 8, P])
        dpos = sb("dn_dpos", [P, 8, P])
        decay = sb("dn_decay", [P, 8, P])
        decayT = sb("dn_decayT", [P, 8, P])
        qkm = sb("dn_qkm", [P, 8, P])
        rhs = sb("dn_rhs", [P, 8, 2, P])
        qe = sb("dn_qe", [P, 8, P])
        kt = sb("dn_kt", [P, 8, P])
        diag = sb("dn_diag", [P, 8, P])
        w = sb("dn_w", [P, 8, 2, P])
        rec = sb("dn_rec", [P, 2, 3, DNH, P])
        sf = Solver(env, "dn_sf", sb, bank[:, 6], bank[:, 0:2])
        sr = Solver(env, "dn_sr", sb, bank[:, 7], bank[:, 2:4])
        block = ctx.enter_context(nc.Block())
        lead = (env.upper_incl, env.lower_incl)

        def dirs(m):
            return m[:].rearrange("p (d h) n -> p d h n", d=2)

        def per_head(v8):
            return spread(v8, P)

        @block.sync
        def _(sp):
            sp.dma_start(dt_bias[:], io["dn_dt_bias"].rearrange("o d h -> o (d h)").to_broadcast([P, 8])).then_inc(rows_in.sem, rows_in.unit)
            sp.dma_start(neg_a[:], io["dn_a_log"].rearrange("o d h -> o (d h)").to_broadcast([P, 8])).then_inc(rows_in.sem, rows_in.unit)

            def load(t):
                cols = ds(t * P, P)
                sp.dma_start(qkvT[:], io["ch"][0:3 * DNW, cols].rearrange("(c p) t -> p c t", p=P)).then_inc(qkv_in.sem, qkv_in.unit)
                sp.dma_start(abT[:], io["ch"][AB0:RW0, cols]).then_inc(qkv_in.sem, qkv_in.unit)

            load(0)

            def store(t):
                sp.wait_ge(out_ready.sem, out_ready.done(t))
                for d in range(2):
                    sp.dma_start(io["dn_rec"][ds(t * 2 + d, 1)].rearrange("a p x -> p (a x)"),
                                               rec[:, d].rearrange("p x c n -> p (x c n)")).then_inc(rec_stored.sem, rec_stored.unit)

            with sp.Fori(1, NT) as t:
                sp.wait_ge(taken.sem, taken.done(t - 1))
                load(t)
                store(t - 1)
            store(NT - 1)
            sp.wait_ge(rec_stored.sem, rec_stored.done(NT - 1))

        @block.tensor
        def _(pe):
            ident = env.ident[:]
            pe.wait_ge(neg_a_ready.sem, neg_a_ready.done())

            def turn_qk(t):
                pe.wait_ge(qkv_in.sem, qkv_in.done(t))
                for c in range(8):
                    tr = pe.transpose(bank[:, 4 + c // 4, c % 4, :], qkvT[:, c, :], ident)
                tr.then_inc(qk_turned.sem, qk_turned.unit)

            def turn_v(t):
                pe.wait_ge(qk_read.sem, qk_read.done(t))
                for c in range(4):
                    pe.transpose(bank[:, 4, c, :], qkvT[:, 8 + c, :], ident)
                pe.transpose(bank[:, 5, 0, 0:16], abT[:], ident[0:16, 0:16]).then_inc(taken.sem, taken.unit)

            def sum_rows(t):
                pe.wait_ge(gate_steps.sem, gate_steps.done(t))
                pe.wait_ge(ab_read.sem, ab_read.done(t))
                pe.wait_ge(v_read.sem, v_read.done(t))
                for d in range(2):
                    pe.matmul(bank[:, 5, 1, 4 * d:4 * d + 4], lead[d][:], la[:, 4 * d:4 * d + 4], start=True, stop=True)
                pe.matmul(bank[:, 5, 1, 8:16], env.ones[:], la[:], start=True, stop=True).then_inc(rows_summed.sem, rows_summed.unit)

            def sum_columns(t):
                pe.wait_ge(g_copied.sem, g_copied.done(t, 1))
                for c in range(8):
                    mm = pe.matmul(bank[:, 4 + c // 4, c % 4, :], la[:, c:c + 1].to_broadcast([P, P]), lead[c // 4][:],
                                   start=True, stop=True)
                mm.then_inc(summed_g.sem, summed_g.unit)

            def tile(t, after=True, ahead=True):
                if after:
                    pe.wait_ge(o_kept.sem, o_kept.done(t - 1))
                pe.wait_ge(k_ready.sem, k_ready.done(t))
                for c in range(8):
                    tr = pe.transpose(bank[:, 6 + c // 4, c % 4, :], qk[:, c // 4, c % 4, :], ident)
                tr.then_inc(turned_kq.sem, turned_kq.unit)
                if after:
                    pe.wait_ge(out_ready.sem, out_ready.done(t - 1))
                pe.wait_ge(kq_copied.sem, kq_copied.done(t))
                for h in range(DNH):
                    pe.matmul(bank[:, 0, h, :], qkT[:, 1, h, :], qkT[:, 1, h, :], start=True, stop=True)
                    mm = pe.matmul(bank[:, 1, h, :], qkT[:, 1, h, :], qkT[:, 0, h, :], start=True, stop=True)
                mm.then_inc(crossed.sem, crossed.unit)
                pe.wait_ge(a_ready.sem, a_ready.done(t, 2))
                for c in range(8):
                    s = (sf, sr)[c // 4]
                    tr = pe.transpose(bank[:, 4 + c // 4, c % 4, :], s.a[:, c % 4, :], ident)
                tr.then_inc(at_turned.sem, at_turned.unit)
                pe.wait_ge(at_copied.sem, at_copied.done(t))
                pe.wait_ge(a_ready.sem, a_ready.done(t))

                def meanwhile(level):
                    if ahead and level == 1:
                        turn_qk(t + 1)
                    if ahead and level == 2:
                        turn_v(t + 1)
                    if ahead and level == 5:
                        sum_rows(t + 1)
                    if ahead and level == 6:
                        sum_columns(t + 1)

                solve_products(pe, (sf, sr), t, meanwhile)
                pe.wait_ge(scaled.sem, scaled.done(t))
                for d, s in enumerate((sf, sr)):
                    s.solved(pe, t)
                    for h in range(DNH):
                        mm = pe.matmul(bank[:, 2 * d + h // 2, 2 * (h % 2):2 * (h % 2) + 2, :], s.xt[:, h, :],
                                       rhs[:, 4 * d + h], start=True, stop=True)
                    mm.then_inc(w_summed.sem, w_summed.unit)
                pe.wait_ge(w_copied.sem, w_copied.done(t))
                for h in range(DNH):
                    for d in range(2):
                        c = 4 * d + h
                        mm = pe.matmul(bank[:, 6, h, :], qkm[:, c, :], w[:, c, 0, :], start=(d == 0), stop=(d == 1))
                mm.then_inc(out_summed.sem, out_summed.unit)
                if ahead:
                    pe.wait_ge(decay_steps.sem, decay_steps.done(t + 1, 1))
                for c in range(8):
                    d, h = c // 4, c % 4
                    pe.matmul(bank[:, 4 + d, h, :], qe[:, c, :], ident, start=True, stop=False)
                    mm = pe.matmul(bank[:, 4 + d, h, :], w[:, c, 1, :], qkm[:, c, :], start=False, stop=True)
                mm.then_inc(out_summed.sem, out_summed.unit)
                for c in range(8):
                    d, h = c // 4, c % 4
                    pe.matmul(bank[:, d, h, :], w[:, c, 1, :], kt[:, c, :], start=True, stop=True)
                    mm = pe.matmul(bank[:, 2 + d, h, :], kt[:, c, :], w[:, c, 0, :], start=True, stop=True)
                mm.then_inc(out_summed.sem, out_summed.unit)

            turn_qk(0)
            turn_v(0)
            sum_rows(0)
            sum_columns(0)
            pe.wait_ge(decay_steps.sem, decay_steps.done(0, 1))
            tile(0, after=False)
            with pe.Fori(1, NT - 1) as t:
                tile(t)
            tile(NT - 1, ahead=False)

        @block.scalar
        def _(act):
            act.wait_ge(rows_in.sem, rows_in.done())
            act.activation(neg_a[:], neg_a[:], ACT.Exp).then_inc(neg_a_ready.sem, neg_a_ready.unit)

            def read_qk(t):
                act.wait_ge(qk_turned.sem, qk_turned.done(t))
                both = bank[:, 4:6].rearrange("p b c n -> p (b c) n")
                act.activation(sq[:], both, ACT.Square).then_inc(qk_read.sem, qk_read.unit)
                act.activation(raw[:], both, ACT.Identity).then_inc(qk_read.sem, qk_read.unit)

            def read_v(t):
                act.wait_ge(taken.sem, taken.done(t))
                act.activation(ab[:], bank[:, 5, 0, 0:16], ACT.Identity).then_inc(ab_read.sem, ab_read.unit)
                act.wait_ge(scaled.sem, scaled.done(t, 0))
                act.activation(v[:], bank[:, 4], ACT.Identity).then_inc(v_read.sem, v_read.unit)
                act.wait_ge(gate_steps.sem, gate_steps.done(t, 2))
                act.activation(soft[:, 2, :], soft[:, 1, :], ACT.Exp, scale=-1.0).then_inc(gate_act.sem, gate_act.unit)
                act.wait_ge(gate_act.sem, gate_act.done(t, 1))
                act.activation(soft[:, 3, :], soft[:, 2, :], ACT.Ln, bias=1.0).then_inc(gate_act.sem, gate_act.unit)
                act.wait_ge(norm_steps.sem, norm_steps.done(t, 2))
                act.activation(root[:], ss[:], ACT.Sqrt).then_inc(rooted.sem, rooted.unit)
                act.activation(beta[:], ab[:, 8:16], ACT.Sigmoid).then_inc(gate_act.sem, gate_act.unit)

            def decays(t):
                act.wait_ge(decay_steps.sem, decay_steps.done(t))
                act.activation(decay[:], dpos[:], ACT.Exp, scale=-1.0).then_inc(decayed.sem, decayed.unit)
                act.activation(decayT[:], diff[:], ACT.Exp).then_inc(decayed.sem, decayed.unit)
                act.wait_ge(g_copied.sem, g_copied.done(t))
                act.activation(eg[:], g[:, 0:8], ACT.Exp).then_inc(small_exp.sem, small_exp.unit)
                act.activation(etail[:], tail[:], ACT.Exp).then_inc(small_exp.sem, small_exp.unit)
                act.activation(etot[:], g[:, 8:16], ACT.Exp).then_inc(small_exp.sem, small_exp.unit)

            def tile(t, ahead=True):
                act.wait_ge(turned_kq.sem, turned_kq.done(t))
                for x in range(2):
                    act.activation(qkT[:, x], bank[:, 6 + x], ACT.Identity).then_inc(kq_copied.sem, kq_copied.unit)
                act.wait_ge(at_turned.sem, at_turned.done(t))
                for d, s in enumerate((sf, sr)):
                    act.activation(s.at[:], bank[:, 4 + d], ACT.Identity).then_inc(at_copied.sem, at_copied.unit)
                if ahead:
                    read_qk(t + 1)
                    read_v(t + 1)
                for d in range(2):
                    act.wait_ge(w_summed.sem, w_summed.done(t, d + 1))
                    act.activation(w[:, 4 * d:4 * d + 4].rearrange("p c x n -> p (c x) n"),
                                               bank[:, 2 * d:2 * d + 2].rearrange("p b c n -> p (b c) n"), ACT.Identity).then_inc(w_copied.sem, w_copied.unit)
                if ahead:
                    decays(t + 1)
                act.wait_ge(out_summed.sem, out_summed.done(t, 2))
                act.wait_ge(rec_stored.sem, rec_stored.done(t, 0))
                act.activation(rec[:, :, 0], bank[:, 4:6], ACT.Identity).then_inc(out_ready.sem, out_ready.unit)
                act.wait_ge(out_summed.sem, out_summed.done(t, 3))
                for d in range(2):
                    act.activation(rec[:, d, 2], bank[:, 2 + d], ACT.Identity).then_inc(out_ready.sem, out_ready.unit)

            read_qk(0)
            read_v(0)
            decays(0)
            with act.Fori(0, NT - 1) as t:
                tile(t)
            tile(NT - 1, False)

        @block.vector
        def _(dve):
            dve.wait_ge(neg_a_ready.sem, neg_a_ready.done())
            for d, (strict, incl) in enumerate(((env.lower, env.upper_incl), (env.upper, env.lower_incl))):
                dve.tensor_scalar(far[:, d], strict[:], -BIG, BIG, ALU.mult, ALU.add).then_inc(far_ready.sem, far_ready.unit)
                dve.tensor_scalar(far_q[:, d], incl[:], BIG, -BIG, ALU.mult, ALU.add).then_inc(far_ready.sem, far_ready.unit)
            dve.wait_ge(far_ready.sem, far_ready.done())

            def far_from(m, d):
                return m[:, d:d + 1].to_broadcast([P, 4, P])

            def gates(t):
                dve.wait_ge(ab_read.sem, ab_read.done(t))
                dve.tensor_tensor(soft[:, 0, :], ab[:, 0:8], dt_bias[:], ALU.add).then_inc(gate_steps.sem, gate_steps.unit)
                dve.wait_ge(gate_steps.sem, gate_steps.done(t, 1))
                dve.scalar_tensor_tensor(soft[:, 1, :], soft[:, 0, :], -1.0, soft[:, 0, :], ALU.mult, ALU.max).then_inc(gate_steps.sem, gate_steps.unit)
                dve.tensor_scalar(soft[:, 0, :], soft[:, 0, :], 0.0, None, ALU.max).then_inc(gate_steps.sem, gate_steps.unit)
                dve.wait_ge(qk_read.sem, qk_read.done(t))
                dve.tensor_reduce(ss[:], sq[:], AX, ALU.add).then_inc(norm_steps.sem, norm_steps.unit)
                dve.wait_ge(norm_steps.sem, norm_steps.done(t, 1))
                dve.tensor_scalar(ss[:], ss[:], 1e-6, None, ALU.add).then_inc(norm_steps.sem, norm_steps.unit)

            def log_alpha(t):
                dve.wait_ge(gate_act.sem, gate_act.done(t, 2))
                dve.wait_ge(gate_steps.sem, gate_steps.done(t, 3))
                dve.tensor_tensor(soft[:, 1, :], soft[:, 0, :], soft[:, 3, :], ALU.add).then_inc(gate_steps.sem, gate_steps.unit)
                dve.wait_ge(gate_steps.sem, gate_steps.done(t, 4))
                dve.scalar_tensor_tensor(la[:], soft[:, 1, :], -1.0, neg_a[:], ALU.mult, ALU.mult).then_inc(gate_steps.sem, gate_steps.unit)
                dve.wait_ge(rooted.sem, rooted.done(t))
                dve.reciprocal(rnorm[:], root[:]).then_inc(norm_steps.sem, norm_steps.unit)
                dve.wait_ge(norm_steps.sem, norm_steps.done(t, 3))
                dve.tensor_scalar(rnorm[:, 0:4], rnorm[:, 0:4], float(P) ** -0.5, None, ALU.mult).then_inc(norm_steps.sem, norm_steps.unit)

            def copy_rows(t):
                dve.wait_ge(rows_summed.sem, rows_summed.done(t))
                dve.tensor_copy(g[:], bank[:, 5, 1, 0:16]).then_inc(g_copied.sem, g_copied.unit)

            def decays(t):
                dve.wait_ge(summed_g.sem, summed_g.done(t))
                dve.tensor_tensor(diff[:], bank[:, 4:6].rearrange("p b c n -> p (b c) n"), per_head(g[:, 0:8]), ALU.subtract).then_inc(decay_steps.sem, decay_steps.unit)
                dve.wait_ge(decay_steps.sem, decay_steps.done(t, 1))
                for d in range(2):
                    dve.scalar_tensor_tensor(dirs(dpos)[:, d], dirs(diff)[:, d], 0.0, far_from(far, d), ALU.max, ALU.add).then_inc(decay_steps.sem, decay_steps.unit)
                    dve.scalar_tensor_tensor(dirs(diff)[:, d], dirs(diff)[:, d], 0.0, far_from(far_q, d), ALU.min, ALU.add).then_inc(decay_steps.sem, decay_steps.unit)
                dve.tensor_tensor(tail[:], g[:, 8:16], g[:, 0:8], ALU.subtract).then_inc(g_copied.sem, g_copied.unit)
                dve.wait_ge(gate_act.sem, gate_act.done(t))
                dve.tensor_scalar(neg_beta[:], beta[:], -1.0, None, ALU.mult).then_inc(g_copied.sem, g_copied.unit)
                dve.wait_ge(g_copied.sem, g_copied.done(t))

            def tile(t, ahead=True):
                dve.wait_ge(crossed.sem, crossed.done(t))
                dve.wait_ge(masked.sem, masked.done(t))
                for d, s in enumerate((sf, sr)):
                    dve.tensor_tensor(s.a[:], bank[:, 0], decay[:, 4 * d:4 * d + 4], ALU.mult).then_inc(a_ready.sem, a_ready.unit)
                dve.wait_ge(a_ready.sem, a_ready.done(t, 2))
                sf.start(dve, t, env.ident, env.lower_level)
                sr.start(dve, t, env.ident, env.upper_level)
                for d in range(2):
                    dve.tensor_tensor(qkm[:, 4 * d:4 * d + 4], bank[:, 1], decayT[:, 4 * d:4 * d + 4], ALU.mult).then_inc(a_ready.sem, a_ready.unit)

                def meanwhile(level):
                    if ahead and level == 3:
                        gates(t + 1)
                    if ahead and level == 4:
                        log_alpha(t + 1)
                    if ahead and level == 5:
                        copy_rows(t + 1)

                solve_sums(dve, (sf, sr), t, (env.lower_level, env.upper_level), meanwhile)
                if ahead:
                    decays(t + 1)
                dve.wait_ge(out_summed.sem, out_summed.done(t, 1))
                dve.tensor_copy(env.dn_o[:, ds(t, 1), :].rearrange("p a (c n) -> p (a c) n", n=P), bank[:, 6]).then_inc(o_kept.sem, o_kept.unit)
                dve.wait_ge(out_summed.sem, out_summed.done(t, 3))
                dve.wait_ge(rec_stored.sem, rec_stored.done(t, 0))
                dve.wait_ge(scaled.sem, scaled.done(t))
                for d in range(2):
                    dve.tensor_tensor(rec[:, d, 1], bank[:, d], diag[:, 4 * d:4 * d + 4], ALU.add).then_inc(out_ready.sem, out_ready.unit)

            gates(0)
            log_alpha(0)
            copy_rows(0)
            decays(0)
            with dve.Fori(0, NT - 1) as t:
                tile(t)
            tile(NT - 1, False)

        @block.gpsimd
        def _(pool):
            def normalise(t):
                pool.wait_ge(norm_steps.sem, norm_steps.done(t))
                for x in range(2):
                    pool.tensor_tensor(qk[:, x], raw[:, 4 * x:4 * x + 4], per_head(rnorm[:, 4 * x:4 * x + 4]), ALU.mult).then_inc(k_ready.sem, k_ready.unit)

            def tile(t, ahead=True):
                pool.wait_ge(g_copied.sem, g_copied.done(t))
                pool.wait_ge(decayed.sem, decayed.done(t))
                pool.tensor_tensor(decay[:], decay[:], per_head(neg_beta[:]), ALU.mult).then_inc(masked.sem, masked.unit)
                pool.wait_ge(at_copied.sem, at_copied.done(t, 1))
                sf.start_t(pool, t, env.ident, env.upper_level)
                pool.wait_ge(at_copied.sem, at_copied.done(t, 2))
                sr.start_t(pool, t, env.ident, env.lower_level)
                pool.wait_ge(small_exp.sem, small_exp.done(t))
                pool.tensor_tensor(neg_beg[:], neg_beta[:], eg[:], ALU.mult).then_inc(scaled.sem, scaled.unit)
                pool.wait_ge(scaled.sem, scaled.done(t, 1))
                for d in range(2):
                    cs = slice(4 * d, 4 * d + 4)
                    for out, in_, factor in ((rhs[:, cs, 0], v[:], beta), (rhs[:, cs, 1], qk[:, 1], neg_beg),
                                             (qe[:, cs], qk[:, 0], eg), (kt[:, cs], qk[:, 1], etail),
                                             (diag[:, cs], env.ident[:].unsqueeze(1).to_broadcast([P, 4, P]), etot)):
                        pool.tensor_tensor(out, in_, per_head(factor[:, cs]), ALU.mult).then_inc(scaled.sem, scaled.unit)
                pool.wait_ge(scaled.sem, scaled.done(t))
                if ahead:
                    normalise(t + 1)

            normalise(0)
            with pool.Fori(0, NT - 1) as t:
                tile(t)
            tile(NT - 1, False)


RCH = RWW // P


def rwkv(env):
    nc, io = env.nc, env.io
    E = env.event
    weights_in = E("rw_weights_loaded", per=3, dma=True)
    consts_ready = E("rw_consts_ready", per=5)
    masks_ready = E("rw_masks_ready", per=4)
    cols_in = E("rw_cols_loaded", per=4, dma=True)
    low_ready = E("rw_low_ready", per=2)
    low_summed = E("rw_low_summed", per=2)
    biased = E("rw_biased", per=2)
    sigmoided = E("rw_sigmoided", per=2)
    log_decay = E("rw_log_decay")
    scanned = E("rw_scanned")
    centred = E("rw_centred")
    decayed = E("rw_decayed", per=2)
    kk_steps = E("rw_kk_steps", per=2)
    kk_summed = E("rw_kk_summed")
    kk_norm = E("rw_kk_norm", per=2)
    rooted = E("rw_rooted")
    b_steps = E("rw_b_steps", per=3)
    kp_steps = E("rw_kp_steps", per=3)
    bonus_steps = E("rw_bonus_steps", per=2)
    bonus_summed = E("rw_bonus_summed")
    bonus_copied = E("rw_bonus_copied")
    bonus_ready = E("rw_bonus_ready")
    v_turned = E("rw_v_turned")
    v_ready = E("rw_v_ready", per=2)
    side_stored = E("rw_side_stored", dma=True)
    prods = E("rw_prods", per=8)
    edges_kept = E("rw_edges_kept", per=4)
    tok_turned = E("rw_tok_turned", per=2)
    tok_copied = E("rw_tok_copied", per=6)
    crossed = E("rw_crossed", per=16)
    cross_kept = E("rw_cross_kept", per=16)
    a_kept = E("rw_a_kept", per=4)
    m2v_summed = E("rw_m2v_summed", per=2)
    m2v_copied = E("rw_m2v_copied", per=2)
    w_summed = E("rw_w_summed", per=4)
    w_copied = E("rw_w_copied", per=4)
    out_summed = E("rw_out_summed", per=4)
    o_kept = E("rw_o_kept", per=2)
    out_dve = E("rw_out_dve", per=4)
    out_act = E("rw_out_act", per=2)
    scal_ready = E("rw_scal_ready", per=1)
    rec_stored = E("rw_rec_stored", per=2, dma=True)

    with ExitStack() as ctx:
        sb, pb = tools(nc, ctx)
        bank = pb("rw_banks", [P, 8, 4, P])
        w2 = sb("rw_w2s", [P, RWW])
        a2 = sb("rw_a2s", [64, RWW])
        g2 = sb("rw_g2s", [P, RWW])
        head_ident = sb("rw_head_ident", [P, 64])
        seg = sb("rw_seg", [P, 8, P + 1])
        lw = sb("rw_lw", [P, 8, P + 1])
        cross_mask = sb("rw_cross_mask", [P, 2, 4, P])
        rkvT = sb("rw_rkvT", [P, 3 * RCH, P])
        wdT = sb("rw_wdT", [P, P])
        adT = sb("rw_adT", [64, P])
        gdT = sb("rw_gdT", [P, P])
        pre = sb("rw_pre", [P, 12, P])
        cum = sb("rw_cum", [P, 8, P + 1])
        factors = sb("rw_factors", [P, 2])
        ep = sb("rw_ep", [P, 8, P + 1])
        en = sb("rw_en", [P, 8, P + 1])
        kk = sb("rw_kk", [P, RCH, P])
        sq = sb("rw_sq", [P, RCH, P])
        inv = sb("rw_inv", [P, RCH, P])
        kp = sb("rw_kp", [P, RCH, P])
        nb = sb("rw_nb", [P, RCH, P])
        bon = sb("rw_bon", [P, RCH, P])
        bonus = sb("rw_bonus", [P, 8])
        v2 = [sb(f"rw_v{s}", [P, RWH, 64]) for s in range(2)]
        kr2 = [sb(f"rw_kr{s}", [P, 2, RCH, 2, P]) for s in range(2)]
        bt2 = [sb(f"rw_bt{s}", [P, 2, RCH, P]) for s in range(2)]
        kt2 = [sb(f"rw_kt{s}", [P, 2, RCH, P]) for s in range(2)]
        edges2 = [sb(f"rw_edges{s}", [P, 2, 8]) for s in range(2)]
        side = sb("rw_side", [P, 2, RWW])
        tok_b = sb("rw_tok_b", [P, RWH, 64])
        tok_k = sb("rw_tok_k", [P, RWH, 64])
        rhs = sb("rw_rhs", [P, RWH, 2, 64])
        w = sb("rw_w", [P, RWH, 2, 64])
        cross = sb("rw_cross", [P, RWH, 4, P])
        rec = sb("rw_rec", [P, 2, 1032])
        solvers = (Solver(env, "rw_s0", sb, bank[:, 6], bank[:, 0:2], cross[:, 0:RWH:2, 0, :]),
                   Solver(env, "rw_s1", sb, bank[:, 7], bank[:, 2:4], cross[:, 1:RWH:2, 0, :]))
        block = ctx.enter_context(nc.Block())
        r, k = rkvT[:, 0:RCH], rkvT[:, RCH:2 * RCH]
        levels = (env.lower_level, env.upper_level)
        evens_then_odds = (*range(0, RWH, 2), *range(1, RWH, 2))

        def per_channel(at, n=RCH):
            return spread(env.vec[:, at:at + n], P)

        @block.sync
        def _(sp):
            sp.dma_start(w2[:], io["rw_w2"].rearrange("o d r c -> (o d r) c")).then_inc(weights_in.sem, weights_in.unit)
            sp.dma_start(a2[:], io["rw_a2"][0]).then_inc(weights_in.sem, weights_in.unit)
            sp.dma_start(g2[:], io["rw_g2"][0]).then_inc(weights_in.sem, weights_in.unit)

            def load(t):
                cols = ds(t * P, P)
                low = RW0 + 3 * RWW
                sp.dma_start(rkvT[:], io["ch"][RW0:low, cols].rearrange("(c p) t -> p c t", p=P)).then_inc(cols_in.sem, cols_in.unit)
                sp.dma_start(wdT[:], io["ch"][low:low + 128, cols]).then_inc(cols_in.sem, cols_in.unit)
                sp.dma_start(adT[:], io["ch"][low + 128:low + 192, cols]).then_inc(cols_in.sem, cols_in.unit)
                sp.dma_start(gdT[:], io["ch"][low + 192:G0, cols]).then_inc(cols_in.sem, cols_in.unit)

            def after_preparation(t):
                sp.wait_ge(low_summed.sem, low_summed.done(t))
                sp.wait_ge(v_turned.sem, v_turned.done(t))
                sp.wait_ge(prods.sem, prods.done(t))
                sp.wait_ge(bonus_steps.sem, bonus_steps.done(t))

            def store_side(t):
                sp.wait_ge(bonus_ready.sem, bonus_ready.done(t))
                sp.wait_ge(v_ready.sem, v_ready.done(t))
                sp.dma_start(io["rw_side"][ds(t, 1)].rearrange("a p x -> p (a x)"),
                             side[:].rearrange("p x n -> p (x n)")).then_inc(side_stored.sem, side_stored.unit)

            def store_rec(t):
                sp.wait_ge(out_dve.sem, out_dve.done(t))
                sp.wait_ge(out_act.sem, out_act.done(t))
                sp.wait_ge(scal_ready.sem, scal_ready.done(t))
                for d in range(2):
                    sp.dma_start(io["rw_rec"][ds(t * 2 + d, 1)].rearrange("a p x -> p (a x)"),
                                 rec[:, d]).then_inc(rec_stored.sem, rec_stored.unit)

            load(0)
            after_preparation(0)
            load(1)
            store_side(0)
            with sp.Fori(2, NT) as t:
                after_preparation(t - 1)
                load(t)
                store_side(t - 1)
                store_rec(t - 2)
            store_side(NT - 1)
            store_rec(NT - 2)
            store_rec(NT - 1)
            sp.wait_ge(rec_stored.sem, rec_stored.done(NT - 1))
            sp.wait_ge(side_stored.sem, side_stored.done(NT - 1))

        @block.tensor
        def _(pe):
            pe.wait_ge(weights_in.sem, weights_in.done())

            def outputs_read(t, d):
                pe.wait_ge(out_dve.sem, out_dve.done(t, 2 * d + 2))
                pe.wait_ge(out_act.sem, out_act.done(t, d + 1))

            def prepare(t, after_outputs=True):
                pe.wait_ge(cols_in.sem, cols_in.done(t))
                for c in range(RCH):
                    tr = pe.transpose(bank[:, 5, c, :], rkvT[:, 2 * RCH + c, :], env.ident[:])
                tr.then_inc(v_turned.sem, v_turned.unit)
                pe.wait_ge(kk_steps.sem, kk_steps.done(t))
                pe.matmul(bank[:, 4].rearrange("p c n -> p (c n)"), env.headones[:], sq[:].rearrange("p c n -> p (c n)"),
                          start=True, stop=True).then_inc(kk_summed.sem, kk_summed.unit)
                pe.wait_ge(low_ready.sem, low_ready.done(t))
                for d in range(2):
                    rows = slice(64 * d, 64 * d + 64)
                    for c in range(RCH):
                        pe.matmul(bank[:, d, c, :], w2[rows, c * P:(c + 1) * P], wdT[rows, :], start=True, stop=True)
                if after_outputs:
                    outputs_read(t - 1, 0)
                for c in range(RCH):
                    mm = pe.matmul(bank[:, 2, c, :], a2[:, c * P:(c + 1) * P], adT[:], start=True, stop=True)
                mm.then_inc(low_summed.sem, low_summed.unit)
                pe.matmul(bank[:, 3].rearrange("p c n -> p (c n)"), gdT[:], g2[:], start=True, stop=True).then_inc(low_summed.sem, low_summed.unit)
                pe.wait_ge(biased.sem, biased.done(t))
                pe.wait_ge(v_ready.sem, v_ready.done(t))
                pe.wait_ge(kk_norm.sem, kk_norm.done(t, 1))

            def sum_bonus(t):
                pe.wait_ge(bonus_steps.sem, bonus_steps.done(t))
                for c in range(RCH):
                    mm = pe.matmul(bank[:, 7, 0, 2 * c:2 * c + 2], bon[:, c, :], env.headones[:, 0:P:64], start=True, stop=True)
                mm.then_inc(bonus_summed.sem, bonus_summed.unit)

            def tile(t, s, ahead=True):
                kr, bt, kt, v = kr2[s], bt2[s], kt2[s], v2[s]
                pe.wait_ge(prods.sem, prods.done(t))
                pe.wait_ge(bonus_copied.sem, bonus_copied.done(t))
                for d in range(2):
                    for c in range(RCH):
                        pe.transpose(bank[:, 4, c, :], kr[:, d, c, 0, :], env.ident[:])
                        pe.transpose(bank[:, 5, c, :], bt[:, d, c, :], env.ident[:])
                        tr = pe.transpose(bank[:, 6, c, :], kt[:, d, c, :], env.ident[:])
                    tr.then_inc(tok_turned.sem, tok_turned.unit)
                    for h in range(RWH):
                        rows, c = slice(64 * (h % 2), 64 * (h % 2) + 64), h // 2
                        both = kr[rows, d, c].rearrange("p x n -> p (x n)")
                        if h >= 4:
                            pe.wait_ge(cross_kept.sem, cross_kept.done(t, 8 * d + h - 3))
                        if h == 1:
                            pe.wait_ge(tok_copied.sem, tok_copied.done(t, 3 * d + 1))
                        pe.matmul(bank[:, h % 4, 0:2, :], bt[rows, d, c, :], both, start=True, stop=True)
                        pe.matmul(bank[:, h % 4, 2:4, :], kt[rows, d, c, :], both, start=True, stop=True)
                        mm = pe.matmul(bank[:, (7, 4)[h % 2], c, :], kr[rows, d, c, 0, :], bt[rows, d, c, :],
                                       start=True, stop=True)
                        mm.then_inc(crossed.sem, crossed.unit)
                    pe.wait_ge(tok_copied.sem, tok_copied.done(t, 3 * d + 3))
                    pe.wait_ge(a_kept.sem, a_kept.done(t, 2 * d + 2))
                    pe.wait_ge(cross_kept.sem, cross_kept.done(t, 8 * d + 8))
                    solve_products(pe, solvers, t * 2 + d)
                    for h in range(RWH):
                        mm = pe.matmul(bank[:, 4].rearrange("p c (x n) -> p (c x) n", n=64)[:, h, :], cross[:, h, 2, :], v[:, h, :],
                                       start=True, stop=True)
                    mm.then_inc(m2v_summed.sem, m2v_summed.unit)
                    pe.wait_ge(m2v_copied.sem, m2v_copied.done(t, d + 1))
                    for n, solver in enumerate(solvers):
                        solver.solved(pe, t * 2 + d)
                        for h in range(n, RWH, 2):
                            mm = pe.matmul(bank[:, n, h // 2, :], solver.xt[:, h // 2, :], rhs[:, h].rearrange("p x n -> p (x n)"),
                                           start=True, stop=True)
                        mm.then_inc(w_summed.sem, w_summed.unit)
                    if d == 1 and ahead:
                        sum_bonus(t + 1)
                    for h in evens_then_odds:
                        if h < 2:
                            pe.wait_ge(w_copied.sem, w_copied.done(t, 2 * d + h + 1))
                        o = bank[:, 5].rearrange("p c (x n) -> p (c x) n", n=64)[:, h, :]
                        pe.matmul(o, cross[:, h, 3, :], v[:, h, :], start=True, stop=False)
                        mm = pe.matmul(o, cross[:, h, 1, :], w[:, h, 1, :], start=False, stop=True)
                    mm.then_inc(out_summed.sem, out_summed.unit)
                    for h in evens_then_odds:
                        rows, c = slice(64 * (h % 2), 64 * (h % 2) + 64), h // 2
                        pe.matmul(bank[rows, 2, c, :], w[:, h, 0, :], cross[:, h, 1, :], start=True, stop=True)
                        small = bank[rows, 3].rearrange("p (x c2) (y n) -> p x (c2 y) n", x=2, n=64)
                        pe.matmul(small[:, 0, c, :], w[:, h, 0, :], tok_b[:, h, :], start=True, stop=True)
                        pe.matmul(small[:, 1, c, :], tok_k[:, h, :], v[:, h, :], start=True, stop=False)
                        mm = pe.matmul(small[:, 1, c, :], tok_b[:, h, :], w[:, h, 1, :], start=False, stop=True)
                    mm.then_inc(out_summed.sem, out_summed.unit)
                    pe.wait_ge(o_kept.sem, o_kept.done(t, d + 1))
                    if d == 1 or not ahead:
                        outputs_read(t, d)
                    if d == 0 and ahead:
                        prepare(t + 1)

            prepare(0, False)
            sum_bonus(0)
            with pe.Fori(0, NT // 2 - 1) as i:
                for s in range(2):
                    tile(i * 2 + s, s)
            tile(NT - 2, 0)
            tile(NT - 1, 1, False)

        @block.scalar
        def _(act):
            def squash_low(t):
                act.wait_ge(cols_in.sem, cols_in.done(t))
                act.activation(wdT[:], wdT[:], ACT.Tanh).then_inc(low_ready.sem, low_ready.unit)
                act.activation(gdT[:], gdT[:], ACT.Sigmoid).then_inc(low_ready.sem, low_ready.unit)

            def read_prepared(t, s):
                act.wait_ge(v_turned.sem, v_turned.done(t))
                act.activation(v2[s][:].rearrange("p (c x) n -> p c (x n)", x=2), bank[:, 5], ACT.Identity).then_inc(v_ready.sem, v_ready.unit)
                act.wait_ge(low_summed.sem, low_summed.done(t))
                act.wait_ge(side_stored.sem, side_stored.done(t, 0))
                act.activation(side[:, 1], bank[:, 3].rearrange("p c n -> p (c n)"), ACT.Identity).then_inc(v_ready.sem, v_ready.unit)

            def squash(t, s):
                for x in range(2):
                    cs = (slice(0, 8), slice(8, 12))[x]
                    act.wait_ge(biased.sem, biased.done(t, x + 1))
                    act.activation(pre[:, cs], pre[:, cs], ACT.Sigmoid).then_inc(sigmoided.sem, sigmoided.unit)
                act.wait_ge(kk_norm.sem, kk_norm.done(t, 1))
                act.activation(inv[:], sq[:], ACT.Sqrt).then_inc(rooted.sem, rooted.unit)
                act.wait_ge(centred.sem, centred.done(t))
                act.activation(ep[:], en[:], ACT.Exp).then_inc(decayed.sem, decayed.unit)
                act.wait_ge(decayed.sem, decayed.done(t, 1))
                act.activation(en[:], en[:], ACT.Exp, scale=-1.0).then_inc(decayed.sem, decayed.unit)
                act.wait_ge(decayed.sem, decayed.done(t))
                for d, (before, at0, behind, at1) in enumerate(((en, 0, ep, P), (ep, P, en, 0))):
                    act.activation(edges2[s][:, d, 0:4], before[:, 4 * d:4 * d + 4, at0], ACT.Identity).then_inc(edges_kept.sem, edges_kept.unit)
                    act.activation(edges2[s][:, d, 4:8], behind[:, 4 * d:4 * d + 4, at1], ACT.Identity).then_inc(edges_kept.sem, edges_kept.unit)

            def tile(t, s, ahead=True):
                for d in range(2):
                    act.wait_ge(tok_turned.sem, tok_turned.done(t, d + 1))
                    dst = rhs[:, :, 0, :].rearrange("p (c x) n -> p c x n", x=2)
                    act.activation(dst, bank[:, 4].rearrange("p c (x n) -> p c x n", x=2), ACT.Identity).then_inc(tok_copied.sem, tok_copied.unit)
                    act.activation(tok_b[:].rearrange("p (c x) n -> p c (x n)", x=2), bank[:, 5], ACT.Identity).then_inc(tok_copied.sem, tok_copied.unit)
                    act.activation(tok_k[:].rearrange("p (c x) n -> p c (x n)", x=2), bank[:, 6], ACT.Identity).then_inc(tok_copied.sem, tok_copied.unit)
                    if ahead:
                        if d == 0:
                            squash_low(t + 1)
                        else:
                            squash(t + 1, 1 - s)
                    act.wait_ge(m2v_summed.sem, m2v_summed.done(t, d + 1))
                    act.activation(rhs[:, :, 1, :], bank[:, 4].rearrange("p c (x n) -> p (c x) n", x=2), ACT.Identity).then_inc(m2v_copied.sem, m2v_copied.unit)
                    for n in range(2):
                        act.wait_ge(w_summed.sem, w_summed.done(t, 2 * d + n + 1))
                        act.activation(w[:, n:RWH:2].rearrange("p h x n -> p h (x n)"), bank[:, n], ACT.Identity).then_inc(w_copied.sem, w_copied.unit)
                    act.wait_ge(out_summed.sem, out_summed.done(t, 2 * d + 2))
                    if d == 0:
                        act.wait_ge(rec_stored.sem, rec_stored.done(t, 0))
                    act.activation(rec[:, d, 768:1024], bank[:, 3, 2:4].rearrange("p c n -> p (c n)"), ACT.Identity).then_inc(out_act.sem, out_act.unit)
                    if d == 0:
                        act.wait_ge(edges_kept.sem, edges_kept.done(t))
                        act.activation(rec[:, :, 1024:1032], edges2[s][:], ACT.Identity).then_inc(scal_ready.sem, scal_ready.unit)
                        if ahead:
                            read_prepared(t + 1, 1 - s)

            squash_low(0)
            read_prepared(0, 0)
            squash(0, 0)
            with act.Fori(0, NT // 2 - 1) as i:
                for s in range(2):
                    tile(i * 2 + s, s)
            tile(NT - 2, 0)
            tile(NT - 1, 1, False)

        @block.vector
        def _(dve):
            dve.wait_ge(masks_ready.sem, masks_ready.done())
            dve.tensor_tensor(head_ident[:], env.ident[:, 0:64], env.ident[:, 64:128], ALU.add).then_inc(consts_ready.sem, consts_ready.unit)
            for d, (strict, incl) in enumerate(((env.upper, env.upper_incl), (env.lower, env.lower_incl))):
                for x, m in enumerate((strict, incl)):
                    dve.tensor_copy(cross_mask[:, d, x:4:2, :], m[:].unsqueeze(1).to_broadcast([P, 2, P])).then_inc(consts_ready.sem, consts_ready.unit)
            dve.wait_ge(consts_ready.sem, consts_ready.done())

            def read_prepared(t):
                dve.wait_ge(kk_summed.sem, kk_summed.done(t))
                dve.tensor_scalar(sq[:], bank[:, 4], 1e-12, None, ALU.add).then_inc(kk_norm.sem, kk_norm.unit)
                dve.wait_ge(low_summed.sem, low_summed.done(t, 1))
                dve.tensor_tensor(pre[:, 0:8], bank[:, 0:2].rearrange("p b c n -> p (b c) n"), per_channel(V_W0, 8),
                                  ALU.add).then_inc(biased.sem, biased.unit)
                dve.tensor_tensor(pre[:, 8:12], bank[:, 2], per_channel(V_A0), ALU.add).then_inc(biased.sem, biased.unit)

            def scan(t):
                dve.wait_ge(log_decay.sem, log_decay.done(t))
                dve.tensor_tensor_scan(cum[:].rearrange("p c n -> p (c n)"), seg[:].rearrange("p c n -> p (c n)"),
                                       lw[:].rearrange("p c n -> p (c n)"), 0.0, ALU.mult, ALU.add).then_inc(scanned.sem, scanned.unit)

            def invert(t):
                dve.wait_ge(rooted.sem, rooted.done(t))
                dve.reciprocal(inv[:], inv[:]).then_inc(kk_norm.sem, kk_norm.unit)

            def copy_bonus(t):
                dve.wait_ge(bonus_summed.sem, bonus_summed.done(t))
                dve.tensor_copy(bonus[:], bank[:, 7, 0, 0:8]).then_inc(bonus_copied.sem, bonus_copied.unit)

            def tile(t, s, ahead=True):
                kr = kr2[s]
                for d in range(2):
                    strict_a = (env.lower, env.upper)[d]
                    for h in range(RWH):
                        dve.wait_ge(crossed.sem, crossed.done(t, 8 * d + h + 1))
                        if h == RWH - 1:
                            dve.tensor_tensor(solvers[0].a[:], bank[:, 7], strict_a[:].unsqueeze(1).to_broadcast([P, 4, P]),
                                              ALU.mult).then_inc(a_kept.sem, a_kept.unit)
                            dve.wait_ge(a_kept.sem, a_kept.done(t, 2 * d + 1))
                            solvers[0].start(dve, t * 2 + d, env.ident, levels[d])
                        dve.tensor_tensor(cross[:, h], bank[:, h % 4], cross_mask[:, d], ALU.mult).then_inc(cross_kept.sem, cross_kept.unit)
                    dve.tensor_tensor(solvers[1].a[:], bank[:, 4], strict_a[:].unsqueeze(1).to_broadcast([P, 4, P]),
                                      ALU.mult).then_inc(a_kept.sem, a_kept.unit)
                    dve.wait_ge(a_kept.sem, a_kept.done(t, 2 * d + 2))
                    solvers[1].start(dve, t * 2 + d, env.ident, levels[d])

                    def meanwhile(level):
                        if d == 1 and ahead and level == 3:
                            scan(t + 1)
                        if d == 1 and ahead and level == 5:
                            invert(t + 1)

                    solve_sums(dve, solvers, t * 2 + d, (levels[d], levels[d]), meanwhile)
                    if d == 1 and ahead:
                        copy_bonus(t + 1)
                    dve.wait_ge(out_summed.sem, out_summed.done(t, 2 * d + 1))
                    kept = env.rw_o[:, ds(t, 1), :].rearrange("p a n -> p (a n)")
                    o0 = bank[:, 5].rearrange("p c n -> p (c n)")
                    if d == 0:
                        dve.tensor_copy(kept, o0).then_inc(o_kept.sem, o_kept.unit)
                    else:
                        dve.wait_ge(o_kept.sem, o_kept.done(t, 1))
                        dve.tensor_tensor(kept, kept, o0, ALU.add).then_inc(o_kept.sem, o_kept.unit)
                    dve.wait_ge(out_summed.sem, out_summed.done(t, 2 * d + 2))
                    if d == 0:
                        dve.wait_ge(rec_stored.sem, rec_stored.done(t, 0))
                    dve.tensor_tensor(rec[:, d, 0:512].rearrange("p (c n) -> p c n", n=P), bank[:, 2], kr[:, d, :, 1, :], ALU.add).then_inc(out_dve.sem, out_dve.unit)
                    dve.wait_ge(out_act.sem, out_act.done(t, d + 1))
                    dve.tensor_tensor(rec[:, d, 512:768].rearrange("p (c n) -> p c n", n=64),
                                                 bank[:, 3, 0:2].rearrange("p c (x n) -> p (c x) n", n=64),
                                                 head_ident[:].unsqueeze(1).to_broadcast([P, RCH, 64]), ALU.add).then_inc(out_dve.sem, out_dve.unit)

                    if d == 0 and ahead:
                        read_prepared(t + 1)

            read_prepared(0)
            scan(0)
            invert(0)
            copy_bonus(0)
            with dve.Fori(0, NT // 2 - 1) as i:
                for s in range(2):
                    tile(i * 2 + s, s)
            tile(NT - 2, 0)
            tile(NT - 1, 1, False)

        @block.gpsimd
        def _(pool):
            pool.memset(seg[:], 1.0).then_inc(masks_ready.sem, masks_ready.unit)
            pool.wait_ge(masks_ready.sem, masks_ready.done(0, 1))
            pool.memset(seg[:, :, 0:1], 0.0)
            pool.memset(factors[:, 0:1], HALF_DECAY).then_inc(masks_ready.sem, masks_ready.unit)
            pool.memset(factors[:, 1:2], -1.0).then_inc(masks_ready.sem, masks_ready.unit)
            pool.memset(lw[:], 0.0).then_inc(masks_ready.sem, masks_ready.unit)
            pool.wait_ge(masks_ready.sem, masks_ready.done())

            def start_solvers(t, d):
                for n in range(2):
                    pool.wait_ge(cross_kept.sem, cross_kept.done(t, 8 * d + 7 + n))
                    solvers[n].start_t(pool, t * 2 + d, env.ident, levels[1 - d])

            def factor(n, tiles, width):
                return spread(factors[:, n:n + 1].to_broadcast([P, tiles]), width)

            def prepare(t, s, solving=True):
                pool.wait_ge(cols_in.sem, cols_in.done(t))
                pool.tensor_tensor(kk[:], k, per_channel(V_KK), ALU.mult).then_inc(kk_steps.sem, kk_steps.unit)
                pool.wait_ge(kk_steps.sem, kk_steps.done(t, 1))
                pool.tensor_tensor(sq[:], kk[:], kk[:], ALU.mult).then_inc(kk_steps.sem, kk_steps.unit)
                if solving:
                    start_solvers(t - 1, 1)
                pool.wait_ge(sigmoided.sem, sigmoided.done(t, 1))
                pool.tensor_tensor(lw[:, :, 1:P + 1], pre[:, 0:8], factor(0, 8, P), ALU.mult).then_inc(log_decay.sem, log_decay.unit)
                pool.wait_ge(sigmoided.sem, sigmoided.done(t, 2))
                pool.tensor_tensor(kp[:], pre[:, 8:12], per_channel(V_KA), ALU.mult).then_inc(kp_steps.sem, kp_steps.unit)
                pool.wait_ge(kp_steps.sem, kp_steps.done(t, 1))
                pool.tensor_tensor(kp[:], kp[:], spread(env.ka_rest[:], P), ALU.add).then_inc(kp_steps.sem, kp_steps.unit)
                pool.wait_ge(kp_steps.sem, kp_steps.done(t, 2))
                pool.tensor_tensor(kp[:], kp[:], k, ALU.mult).then_inc(kp_steps.sem, kp_steps.unit)
                pool.wait_ge(kp_steps.sem, kp_steps.done(t, 3))
                pool.wait_ge(scanned.sem, scanned.done(t))
                pool.tensor_tensor(en[:], cum[:], cum[:, :, 64:65].to_broadcast([P, 8, P + 1]), ALU.subtract).then_inc(centred.sem, centred.unit)
                pool.wait_ge(bonus_summed.sem, bonus_summed.done(t, 0))
                pool.tensor_tensor(bon[:], kp[:], r, ALU.mult).then_inc(bonus_steps.sem, bonus_steps.unit)
                pool.wait_ge(bonus_steps.sem, bonus_steps.done(t, 1))
                pool.tensor_tensor(bon[:], bon[:], per_channel(V_RK), ALU.mult).then_inc(bonus_steps.sem, bonus_steps.unit)
                pool.wait_ge(kk_norm.sem, kk_norm.done(t))
                pool.tensor_tensor(kk[:], kk[:], inv[:], ALU.mult).then_inc(b_steps.sem, b_steps.unit)
                pool.wait_ge(b_steps.sem, b_steps.done(t, 1))
                pool.tensor_tensor(nb[:], kk[:], pre[:, 8:12], ALU.mult).then_inc(b_steps.sem, b_steps.unit)
                pool.wait_ge(b_steps.sem, b_steps.done(t, 2))
                pool.tensor_tensor(nb[:], nb[:], factor(1, RCH, P), ALU.mult).then_inc(b_steps.sem, b_steps.unit)
                kr, bt, kt = kr2[s], bt2[s], kt2[s]
                pool.wait_ge(decayed.sem, decayed.done(t))
                pool.tensor_tensor(kr[:, 0, :, 1, :], r, ep[:, 0:4, 1:P + 1], ALU.mult).then_inc(prods.sem, prods.unit)
                pool.tensor_tensor(kr[:, 1, :, 1, :], r, en[:, 4:8, 0:P], ALU.mult).then_inc(prods.sem, prods.unit)
                pool.tensor_tensor(kt[:, 0], kp[:], en[:, 0:4, 1:P + 1], ALU.mult).then_inc(prods.sem, prods.unit)
                pool.tensor_tensor(kt[:, 1], kp[:], ep[:, 4:8, 0:P], ALU.mult).then_inc(prods.sem, prods.unit)
                pool.tensor_tensor(kr[:, 0, :, 0, :], kk[:], ep[:, 0:4, 0:P], ALU.mult).then_inc(prods.sem, prods.unit)
                pool.tensor_tensor(kr[:, 1, :, 0, :], kk[:], en[:, 4:8, 1:P + 1], ALU.mult).then_inc(prods.sem, prods.unit)
                pool.wait_ge(b_steps.sem, b_steps.done(t, 3))
                pool.tensor_tensor(bt[:, 0], nb[:], en[:, 0:4, 1:P + 1], ALU.mult).then_inc(prods.sem, prods.unit)
                pool.tensor_tensor(bt[:, 1], nb[:], ep[:, 4:8, 0:P], ALU.mult).then_inc(prods.sem, prods.unit)
                pool.wait_ge(prods.sem, prods.done(t))
                pool.wait_ge(bonus_copied.sem, bonus_copied.done(t))
                pool.wait_ge(v_ready.sem, v_ready.done(t))
                pool.wait_ge(side_stored.sem, side_stored.done(t, 0))
                pool.tensor_tensor(side[:, 0].rearrange("p (h n) -> p h n", n=64), v2[s][:], spread(bonus[:], 64),
                                   ALU.mult).then_inc(bonus_ready.sem, bonus_ready.unit)
                pool.wait_ge(bonus_ready.sem, bonus_ready.done(t))

            prepare(0, 0, False)
            with pool.Fori(0, NT // 2 - 1) as i:
                for s in range(2):
                    start_solvers(i * 2 + s, 0)
                    prepare(i * 2 + s + 1, 1 - s)
            start_solvers(NT - 2, 0)
            prepare(NT - 1, 1)
            start_solvers(NT - 1, 0)
            start_solvers(NT - 1, 1)


def recur(env):
    nc, io = env.nc, env.io
    E = env.event
    loaded = [E(f"rc_loaded{s}", per=4, dma=True) for s in range(2)]
    cleared = E("rc_cleared", per=2)
    scaled = E("rc_scaled", per=2)
    dn_summed = E("rc_dn_summed", per=2)
    rw_summed = E("rc_rw_summed", per=2)
    dn_o_added = E("rc_dn_o_added", per=2)
    dn_state = E("rc_dn_state", per=2)
    rw_o_added = E("rc_rw_o_added", per=2)
    rw_mid = E("rc_rw_mid", per=4)
    rw_state = E("rc_rw_state", per=2)
    DNR, RWR = 3 * DNW, 1032
    with ExitStack() as ctx:
        sb, pb = tools(nc, ctx)
        bank = pb("rc_banks", [P, 8, 512])
        dn_rec = sb("rc_dn_rec", [P, 2, 2, 3, DNH, P])
        rw_rec = sb("rc_rw_rec", [P, 2, 2, RWR])
        dn_s = sb("rc_dn_s", [P, 2, DNH, P])
        rw_s = sb("rc_rw_s", [P, 2, RCH, 64])
        block = ctx.enter_context(nc.Block())

        def steps(eng, body, before=None):
            done = 0
            for g, (t0, n) in enumerate(SEQS):
                if before:
                    before(g, done)
                with eng.Fori(0, n // 2) as i:
                    for s in range(2):
                        step = i * 2 + s
                        body(s, g, (t0 + step, t0 + n - 1 - step), done + step, done // 2 + i)
                done += n

        @block.sync
        def _(sp):
            def load(s, tiles, slot_turn):
                for d in range(2):
                    r = tiles[d] * 2 + d
                    sp.dma_start(dn_rec[:, s, d].rearrange("p x c n -> p (x c n)"),
                                              io["dn_rec"][ds(r, 1)].rearrange("a p x -> p (a x)")).then_inc(loaded[s].sem, loaded[s].unit)
                    sp.dma_start(rw_rec[:, s, d], io["rw_rec"][ds(r, 1)].rearrange("a p x -> p (a x)")).then_inc(loaded[s].sem, loaded[s].unit)
            done = 0
            for g, (t0, n) in enumerate(SEQS):
                if g == 0:
                    for s in range(2):
                        load(s, (t0 + s, t0 + n - 1 - s), 0)
                with sp.Fori(1 if g == 0 else 0, n // 2) as i:
                    for s in range(2):
                        sp.wait_ge(dn_state.sem, dn_state.done(done - 2 + i * 2 + s))
                        sp.wait_ge(rw_state.sem, rw_state.done(done - 2 + i * 2 + s))
                        load(s, (t0 + i * 2 + s, t0 + n - 1 - s - i * 2), 0)
                done += n

        @block.tensor
        def _(pe):
            def body(s, g, tiles, turn, slot_turn):
                pe.wait_ge(loaded[s].sem, loaded[s].done(slot_turn))
                for d in range(2):
                    rec = dn_rec[:, s, d]
                    for h in range(DNH):
                        pe.matmul(bank[:, 2 * d, h * P:(h + 1) * P], rec[:, 0, h, :], dn_s[:, d, h, :], start=True, stop=True)
                        mm = pe.matmul(bank[:, 2 * d + 1, h * P:(h + 1) * P], rec[:, 1, h, :], dn_s[:, d, h, :], start=True, stop=True)
                    mm.then_inc(dn_summed.sem, dn_summed.unit)
                pe.wait_ge(scaled.sem, scaled.done(turn))
                for d in range(2):
                    for h in range(RWH):
                        rows, c = slice(64 * (h % 2), 64 * (h % 2) + 64), h // 2
                        b = 4 + 2 * d + h % 2
                        state = rw_s[rows, d, c, :]
                        pe.matmul(bank[:, b, c * 64:c * 64 + 64], rw_rec[rows, s, d, c * P:(c + 1) * P], state, start=True, stop=True)
                        mm = pe.matmul(bank[rows, b, 256 + c * 64:320 + c * 64], rw_rec[rows, s, d, 512 + c * 64:576 + c * 64], state,
                                       start=True, stop=True)
                    mm.then_inc(rw_summed.sem, rw_summed.unit)
                pe.wait_ge(dn_o_added.sem, dn_o_added.done(turn))
                pe.wait_ge(dn_state.sem, dn_state.done(turn))

            steps(pe, body, lambda g, done: pe.wait_ge(cleared.sem, cleared.done(g)))

        @block.vector
        def _(dve):
            def clear(g, done):
                dve.memset(dn_s[:], 0.0).then_inc(cleared.sem, cleared.unit)
                dve.memset(rw_s[:], 0.0).then_inc(cleared.sem, cleared.unit)
                dve.wait_ge(cleared.sem, cleared.done(g))

            def body(s, g, tiles, turn, slot_turn):
                dve.wait_ge(loaded[s].sem, loaded[s].done(slot_turn))
                for d in range(2):
                    before = rw_rec[:, s, d, 1024:1028]
                    dve.tensor_tensor(rw_s[:, d], rw_s[:, d], spread(before, 64), ALU.mult).then_inc(scaled.sem, scaled.unit)
                for d in range(2):
                    dve.wait_ge(dn_summed.sem, dn_summed.done(turn, d + 1))
                    o = env.dn_o[:, ds(tiles[d], 1), :].rearrange("p a n -> p (a n)")
                    dve.tensor_tensor(dn_s[:, d].rearrange("p c n -> p (c n)"), bank[:, 2 * d + 1],
                                                  dn_rec[:, s, d, 2].rearrange("p c n -> p (c n)"), ALU.add).then_inc(dn_state.sem, dn_state.unit)
                    dve.tensor_tensor(o, o, bank[:, 2 * d], ALU.add).then_inc(dn_o_added.sem, dn_o_added.unit)
                for d in range(2):
                    dve.wait_ge(rw_summed.sem, rw_summed.done(turn, d + 1))
                    for x in range(2):
                        rows, b = slice(64 * x, 64 * x + 64), 4 + 2 * d + x
                        dve.tensor_tensor(rw_s[rows, d], bank[rows, b, 256:512].rearrange("p (c n) -> p c n", n=64),
                                                    rw_rec[rows, s, d, 768:1024].rearrange("p (c n) -> p c n", n=64), ALU.add).then_inc(rw_mid.sem, rw_mid.unit)
                    dve.wait_ge(rw_mid.sem, rw_mid.done(turn, 2 * d + 2))
                    dve.tensor_tensor(rw_s[:, d], rw_s[:, d], spread(rw_rec[:, s, d, 1028:1032], 64), ALU.mult).then_inc(rw_state.sem, rw_state.unit)
                    o = env.rw_o[:, ds(tiles[d], 1), :].rearrange("p a (c x n) -> p x (a c) n", c=RCH, x=2)
                    dve.tensor_tensor(o, o, bank[:, 4 + 2 * d:6 + 2 * d, 0:256].rearrange("p x (c n) -> p x c n", n=64),
                                                    ALU.add).then_inc(rw_o_added.sem, rw_o_added.unit)
                dve.wait_ge(dn_o_added.sem, dn_o_added.done(turn))
                dve.wait_ge(dn_state.sem, dn_state.done(turn))
                dve.wait_ge(rw_o_added.sem, rw_o_added.done(turn))
                dve.wait_ge(rw_state.sem, rw_state.done(turn))

            steps(dve, body, clear)


def head_out(env):
    nc, io = env.nc, env.io
    E = env.event
    rows_in = E("ho_rows_loaded", per=3, dma=True)
    z_in = E("ho_z_loaded", dma=True)
    side_in = E("ho_side_loaded", dma=True)
    z_turned = E("ho_z_turned")
    squared = E("ho_squared", per=2)
    rooted = E("ho_rooted", per=2)
    z_copied = E("ho_z_copied")
    dn_steps = E("ho_dn_steps", per=3)
    dn_products = E("ho_dn_products", per=3)
    rw_steps = E("ho_rw_steps", per=11)
    y_turned = E("ho_y_turned", per=2)
    y_copied = E("ho_y_copied", per=2)
    y_stored = E("ho_y_stored", dma=True)
    with ExitStack() as ctx:
        sb, pb = tools(nc, ctx)
        bank = pb("ho_banks", [P, 3, 4, P])
        norm_w = sb("ho_norm_w", [P, P])
        ln_w = sb("ho_ln_w", [P, RWW])
        ln_b = sb("ho_ln_b", [P, RWW])
        zT = sb("ho_zT", [P, 4, P])
        z = sb("ho_z", [P, 4, P])
        side = sb("ho_side", [P, 2, RWW])
        sq = sb("ho_sq", [P, 2, RWW])
        st = sb("ho_st", [P, 2, 8])
        mean = sb("ho_mean", [P, 8])
        y = sb("ho_y", [P, 2, RWW])
        yT = sb("ho_yT", [P, 8, P])
        block = ctx.enter_context(nc.Block())

        @block.sync
        def _(sp):
            sp.dma_start(norm_w[:], io["dn_norm_w"].to_broadcast([P, P])).then_inc(rows_in.sem, rows_in.unit)
            sp.dma_start(ln_w[:], io["rw_ln_w"].to_broadcast([P, RWW])).then_inc(rows_in.sem, rows_in.unit)
            sp.dma_start(ln_b[:], io["rw_ln_b"].to_broadcast([P, RWW])).then_inc(rows_in.sem, rows_in.unit)

            def load(t):
                sp.dma_start(zT[:], io["ch"][Z0:AB0, ds(t * P, P)].rearrange("(c p) t -> p c t", p=P)).then_inc(z_in.sem, z_in.unit)
                sp.dma_start(side[:].rearrange("p x n -> p (x n)"), io["rw_side"][ds(t, 1)].rearrange("a p x -> p (a x)")).then_inc(side_in.sem, side_in.unit)
            load(0)
            with sp.Fori(1, NT) as t:
                sp.wait_ge(z_turned.sem, z_turned.done(t - 1))
                sp.wait_ge(rw_steps.sem, rw_steps.done(t - 1))
                load(t)

        @block.tensor
        def _(pe):
            with pe.Fori(0, NT) as t:
                pe.wait_ge(z_in.sem, z_in.done(t))
                for c in range(4):
                    tr = pe.transpose(bank[:, 0, c, :], zT[:, c, :], env.ident[:])
                tr.then_inc(z_turned.sem, z_turned.unit)
                for b, steps in ((0, dn_products), (1, rw_steps)):
                    pe.wait_ge(steps.sem, steps.done(t))
                    for c in range(4):
                        tr = pe.transpose(bank[:, 1 + b, c, :], y[:, b, c * P:(c + 1) * P], env.ident[:])
                    tr.then_inc(y_turned.sem, y_turned.unit)
                pe.wait_ge(z_copied.sem, z_copied.done(t))
                pe.wait_ge(y_copied.sem, y_copied.done(t))

        @block.scalar
        def _(act):
            with act.Fori(0, NT) as t:
                o = env.dn_o[:, ds(t, 1), :].rearrange("p a n -> p (a n)")
                act.activation(sq[:, 0], o, ACT.Square).then_inc(squared.sem, squared.unit)
                act.wait_ge(z_turned.sem, z_turned.done(t))
                act.wait_ge(dn_products.sem, dn_products.done(t, 0))
                act.activation(z[:], bank[:, 0], ACT.Identity).then_inc(z_copied.sem, z_copied.unit)
                act.wait_ge(rw_steps.sem, rw_steps.done(t, 3))
                act.activation(sq[:, 1], y[:, 1], ACT.Square).then_inc(squared.sem, squared.unit)
                act.wait_ge(dn_steps.sem, dn_steps.done(t, 2))
                act.activation(st[:, 0, 0:4], st[:, 0, 0:4], ACT.Sqrt).then_inc(rooted.sem, rooted.unit)
                act.wait_ge(rw_steps.sem, rw_steps.done(t, 5))
                act.activation(st[:, 1], st[:, 1], ACT.Sqrt).then_inc(rooted.sem, rooted.unit)
                act.wait_ge(y_stored.sem, y_stored.done(t, 0))
                for b in range(2):
                    act.wait_ge(y_turned.sem, y_turned.done(t, b + 1))
                    act.activation(yT[:, 4 * b:4 * b + 4], bank[:, 1 + b], ACT.Identity).then_inc(y_copied.sem, y_copied.unit)
                act.wait_ge(y_copied.sem, y_copied.done(t))
                act.dma_start(io["yT"][:, ds(t * P, P)].rearrange("(c p) t -> p c t", p=P), yT[:]).then_inc(y_stored.sem, y_stored.unit)
            act.wait_ge(y_stored.sem, y_stored.done(NT - 1))

        @block.vector
        def _(dve):
            dve.wait_ge(rows_in.sem, rows_in.done())
            with dve.Fori(0, NT) as t:
                o = env.rw_o[:, ds(t, 1), :].rearrange("p a (h n) -> p (a h) n", n=64)
                yr = y[:, 1].rearrange("p (h n) -> p h n", n=64)
                dve.tensor_reduce(mean[:], o, AX, ALU.add).then_inc(rw_steps.sem, rw_steps.unit)
                dve.wait_ge(rw_steps.sem, rw_steps.done(t, 1))
                dve.tensor_scalar(mean[:], mean[:], 1.0 / 64, None, ALU.mult).then_inc(rw_steps.sem, rw_steps.unit)
                dve.wait_ge(rw_steps.sem, rw_steps.done(t, 2))
                dve.wait_ge(y_turned.sem, y_turned.done(t, 0))
                dve.tensor_tensor(yr, o, spread(mean[:], 64), ALU.subtract).then_inc(rw_steps.sem, rw_steps.unit)
                dve.wait_ge(rw_steps.sem, rw_steps.done(t, 3))
                dve.wait_ge(squared.sem, squared.done(t, 1))
                dve.tensor_reduce(st[:, 0, 0:4], sq[:, 0].rearrange("p (h n) -> p h n", n=P), AX, ALU.add).then_inc(dn_steps.sem, dn_steps.unit)
                dve.wait_ge(dn_steps.sem, dn_steps.done(t, 1))
                dve.tensor_scalar(st[:, 0, 0:4], st[:, 0, 0:4], 1.0 / P, 1e-6, ALU.mult, ALU.add).then_inc(dn_steps.sem, dn_steps.unit)
                dve.wait_ge(dn_steps.sem, dn_steps.done(t, 2))
                dve.wait_ge(squared.sem, squared.done(t, 2))
                dve.tensor_reduce(st[:, 1], sq[:, 1].rearrange("p (h n) -> p h n", n=64), AX, ALU.add).then_inc(rw_steps.sem, rw_steps.unit)
                dve.wait_ge(rw_steps.sem, rw_steps.done(t, 4))
                dve.tensor_scalar(st[:, 1], st[:, 1], 1.0 / 64, 64e-5, ALU.mult, ALU.add).then_inc(rw_steps.sem, rw_steps.unit)
                dve.wait_ge(rw_steps.sem, rw_steps.done(t, 5))
                dve.wait_ge(rooted.sem, rooted.done(t, 1))
                dve.reciprocal(st[:, 0, 0:4], st[:, 0, 0:4]).then_inc(dn_steps.sem, dn_steps.unit)
                dve.wait_ge(dn_steps.sem, dn_steps.done(t, 3))
                dve.wait_ge(rooted.sem, rooted.done(t, 2))
                dve.reciprocal(st[:, 1], st[:, 1]).then_inc(rw_steps.sem, rw_steps.unit)
                dve.wait_ge(rw_steps.sem, rw_steps.done(t, 6))
                dve.tensor_tensor(yr, yr, spread(st[:, 1], 64), ALU.mult).then_inc(rw_steps.sem, rw_steps.unit)
                dve.wait_ge(rw_steps.sem, rw_steps.done(t, 7))
                dve.tensor_tensor(y[:, 1], y[:, 1], ln_w[:], ALU.mult).then_inc(rw_steps.sem, rw_steps.unit)
                dve.wait_ge(rw_steps.sem, rw_steps.done(t, 8))
                dve.tensor_tensor(y[:, 1], y[:, 1], ln_b[:], ALU.add).then_inc(rw_steps.sem, rw_steps.unit)
                dve.wait_ge(rw_steps.sem, rw_steps.done(t, 9))
                dve.wait_ge(side_in.sem, side_in.done(t))
                dve.tensor_tensor(y[:, 1], y[:, 1], side[:, 0], ALU.add).then_inc(rw_steps.sem, rw_steps.unit)
                dve.wait_ge(rw_steps.sem, rw_steps.done(t, 10))
                dve.tensor_tensor(y[:, 1], y[:, 1], side[:, 1], ALU.mult).then_inc(rw_steps.sem, rw_steps.unit)
                dve.wait_ge(rw_steps.sem, rw_steps.done(t, 11))

        @block.gpsimd
        def _(pool):
            with pool.Fori(0, NT) as t:
                pool.wait_ge(rows_in.sem, rows_in.done())
                yd = y[:, 0].rearrange("p (h n) -> p h n", n=P)
                od = env.dn_o[:, ds(t, 1), :].rearrange("p a (h n) -> p (a h) n", n=P)
                pool.wait_ge(y_turned.sem, y_turned.done(t, 0))
                pool.wait_ge(dn_steps.sem, dn_steps.done(t, 3))
                pool.tensor_tensor(yd, od, spread(st[:, 0, 0:4], P), ALU.mult).then_inc(dn_products.sem, dn_products.unit)
                pool.wait_ge(dn_products.sem, dn_products.done(t, 1))
                pool.tensor_tensor(yd, yd, norm_w[:].unsqueeze(1).to_broadcast([P, 4, P]), ALU.mult).then_inc(dn_products.sem, dn_products.unit)
                pool.wait_ge(dn_products.sem, dn_products.done(t, 2))
                pool.wait_ge(z_copied.sem, z_copied.done(t))
                pool.tensor_tensor(yd, yd, z[:], ALU.mult).then_inc(dn_products.sem, dn_products.unit)


def mix_out(env):
    nc, io = env.nc, env.io
    E = env.event
    w_in = [E(f"mx_w_loaded{x}", per=2, dma=True) for x in range(2)]
    y_in = [E(f"mx_y_loaded{b}", dma=True) for b in range(NB)]
    gate_in = [E(f"mx_gate_loaded{s}", per=2, dma=True) for s in range(2)]
    br_summed = E("mx_br_summed", per=NB)
    br_steps = E("mx_br_steps", per=2 * NB)
    merged_ready = E("mx_merged_ready", per=NB)
    NC8 = D // P
    with ExitStack() as ctx:
        sb, pb = tools(nc, ctx)
        merged = sb("mx_merged", [P, NC8, TOK])
        w_out = sb("mx_w_out", [P, KD, D])
        w_out_in = E("mx_w_out_loaded", dma=True)
        with ExitStack() as inner:
            sb, pb = tools(nc, inner)
            wb = sb("mx_wb", [P, 2, 4, D])
            yT = sb("mx_yT", [P, 8, TOK])
            gate = sb("mx_gate", [P, 2, 2, TOK])
            bank = pb("mx_banks", [P, 2, NB, BLK])
            block = inner.enter_context(nc.Block())

            @block.sync
            def _(sp):
                def load_y(b):
                    cols = slice(b * BLK, (b + 1) * BLK)
                    sp.dma_start(yT[:, :, cols], io["yT"][:, cols].rearrange("(k p) t -> p k t", p=P)).then_inc(y_in[b].sem, y_in[b].unit)

                def load_w(x):
                    cols = slice(x * D // 2, (x + 1) * D // 2)
                    for br, name in enumerate(("w_br_dn", "w_br_rw")):
                        sp.dma_start(wb[:, br, :, cols], io[name][0][:, cols].rearrange("(k p) n -> p k n", p=P)).then_inc(w_in[x].sem, w_in[x].unit)
                load_y(0)
                load_w(0)
                load_y(1)
                load_y(2)

                def load(s, n):
                    for b in range(2):
                        sp.dma_start(gate[:, s, b], io["ch"][ds(G0 + b * D + n * P, P), :]).then_inc(gate_in[s].sem, gate_in[s].unit)
                load(0, 0)
                load_w(1)
                load(1, 1)
                sp.dma_start(w_out[:], io["w_out"][0].rearrange("(k p) n -> p k n", p=P)).then_inc(w_out_in.sem, w_out_in.unit)
                for n in range(2, NC8):
                    sp.wait_ge(merged_ready.sem, merged_ready.done(n - 2))
                    load(n % 2, n)

            @block.tensor
            def _(pe):
                for n in range(NC8):
                    if n % (NC8 // 2) == 0:
                        pe.wait_ge(w_in[n // (NC8 // 2)].sem, w_in[0].done())
                    for b in range(NB):
                        if n == 0:
                            pe.wait_ge(y_in[b].sem, y_in[b].done())
                        if n:
                            pe.wait_ge(br_steps.sem, br_steps.done(n - 1, 2 * b + 2))
                        for br in range(2):
                            for k in range(4):
                                mm = pe.matmul(bank[:, br, b, :], wb[:, br, k, n * P:(n + 1) * P],
                                               yT[:, 4 * br + k, b * BLK:(b + 1) * BLK], start=(k == 0), stop=(k == 3))
                        mm.then_inc(br_summed.sem, br_summed.unit)

            @block.vector
            def _(dve):
                for n in range(NC8):
                    dve.wait_ge(gate_in[n % 2].sem, gate_in[n % 2].done(n // 2))
                    for b in range(NB):
                        dve.wait_ge(br_summed.sem, br_summed.done(n, b + 1))
                        for br in range(2):
                            g = gate[:, n % 2, br, b * BLK:(b + 1) * BLK]
                            dve.tensor_tensor(g, bank[:, br, b, :], g, ALU.mult).then_inc(br_steps.sem, br_steps.unit)
                        dve.wait_ge(br_steps.sem, br_steps.done(n, 2 * b + 2))
                        cols = slice(b * BLK, (b + 1) * BLK)
                        dve.tensor_tensor(merged[:, n, cols], gate[:, n % 2, 0, cols], gate[:, n % 2, 1, cols], ALU.add).then_inc(merged_ready.sem, merged_ready.unit)

        second_norm(env, ctx, merged, w_out, w_out_in)


def second_norm(env, ctx, merged, w_out, w_out_in):
    nc, io = env.nc, env.io
    E = env.event
    rows_in = E("sn_rows_loaded", per=7, dma=True)
    router_in = E("sn_router_loaded", per=2, dma=True)
    gain_ready = E("sn_gain_ready", per=2)
    x_in = [E(f"sn_x_loaded{s}", dma=True) for s in range(2)]
    taken = E("sn_taken")
    mixed = E("sn_mixed", per=2)
    res_steps = E("sn_res_steps", per=4)
    squared = E("sn_squared")
    meaned = E("sn_meaned")
    rooted = E("sn_rooted")
    h_steps = E("sn_h_steps", per=4)
    h_turned = E("sn_h_turned", per=2)
    h_copied = E("sn_h_copied", per=2)
    routed = E("sn_routed")
    logits_kept = E("sn_logits_kept")
    x1_stored = E("sn_x1_stored", dma=True)
    h2_stored = E("sn_h2_stored", dma=True)
    with ExitStack() as inner:
        sb, pb = tools(nc, inner)
        gate1 = sb("sn_gate1", [P, 2, D])
        shift = sb("sn_shift", [P, 2, D])
        gain = sb("sn_gain", [P, 2, D])
        norm2 = sb("sn_norm2", [P, D])
        router = sb("sn_router", [P, KD, NG + NE])
        x = [sb(f"sn_x{s}", [P, D]) for s in range(2)]
        mT = [sb(f"sn_mT{s}", [P, KD, P]) for s in range(2)]
        x1 = sb("sn_res", [P, D])
        h2 = sb("sn_h2", [P, D])
        h2T = sb("sn_h2T", [P, KD, P])
        sq = sb("sn_sq", [P, D])
        ss = sb("sn_ss", [P, 4])
        mix = [pb(f"sn_mix{s}", [P, 2, BLK]) for s in range(2)]
        turned = pb("sn_turned", [P, 2, 4, P])
        log = pb("sn_log", [P, NG + NE])
        block = inner.enter_context(nc.Block())
        part = io["ada_rows"].rearrange("g (s n) -> s g n", s=6)

        @block.sync
        def _(sp):
            for g in range(2):
                for dst, which in ((gate1, 2), (shift, 3), (gain, 4)):
                    sp.dma_start(dst[:, g], part[which, g:g + 1].to_broadcast([P, D])).then_inc(rows_in.sem, rows_in.unit)
            sp.dma_start(norm2[:], io["norm2"].to_broadcast([P, D])).then_inc(rows_in.sem, rows_in.unit)
            sp.dma_start(router[:, :, 0:NG], io["moe_w_group"][0].rearrange("(k p) e -> p k e", p=P)).then_inc(router_in.sem, router_in.unit)
            sp.dma_start(router[:, :, NG:], io["moe_w_expert"][0].rearrange("(k p) e -> p k e", p=P)).then_inc(router_in.sem, router_in.unit)
            for s in range(2):
                sp.dma_start(x[s][:], io["x_prompt"][0, s * P:(s + 1) * P, :]).then_inc(x_in[s].sem, x_in[s].unit)

            def store(t):
                sp.wait_ge(res_steps.sem, res_steps.done(t))
                sp.dma_start(io["x1"][ds(t * P, P), :], x1[:]).then_inc(x1_stored.sem, x1_stored.unit)
                sp.wait_ge(h_steps.sem, h_steps.done(t))
                sp.dma_start(io["h2"][ds(t * P, P), :], h2[:]).then_inc(h2_stored.sem, h2_stored.unit)

            for g, (t0, n) in enumerate(SEQS):
                src = io["x_prompt"][0] if g == 0 else io["x_sample"][0]
                with sp.Fori(1 if g == 0 else 0, n // 2) as i:
                    for s in range(2):
                        sp.wait_ge(res_steps.sem, res_steps.done(t0 + i * 2 + s - 2))
                        sp.dma_start(x[s][:], src[ds((i * 2 + s) * P, P), :]).then_inc(x_in[s].sem, x_in[s].unit)
                        store(t0 + i * 2 + s - 2)
            store(NT - 2)
            store(NT - 1)
            sp.wait_ge(x1_stored.sem, x1_stored.done(NT - 1))
            sp.wait_ge(h2_stored.sem, h2_stored.done(NT - 1))

        @block.tensor
        def _(pe):
            pe.wait_ge(router_in.sem, router_in.done())
            pe.wait_ge(w_out_in.sem, w_out_in.done())

            def mix_tile(t, s):
                pe.wait_ge(taken.sem, taken.done(t))
                if not isinstance(t, int):
                    pe.wait_ge(h_steps.sem, h_steps.done(t - 1, 0))
                for half in range(2):
                    for k in range(KD):
                        mm = pe.matmul(mix[s][:, half, :], mT[s][:, k, :], w_out[:, k, half * BLK:(half + 1) * BLK],
                                       start=(k == 0), stop=(k == KD - 1))
                    mm.then_inc(mixed.sem, mixed.unit)

            def logits_tile(t):
                pe.wait_ge(h_steps.sem, h_steps.done(t))
                for half in range(2):
                    for k in range(4):
                        tr = pe.transpose(turned[:, half, k, :], h2[:, (4 * half + k) * P:(4 * half + k + 1) * P], env.ident[:])
                    tr.then_inc(h_turned.sem, h_turned.unit)
                pe.wait_ge(h_copied.sem, h_copied.done(t))
                pe.wait_ge(logits_kept.sem, logits_kept.done(t, 0))
                for k in range(KD):
                    mm = pe.matmul(log[:], h2T[:, k, :], router[:, k, :], start=(k == 0), stop=(k == KD - 1))
                mm.then_inc(routed.sem, routed.unit)

            mix_tile(0, 0)
            with pe.Fori(0, NT // 2 - 1) as i:
                for s in range(2):
                    mix_tile(i * 2 + s + 1, 1 - s)
                    logits_tile(i * 2 + s)
            mix_tile(NT - 1, 1)
            logits_tile(NT - 2)
            logits_tile(NT - 1)

        @block.scalar
        def _(act):
            def take(t, s):
                act.wait_ge(mixed.sem, mixed.done(t - 1, 0))
                act.activation(mT[s][:], merged[:, :, ds(t * P, P)], ACT.Identity).then_inc(taken.sem, taken.unit)

            def norm(t):
                act.wait_ge(res_steps.sem, res_steps.done(t))
                act.activation(sq[:], x1[:], ACT.Square, accum_out=ss[:, 0:1]).then_inc(squared.sem, squared.unit)
                act.wait_ge(meaned.sem, meaned.done(t))
                act.activation(ss[:, 2:3], ss[:, 1:2], ACT.Sqrt).then_inc(rooted.sem, rooted.unit)
                for half in range(2):
                    act.wait_ge(h_turned.sem, h_turned.done(t, half + 1))
                    if half == 0:
                        act.wait_ge(routed.sem, routed.done(t, 0))
                    act.activation(h2T[:, 4 * half:4 * half + 4], turned[:, half], ACT.Identity).then_inc(h_copied.sem, h_copied.unit)

            act.activation(mT[0][:], merged[:, :, 0:P], ACT.Identity).then_inc(taken.sem, taken.unit)
            act.activation(mT[1][:], merged[:, :, P:2 * P], ACT.Identity).then_inc(taken.sem, taken.unit)
            norm(0)
            with act.Fori(1, NT // 2) as i:
                for s in range(2):
                    take(i * 2 + s, s)
                    norm(i * 2 + s - 1)
            norm(NT - 1)

        @block.vector
        def _(dve):
            dve.wait_ge(rows_in.sem, rows_in.done())
            dve.tensor_scalar(gain[:], gain[:], 1.0, None, ALU.add).then_inc(gain_ready.sem, gain_ready.unit)
            dve.wait_ge(gain_ready.sem, gain_ready.done(0, 1))
            dve.tensor_tensor(gain[:], gain[:], norm2[:].unsqueeze(1).to_broadcast([P, 2, D]), ALU.mult).then_inc(gain_ready.sem, gain_ready.unit)
            dve.wait_ge(gain_ready.sem, gain_ready.done(0, 2))
            for g, (t0, n) in enumerate(SEQS):
                with dve.Fori(0, n // 2) as i:
                    for s in range(2):
                        t = t0 + i * 2 + s
                        dve.wait_ge(x_in[s].sem, x_in[s].done(t0 // 2 + i))
                        dve.wait_ge(x1_stored.sem, x1_stored.done(t, 0))
                        for half in range(2):
                            cols = slice(half * BLK, (half + 1) * BLK)
                            dve.wait_ge(mixed.sem, mixed.done(t, half + 1))
                            dve.tensor_tensor(x1[:, cols], mix[s][:, half], gate1[:, g, cols], ALU.mult).then_inc(res_steps.sem, res_steps.unit)
                        dve.wait_ge(res_steps.sem, res_steps.done(t, 2))
                        for half in range(2):
                            cols = slice(half * BLK, (half + 1) * BLK)
                            dve.tensor_tensor(x1[:, cols], x1[:, cols], x[s][:, cols], ALU.add).then_inc(res_steps.sem, res_steps.unit)
                        dve.wait_ge(squared.sem, squared.done(t))
                        dve.tensor_scalar(ss[:, 1:2], ss[:, 0:1], 1.0 / D, 1e-6, ALU.mult, ALU.add).then_inc(meaned.sem, meaned.unit)
                        dve.wait_ge(rooted.sem, rooted.done(t))
                        dve.reciprocal(ss[:, 3:4], ss[:, 2:3]).then_inc(h_steps.sem, h_steps.unit)
                        dve.wait_ge(h_steps.sem, h_steps.done(t, 1))
                        dve.wait_ge(h2_stored.sem, h2_stored.done(t, 0))
                        dve.tensor_scalar(h2[:], x1[:], ss[:, 3:4], None, ALU.mult).then_inc(h_steps.sem, h_steps.unit)
                        dve.wait_ge(h_steps.sem, h_steps.done(t, 2))
                        dve.tensor_tensor(h2[:], h2[:], gain[:, g], ALU.mult).then_inc(h_steps.sem, h_steps.unit)
                        dve.wait_ge(h_steps.sem, h_steps.done(t, 3))
                        dve.tensor_tensor(h2[:], h2[:], shift[:, g], ALU.add).then_inc(h_steps.sem, h_steps.unit)
                        dve.wait_ge(routed.sem, routed.done(t))
                        dve.tensor_copy(env.logits[:, ds(t, 1), :].rearrange("p a e -> p (a e)"), log[:]).then_inc(logits_kept.sem, logits_kept.unit)


MORE = TOK // P - 1


def route(env):
    nc, io = env.nc, env.io
    E = env.event
    bias_in = E("rt_bias_loaded", per=2, dma=True)
    pool_steps = E("rt_pool_steps", per=NPG + MORE + 4)
    zeroed = E("rt_zeroed", dma=True)
    dve_steps = E("rt_dve_steps", per=1)
    exp_in = E("rt_exp_in", per=2)
    exp_done = E("rt_exp_done", per=2)
    pairs_ready = E("rt_pairs_ready")
    ranked = E("rt_ranked")
    places_ready = E("rt_places_ready")
    scattered = E("rt_scattered", per=2 * NT, dma=True)
    table_in = E("rt_table_loaded", dma=True)
    with ExitStack() as ctx:
        sb, pb = tools(nc, ctx)
        bias = sb("rt_bias", [P, NG + NE])
        order = sb("rt_order", [P, NPG])
        steps128 = sb("rt_steps128", [P, MORE])
        token = sb("rt_token", [P, NT], I32)
        zero = sb("rt_zero", [P, NBLOCKS + 1], I32)
        lg = sb("rt_lg", [P, NT, NG + NE])
        eq = sb("rt_eq", [P, NT, NPG])
        top = sb("rt_top", [P, NT])
        first = sb("rt_first", [P, NT])
        group = sb("rt_group", [P, NT, NG])
        gprob = sb("rt_gprob", [P, NT])
        gexp = sb("rt_gexp", [P, NT, NG])
        in_group = sb("rt_in_group", [P, NT, NPG])
        pick = [sb(f"rt_pick{k}", [P, NT, NPG]) for k in range(2)]
        tops = [sb(f"rt_tops{k}", [P, NT]) for k in range(2)]
        wide = sb("rt_wide", [P, NT, NG, NPG])
        pair = [sb(f"rt_pair{k}", [P, NT, NG, NPG]) for k in range(2)]
        both = sb("rt_both", [P, NT * NE])
        before = sb("rt_before", [P, NT + 1, NE])
        more = sb("rt_more", [P, NE, MORE])
        blocks = sb("rt_blocks", [P, NE])
        ends = sb("rt_ends", [P, NE + 2])
        start = sb("rt_start", [P, NE])
        place = sb("rt_place", [P, NT, NE])
        placef = sb("rt_placef", [P, 2, NT])
        rank_ps = pb("rt_rank_ps", [P, NT * NE])
        total_ps = pb("rt_total_ps", [P, NT * NE])
        block = ctx.enter_context(nc.Block())

        @block.sync
        def _(sp):
            sp.dma_start(bias[:, 0:NG], io["moe_b_group"].to_broadcast([P, NG])).then_inc(bias_in.sem, bias_in.unit)
            sp.dma_start(bias[:, NG:], io["moe_b_expert"].to_broadcast([P, NE])).then_inc(bias_in.sem, bias_in.unit)
            load_expert(sp, env, 0, 0)
            sp.wait_ge(pool_steps.sem, pool_steps.done(0, 1))
            sp.dma_start(io["slot_tok"].rearrange("(p b) o -> p (b o)", p=P), zero[:]).then_inc(zeroed.sem, zeroed.unit)
            sp.wait_ge(zeroed.sem, zeroed.done())
            sp.wait_ge(scattered.sem, scattered.done())
            sp.dma_start(env.slot_tok[:], io["slot_tok"].rearrange("(b p) o -> p (b o)", p=P), allow_slow_non_contiguous=True).then_inc(table_in.sem, table_in.unit)
            sp.wait_ge(table_in.sem, table_in.done())

        @block.gpsimd
        def _(pool):
            pool.memset(zero[:], 0).then_inc(pool_steps.sem, pool_steps.unit)
            for i in range(NPG):
                pool.memset(order[:, i:i + 1], float(NPG - i)).then_inc(pool_steps.sem, pool_steps.unit)
            for i in range(MORE):
                pool.memset(steps128[:, i:i + 1], float(P * (i + 1))).then_inc(pool_steps.sem, pool_steps.unit)
            pool.memset(before[:, 0, :], 0.0).then_inc(pool_steps.sem, pool_steps.unit)
            pool.memset(ends[:, 0:1], 0.0).then_inc(pool_steps.sem, pool_steps.unit)
            pool.iota(token[:], pattern=[[P, NT]], base=0, channel_multiplier=1).then_inc(pool_steps.sem, pool_steps.unit)
            pool.wait_ge(pool_steps.sem, pool_steps.done())
            pool.wait_ge(zeroed.sem, zeroed.done())
            pool.wait_ge(places_ready.sem, places_ready.done())
            for k in range(2):
                for t in range(NT):
                    pool.indirect_dma_start(io["slot_tok"], bass.IndirectOffsetOnAxis(ap=env.places[:, k, t:t + 1], axis=0),
                                                         token[:, t:t + 1], None).then_inc(scattered.sem, scattered.unit)

        @block.scalar
        def _(act):
            act.wait_ge(exp_in.sem, exp_in.done(0, 1))
            act.activation(gexp[:], gexp[:], ACT.Exp).then_inc(exp_done.sem, exp_done.unit)
            act.wait_ge(exp_in.sem, exp_in.done(0, 2))
            act.activation(tops[1][:], tops[1][:], ACT.Exp).then_inc(exp_done.sem, exp_done.unit)

        @block.tensor
        def _(pe):
            pe.wait_ge(pairs_ready.sem, pairs_ready.done())
            pe.matmul(rank_ps[:], env.upper[:], both[:], start=True, stop=True)
            pe.matmul(total_ps[:], env.ones[:], both[:], start=True, stop=True).then_inc(ranked.sem, ranked.unit)

        @block.vector
        def _(dve):
            def over(v, n):
                return spread(v, n)

            def first_max(values, n, top_out, onehot):
                ranks = order[:, NPG - n:NPG].unsqueeze(1).to_broadcast([P, NT, n])
                dve.tensor_reduce(top_out[:], values, AX, ALU.max).then_inc(dve_steps.sem, dve_steps.unit)
                dve.wait_ge(dve_steps.sem, dve_steps.next())
                dve.tensor_tensor(eq[:, :, 0:n], values, over(top_out[:], n), ALU.is_equal).then_inc(dve_steps.sem, dve_steps.unit)
                dve.wait_ge(dve_steps.sem, dve_steps.next())
                dve.tensor_tensor(eq[:, :, 0:n], eq[:, :, 0:n], ranks, ALU.mult).then_inc(dve_steps.sem, dve_steps.unit)
                dve.wait_ge(dve_steps.sem, dve_steps.next())
                dve.tensor_reduce(first[:], eq[:, :, 0:n], AX, ALU.max).then_inc(dve_steps.sem, dve_steps.unit)
                dve.wait_ge(dve_steps.sem, dve_steps.next())
                dve.tensor_tensor(onehot, ranks, over(first[:], n), ALU.is_equal).then_inc(dve_steps.sem, dve_steps.unit)
                dve.wait_ge(dve_steps.sem, dve_steps.next())

            dve.wait_ge(bias_in.sem, bias_in.done())
            dve.wait_ge(pool_steps.sem, pool_steps.done())
            dve.tensor_tensor(lg[:], env.logits[:], bias[:].unsqueeze(1).to_broadcast([P, NT, NG + NE]), ALU.add).then_inc(dve_steps.sem, dve_steps.unit)
            dve.wait_ge(dve_steps.sem, dve_steps.next())
            first_max(lg[:, :, 0:NG], NG, top, group[:])
            dve.tensor_tensor(gexp[:], lg[:, :, 0:NG], over(top[:], NG), ALU.subtract).then_inc(dve_steps.sem, dve_steps.unit)
            dve.wait_ge(dve_steps.sem, dve_steps.next())
            dve.tensor_tensor(wide[:], lg[:, :, NG:].rearrange("p t (g e) -> p t g e", g=NG), spread(group[:], NPG, 3), ALU.mult).then_inc(exp_in.sem, exp_in.unit)
            dve.wait_ge(exp_in.sem, exp_in.done(0, 1))
            dve.tensor_reduce(in_group[:], wide[:].rearrange("p t g e -> p t e g"), AX, ALU.add).then_inc(dve_steps.sem, dve_steps.unit)
            dve.wait_ge(dve_steps.sem, dve_steps.next())
            first_max(in_group[:], NPG, tops[0], pick[0][:])
            dve.scalar_tensor_tensor(in_group[:], pick[0][:], -BIG, in_group[:], ALU.mult, ALU.add).then_inc(dve_steps.sem, dve_steps.unit)
            dve.wait_ge(dve_steps.sem, dve_steps.next())
            first_max(in_group[:], NPG, tops[1], pick[1][:])
            dve.tensor_tensor(tops[1][:], tops[1][:], tops[0][:], ALU.subtract).then_inc(exp_in.sem, exp_in.unit)
            for k in range(2):
                dve.tensor_tensor(pair[k][:], spread(group[:], NPG, 3), spread(pick[k][:], NG, 2), ALU.mult).then_inc(dve_steps.sem, dve_steps.unit)
                dve.wait_ge(dve_steps.sem, dve_steps.next())
            dve.tensor_tensor(both[:], pair[0][:].rearrange("p t g e -> p (t g e)"),
                                             pair[1][:].rearrange("p t g e -> p (t g e)"), ALU.add).then_inc(pairs_ready.sem, pairs_ready.unit)
            dve.wait_ge(exp_done.sem, exp_done.done())
            dve.tensor_reduce(gprob[:], gexp[:], AX, ALU.add).then_inc(dve_steps.sem, dve_steps.unit)
            dve.wait_ge(dve_steps.sem, dve_steps.next())
            dve.reciprocal(gprob[:], gprob[:]).then_inc(dve_steps.sem, dve_steps.unit)
            dve.wait_ge(dve_steps.sem, dve_steps.next())
            dve.tensor_scalar(tops[0][:], tops[1][:], 1.0, None, ALU.add).then_inc(dve_steps.sem, dve_steps.unit)
            dve.wait_ge(dve_steps.sem, dve_steps.next())
            dve.reciprocal(tops[0][:], tops[0][:]).then_inc(dve_steps.sem, dve_steps.unit)
            dve.wait_ge(dve_steps.sem, dve_steps.next())
            dve.tensor_tensor(env.weights[:, 0], tops[0][:], gprob[:], ALU.mult).then_inc(dve_steps.sem, dve_steps.unit)
            dve.wait_ge(dve_steps.sem, dve_steps.next())
            dve.tensor_tensor(env.weights[:, 1], env.weights[:, 0], tops[1][:], ALU.mult).then_inc(dve_steps.sem, dve_steps.unit)
            dve.wait_ge(dve_steps.sem, dve_steps.next())
            dve.wait_ge(ranked.sem, ranked.done())
            totals = total_ps[:].rearrange("p (t e) -> p t e", e=NE)
            for t in range(NT):
                dve.tensor_tensor(before[:, t + 1], before[:, t], totals[:, t], ALU.add).then_inc(dve_steps.sem, dve_steps.unit)
                dve.wait_ge(dve_steps.sem, dve_steps.next())
            dve.tensor_tensor(more[:], spread(before[:, NT], MORE), steps128[:].unsqueeze(1).to_broadcast([P, NE, MORE]), ALU.is_gt).then_inc(dve_steps.sem, dve_steps.unit)
            dve.wait_ge(dve_steps.sem, dve_steps.next())
            dve.tensor_reduce(blocks[:], more[:], AX, ALU.add).then_inc(dve_steps.sem, dve_steps.unit)
            dve.wait_ge(dve_steps.sem, dve_steps.next())
            dve.tensor_scalar(blocks[:], blocks[:], 1.0, None, ALU.add).then_inc(dve_steps.sem, dve_steps.unit)
            dve.wait_ge(dve_steps.sem, dve_steps.next())
            dve.tensor_tensor_scan(ends[:, 1:NE + 1], env.ones[:, 0:NE], blocks[:], 0.0, ALU.mult, ALU.add).then_inc(dve_steps.sem, dve_steps.unit)
            dve.wait_ge(dve_steps.sem, dve_steps.next())
            dve.tensor_scalar(ends[:, NE + 1:], ends[:, NE:NE + 1], -1.0, float(NBLOCKS + 1), ALU.mult, ALU.add).then_inc(dve_steps.sem, dve_steps.unit)
            dve.wait_ge(dve_steps.sem, dve_steps.next())
            dve.tensor_copy(env.first_block[:], ends[:]).then_inc(dve_steps.sem, dve_steps.unit)
            dve.wait_ge(dve_steps.sem, dve_steps.next())
            dve.tensor_scalar(start[:], ends[:, 0:NE], float(P), None, ALU.mult).then_inc(dve_steps.sem, dve_steps.unit)
            dve.wait_ge(dve_steps.sem, dve_steps.next())
            dve.tensor_tensor(place[:], rank_ps[:].rearrange("p (t e) -> p t e", e=NE), before[:, 0:NT], ALU.add).then_inc(dve_steps.sem, dve_steps.unit)
            dve.wait_ge(dve_steps.sem, dve_steps.next())
            dve.tensor_tensor(place[:], place[:], start[:].unsqueeze(1).to_broadcast([P, NT, NE]), ALU.add).then_inc(dve_steps.sem, dve_steps.unit)
            dve.wait_ge(dve_steps.sem, dve_steps.next())
            for k in range(2):
                w = wide[:].rearrange("p t g e -> p t (g e)")
                dve.tensor_tensor(w, place[:], pair[k][:].rearrange("p t g e -> p t (g e)"), ALU.mult).then_inc(dve_steps.sem, dve_steps.unit)
                dve.wait_ge(dve_steps.sem, dve_steps.next())
                dve.tensor_reduce(placef[:, k], w, AX, ALU.add).then_inc(dve_steps.sem, dve_steps.unit)
                dve.wait_ge(dve_steps.sem, dve_steps.next())
            dve.tensor_copy(env.places[:], placef[:]).then_inc(places_ready.sem, places_ready.unit)


def expert_weights(env, ctx):
    sb, _ = tools(env.nc, ctx)
    env.expert_w_in = [env.event(f"ex_w_loaded{s}", per=3, dma=True) for s in range(2)]
    env.expert_w_up = [sb(f"ex_w_up{s}", [P, 2, KD, FF]) for s in range(2)]
    env.expert_w_down = [sb(f"ex_w_down{s}", [P, FF // P, D]) for s in range(2)]


def load_expert(sp, env, s, e):
    w_in, w_up, w_down, io = env.expert_w_in[s], env.expert_w_up[s], env.expert_w_down[s], env.io
    for dst, name in ((w_up[:, 0], "moe_w_gate"), (w_up[:, 1], "moe_w_up")):
        sp.dma_start(dst, io[name][0, ds(e, 1)].rearrange("a (p k) f -> (a p) k f", k=KD)).then_inc(w_in.sem, w_in.unit)
    sp.dma_start(w_down[:], io["moe_w_down"][0, ds(e, 1)].rearrange("a (p k) n -> (a p) k n", k=FF // P)).then_inc(w_in.sem, w_in.unit)


def experts(env):
    nc, io = env.nc, env.io
    E = env.event
    w_in, w_up, w_down = env.expert_w_in, env.expert_w_up, env.expert_w_down
    picked = E("ex_picked")
    settled = E("ex_settled")
    gathered = E("ex_gathered", dma=True)
    x_turned = E("ex_x_turned")
    x_copied = E("ex_x_copied")
    gu_summed = E("ex_gu_summed")
    silued = E("ex_silued")
    hid_ready = E("ex_hid_ready")
    hid_turned = E("ex_hid_turned")
    hid_copied = E("ex_hid_copied")
    y_summed = E("ex_y_summed")
    y_act = E("ex_y_act")
    y_dve = E("ex_y_dve")
    y_stored = E("ex_y_stored", dma=True)
    zero_ready = E("ex_zero_ready")
    rest_zeroed = E("ex_rest_zeroed", dma=True)
    KF = FF // P
    with ExitStack() as ctx:
        sb, pb = tools(nc, ctx)
        x = sb("ex_x", [P, D])
        idx = sb("ex_idx", [P, 1], I32)
        xT = sb("ex_xT", [P, KD, P])
        sg = sb("ex_sg", [P, FF])
        hid = sb("ex_hid", [P, FF])
        hidT = sb("ex_hidT", [P, KF, P])
        y = sb("ex_y", [P, 2, BLK])
        zero = sb("ex_zero", [P, D])
        gu = pb("ex_gu", [P, 2, FF])
        tx = pb("ex_tx", [P, KD, P])
        th = pb("ex_th", [P, KF, P])
        yp = pb("ex_yp", [P, 2, BLK])
        block = ctx.enter_context(nc.Block())

        def bound(eng, e):
            at = env.first_block[0:1, ds(e, 1)] if not isinstance(e, int) else env.first_block[0:1, e:e + 1]
            return eng.value_load(at, min_val=0, max_val=NBLOCKS)

        @block.sync
        def _(sp):
            sp.wait_ge(zero_ready.sem, zero_ready.done())
            rest = bound(sp, NE + 1)
            with sp.Fori(0, rest) as b:
                sp.dma_start(io["yslots"][ds((NBLOCKS - b) * P, P), :], zero[:]).then_inc(rest_zeroed.sem, rest_zeroed.unit)
            sp.wait_ge(rest_zeroed.sem, rest_zeroed.done(rest, 0))
            load_expert(sp, env, 1, 1)
            with sp.Fori(1, NE // 2) as i:
                for s in range(2):
                    sp.wait_ge(y_summed.sem, y_summed.done(bound(sp, i * 2 + s - 1), 0))
                    load_expert(sp, env, s, i * 2 + s)

        @block.gpsimd
        def _(pool):
            pool.memset(zero[:], 0.0).then_inc(zero_ready.sem, zero_ready.unit)
            with pool.Fori(0, bound(pool, NE) + 1) as b:
                pool.wait_ge(x_turned.sem, x_turned.done(b, 0))
                pool.wait_ge(settled.sem, settled.done(b, 0))
                pool.tensor_copy(idx[:], env.slot_tok[:, ds(b, 1)]).then_inc(picked.sem, picked.unit)
                pool.wait_ge(picked.sem, picked.done(b))
                settle_pool(pool, env).then_inc(settled.sem, settled.unit)
                pool.indirect_dma_start(x[:], None, io["h2"], bass.IndirectOffsetOnAxis(ap=idx[:, 0:1], axis=0)).then_inc(gathered.sem, gathered.unit)
            total = bound(pool, NE)
            pool.wait_ge(settled.sem, settled.done(total))
            pool.wait_ge(gathered.sem, gathered.done(total))
            settle_pool(pool, env)

        @block.tensor
        def _(pe):
            def turn_x(b):
                pe.wait_ge(gathered.sem, gathered.done(b))
                for k in range(KD):
                    tr = pe.transpose(tx[:, k, :], x[:].rearrange("t (p k) -> t k p", k=KD)[:, k, :], env.ident[:])
                tr.then_inc(x_turned.sem, x_turned.unit)

            turn_x(0)
            with pe.Fori(0, NE // 2) as i:
                for s in range(2):
                    first, end = bound(pe, i * 2 + s), bound(pe, i * 2 + s + 1)
                    with pe.Fori(first, end) as b:
                        pe.wait_ge(w_in[s].sem, w_in[s].done(i))
                        pe.wait_ge(x_copied.sem, x_copied.done(b))
                        for u in range(2):
                            for k in range(KD):
                                mm = pe.matmul(gu[:, u, :], xT[:, k, :], w_up[s][:, u, k, :], start=(k == 0), stop=(k == KD - 1))
                        mm.then_inc(gu_summed.sem, gu_summed.unit)
                        turn_x(b + 1)
                        pe.wait_ge(hid_ready.sem, hid_ready.done(b))
                        for k in range(KF):
                            tr = pe.transpose(th[:, k, :], hid[:].rearrange("t (p k) -> t k p", k=KF)[:, k, :], env.ident[:])
                        tr.then_inc(hid_turned.sem, hid_turned.unit)
                        pe.wait_ge(hid_copied.sem, hid_copied.done(b))
                        pe.wait_ge(y_act.sem, y_act.done(b, 0))
                        pe.wait_ge(y_dve.sem, y_dve.done(b, 0))
                        for half in range(2):
                            for k in range(KF):
                                mm = pe.matmul(yp[:, half, :], hidT[:, k, :], w_down[s][:, k, half * BLK:(half + 1) * BLK],
                                               start=(k == 0), stop=(k == KF - 1))
                        mm.then_inc(y_summed.sem, y_summed.unit)

        @block.scalar
        def _(act):
            act.wait_ge(x_turned.sem, x_turned.done(0))
            act.activation(xT[:], tx[:], ACT.Identity).then_inc(x_copied.sem, x_copied.unit)
            total = bound(act, NE)
            with act.Fori(0, total) as b:
                act.wait_ge(gu_summed.sem, gu_summed.done(b))
                act.activation(sg[:], gu[:, 0, :], ACT.Silu).then_inc(silued.sem, silued.unit)
                act.wait_ge(x_turned.sem, x_turned.done(b + 1))
                act.activation(xT[:], tx[:], ACT.Identity).then_inc(x_copied.sem, x_copied.unit)
                act.wait_ge(y_summed.sem, y_summed.done(b))
                act.wait_ge(y_stored.sem, y_stored.done(b, 0))
                act.activation(y[:, 0], yp[:, 0], ACT.Identity).then_inc(y_act.sem, y_act.unit)
                act.wait_ge(y_act.sem, y_act.done(b))
                act.wait_ge(y_dve.sem, y_dve.done(b))
                act.dma_start(io["yslots"][ds(b * P, P), :], y[:].rearrange("p x n -> p (x n)")).then_inc(y_stored.sem, y_stored.unit)
            act.wait_ge(y_stored.sem, y_stored.done(total, 0))
            act.activation(env.settled[:, 1:2], env.ones[:, 0:1], ACT.Identity)

        @block.vector
        def _(dve):
            with dve.Fori(0, bound(dve, NE)) as b:
                dve.wait_ge(silued.sem, silued.done(b))
                dve.tensor_tensor(hid[:], sg[:], gu[:, 1, :], ALU.mult).then_inc(hid_ready.sem, hid_ready.unit)
                dve.wait_ge(hid_turned.sem, hid_turned.done(b))
                dve.tensor_copy(hidT[:], th[:]).then_inc(hid_copied.sem, hid_copied.unit)
                dve.wait_ge(y_summed.sem, y_summed.done(b))
                dve.wait_ge(y_stored.sem, y_stored.done(b, 0))
                dve.tensor_copy(y[:, 1], yp[:, 1]).then_inc(y_dve.sem, y_dve.unit)


def combine(env):
    nc, io = env.nc, env.io
    E = env.event
    rows_in = E("cb_rows_loaded", per=3, dma=True)
    picked = E("cb_picked")
    settled = E("cb_settled")
    got = [E(f"cb_got{s}", per=2, dma=True) for s in range(2)]
    x_in = [E(f"cb_x_loaded{s}", dma=True) for s in range(2)]
    mix_steps = E("cb_mix_steps", per=4)
    squared = E("cb_squared")
    meaned = E("cb_meaned")
    rooted = E("cb_rooted")
    norm_steps = E("cb_norm_steps", per=3)
    stored = [E(f"cb_stored{s}", dma=True) for s in range(2)]
    with ExitStack() as ctx:
        sb, pb = tools(nc, ctx)
        gate2 = sb("cb_gate2", [P, 2, D])
        final = sb("cb_final", [P, D])
        idx = [sb(f"cb_idx{s}", [P, 2], I32) for s in range(2)]
        got_rows = [sb(f"cb_rows{s}", [P, 2, D]) for s in range(2)]
        x1 = [sb(f"cb_x1{s}", [P, D]) for s in range(2)]
        sq = sb("cb_sq", [P, D])
        ss = sb("cb_ss", [P, 4])
        out = [sb(f"cb_out{s}", [P, D]) for s in range(2)]
        block = ctx.enter_context(nc.Block())

        @block.sync
        def _(sp):
            for g in range(2):
                sp.dma_start(gate2[:, g], io["ada_rows"][g:g + 1, 5 * D:6 * D].to_broadcast([P, D])).then_inc(rows_in.sem, rows_in.unit)
            sp.dma_start(final[:], io["final_norm"].rearrange("(o d) -> o d", o=1).to_broadcast([P, D])).then_inc(rows_in.sem, rows_in.unit)
            for s in range(2):
                sp.dma_start(x1[s][:], io["x1"][s * P:(s + 1) * P, :]).then_inc(x_in[s].sem, x_in[s].unit)
            with sp.Fori(1, NT // 2) as i:
                for s in range(2):
                    sp.wait_ge(norm_steps.sem, norm_steps.done(i * 2 + s - 2))
                    sp.dma_start(x1[s][:], io["x1"][ds((i * 2 + s) * P, P), :]).then_inc(x_in[s].sem, x_in[s].unit)

        @block.gpsimd
        def _(pool):
            def gather(t, s):
                pool.wait_ge(settled.sem, settled.done(t, 0))
                pool.tensor_copy(idx[s][:], env.places[:, :, ds(t, 1)].rearrange("p k a -> p (k a)")).then_inc(picked.sem, picked.unit)
                pool.wait_ge(picked.sem, picked.done(t))
                settle_pool(pool, env).then_inc(settled.sem, settled.unit)
                for k in range(2):
                    pool.indirect_dma_start(got_rows[s][:, k], None, io["yslots"],
                                            bass.IndirectOffsetOnAxis(ap=idx[s][:, k:k + 1], axis=0)).then_inc(got[s].sem, got[s].unit)

            for s in range(2):
                gather(s, s)
            with pool.Fori(1, NT // 2) as i:
                for s in range(2):
                    pool.wait_ge(norm_steps.sem, norm_steps.done(i * 2 + s - 2))
                    gather(i * 2 + s, s)

        @block.scalar
        def _(act):
            for g, (t0, n) in enumerate(SEQS):
                with act.Fori(0, n // 2) as i:
                    for s in range(2):
                        t = t0 + i * 2 + s
                        act.wait_ge(mix_steps.sem, mix_steps.done(t))
                        act.activation(sq[:], x1[s][:], ACT.Square, accum_out=ss[:, 0:1]).then_inc(squared.sem, squared.unit)
                        act.wait_ge(meaned.sem, meaned.done(t))
                        act.activation(ss[:, 2:3], ss[:, 1:2], ACT.Sqrt).then_inc(rooted.sem, rooted.unit)
                        act.wait_ge(norm_steps.sem, norm_steps.done(t))
                        dst = io["y_prompt"][0] if g == 0 else io["y_sample"][0]
                        act.dma_start(dst[ds((i * 2 + s) * P, P), :], out[s][:]).then_inc(stored[s].sem, stored[s].unit)
            for s in range(2):
                act.wait_ge(stored[s].sem, stored[s].done(NT // 2 - 1))

        @block.vector
        def _(dve):
            dve.wait_ge(rows_in.sem, rows_in.done())
            for g, (t0, n) in enumerate(SEQS):
                with dve.Fori(0, n // 2) as i:
                    for s in range(2):
                        t = t0 + i * 2 + s
                        half_turn = t0 // 2 + i
                        rows = got_rows[s]
                        dve.wait_ge(got[s].sem, got[s].done(half_turn))
                        dve.tensor_scalar(rows[:, 0], rows[:, 0], env.weights[:, 0, ds(t, 1)], None, ALU.mult).then_inc(mix_steps.sem, mix_steps.unit)
                        dve.wait_ge(mix_steps.sem, mix_steps.done(t, 1))
                        dve.scalar_tensor_tensor(rows[:, 0], rows[:, 1], env.weights[:, 1, ds(t, 1)], rows[:, 0],
                                                              ALU.mult, ALU.add).then_inc(mix_steps.sem, mix_steps.unit)
                        dve.wait_ge(mix_steps.sem, mix_steps.done(t, 2))
                        dve.tensor_tensor(rows[:, 0], rows[:, 0], gate2[:, g], ALU.mult).then_inc(mix_steps.sem, mix_steps.unit)
                        dve.wait_ge(mix_steps.sem, mix_steps.done(t, 3))
                        dve.wait_ge(x_in[s].sem, x_in[s].done(half_turn))
                        dve.tensor_tensor(x1[s][:], rows[:, 0], x1[s][:], ALU.add).then_inc(mix_steps.sem, mix_steps.unit)
                        dve.wait_ge(squared.sem, squared.done(t))
                        dve.tensor_scalar(ss[:, 1:2], ss[:, 0:1], 1.0 / D, 1e-6, ALU.mult, ALU.add).then_inc(meaned.sem, meaned.unit)
                        dve.wait_ge(rooted.sem, rooted.done(t))
                        dve.reciprocal(ss[:, 3:4], ss[:, 2:3]).then_inc(norm_steps.sem, norm_steps.unit)
                        dve.wait_ge(norm_steps.sem, norm_steps.done(t, 1))
                        dve.wait_ge(stored[s].sem, stored[s].done(half_turn, 0))
                        dve.tensor_scalar(out[s][:], x1[s][:], ss[:, 3:4], None, ALU.mult).then_inc(norm_steps.sem, norm_steps.unit)
                        dve.wait_ge(norm_steps.sem, norm_steps.done(t, 2))
                        dve.tensor_tensor(out[s][:], out[s][:], final[:], ALU.mult).then_inc(norm_steps.sem, norm_steps.unit)


SCRATCH = {
    "ada_rows": ((2, 6 * D), F32),
    "ch": ((IN_COLS, TOK), F32),
    "dn_rec": ((NT * 2, P, 3 * DNH * P), F32),
    "rw_rec": ((NT * 2, P, 1032), F32),
    "rw_side": ((NT, P, 2 * RWW), F32),
    "yT": ((DNW + RWW, TOK), F32),
    "x1": ((TOK, D), F32),
    "h2": ((TOK, D), F32),
    "slot_tok": (((NBLOCKS + 1) * P, 1), I32),
    "yslots": ((SLOTS + P, D), F32),
}
OUTPUTS = {"y_prompt": ((1, SEQ[0], D), F32), "y_sample": ((1, SEQ[1], D), F32)}


def program(nc, io):
    with ExitStack() as ctx:
        env = Env(nc, ctx, io)
        constants(env)
        with ExitStack() as stage:
            ada_and_norm(env, stage)
            project(env)
        env.recycle()
        with ExitStack() as stage:
            env.dn_o = stage.enter_context(nc.sbuf_tensor("dn_o", [P, NT, DNW], F32))
            env.rw_o = stage.enter_context(nc.sbuf_tensor("rw_o", [P, NT, RWW], F32))
            delta(env)
            env.recycle()
            rwkv(env)
            env.recycle()
            recur(env)
            head_out(env)
        env.logits = env.keep("logits", [P, NT, NG + NE])
        mix_out(env)
        env.recycle()
        routed(env)
        with ExitStack() as stage:
            expert_weights(env, stage)
            route(env)
            experts(env)
        combine(env)


def routed(env):
    env.places = env.keep("places", [P, 2, NT], I32)
    env.weights = env.keep("weights", [P, 2, NT])
    env.first_block = env.keep("first_block", [P, NE + 2], I32)
    env.slot_tok = env.keep("slot_tok_cols", [P, NBLOCKS + 1], I32)


INPUTS = ("x_prompt", "x_sample", "c_prompt", "c_sample", "w_ada", "b_ada", "norm1", "norm2", "w_in",
          "dn_conv_w", "dn_a_log", "dn_dt_bias", "dn_norm_w", "rw_mu", "rw_w0", "rw_w2", "rw_a0", "rw_a2",
          "rw_g2", "rw_k_k", "rw_k_a", "rw_r_k", "rw_ln_w", "rw_ln_b", "w_br_dn", "w_br_rw", "w_out",
          "moe_w_group", "moe_b_group", "moe_w_expert", "moe_b_expert", "moe_w_gate", "moe_w_up",
          "moe_w_down", "final_norm")


def kernel(**inputs):
    import numpy as np
    import concourse.bacc as bacc
    from concourse import mybir
    from concourse.bass_utils import run_bass_kernel_spmd as run

    nc = bacc.Bacc("TRN2", target_bir_lowering=False, num_devices=1)
    arrays, io = {}, {}
    for name in INPUTS:
        a = np.ascontiguousarray(inputs[name])
        arrays[f"in_{name}"] = a
        io[name] = nc.dram_tensor(f"in_{name}", a.shape, mybir.dt.from_np(a.dtype), kind="ExternalInput").ap()
    for name, (shape, dt) in SCRATCH.items():
        io[name] = nc.dram_tensor(f"scratch_{name}", shape, dt).ap()
    for name, (shape, dt) in OUTPUTS.items():
        io[name] = nc.dram_tensor(f"out_{name}", shape, dt, kind="ExternalOutput").ap()
    program(nc, io)
    r = run(nc, [arrays], core_ids=[0])
    return tuple(r.results[0][f"out_{name}"] for name in OUTPUTS)
```
